# Optimizing a Trainium2 kernel written in Bass

```python
import math
import jax
import jax.numpy as jnp
from jax import lax
import numpy as np

D_MODEL = 2048
BATCH = 1
SEQ = 256
DEPTH = 2

CHUNK = 64
N_META = 16
Q_BLOCK = 128
N_MIXERS = 4
NORM_EPS = 1e-6
LN_EPS = 1e-5

SWA_HEADS = 32
SWA_KV_HEADS = 8
SWA_GROUP = SWA_HEADS // SWA_KV_HEADS
SWA_HEAD_DIM = D_MODEL // SWA_HEADS
SWA_WINDOW = 128
SWA_WINDOW_CHUNKS = SWA_WINDOW // CHUNK

DIFF_HEAD_DIM = 128
DIFF_HEADS = D_MODEL // (2 * DIFF_HEAD_DIM)

CONV_WIDTH = 31

MLA_HEADS = 16
MLA_Q_RANK = 512
MLA_KV_RANK = 512
MLA_NOPE_DIM = 128
MLA_ROPE_DIM = 64
MLA_V_DIM = 128
ROPE_THETA = 10000.0

D_FF = 4 * D_MODEL

N_SWA_LAYERS = (DEPTH + N_MIXERS - 1) // N_MIXERS
N_DIFF_LAYERS = (DEPTH + N_MIXERS - 2) // N_MIXERS
N_CONV_LAYERS = (DEPTH + N_MIXERS - 3) // N_MIXERS
N_MLA_LAYERS = (DEPTH + N_MIXERS - 4) // N_MIXERS

kernel_name = "hybrid_chunk_causal_interleaved_trunk"

def rms_norm(x, g, eps=NORM_EPS):
    xf = x.astype(jnp.float32)
    y = xf * lax.rsqrt(jnp.mean(xf * xf, axis=-1, keepdims=True) + eps)
    return (y * g.astype(jnp.float32)).astype(x.dtype)

def layer_norm(x, g, b):
    xf = x.astype(jnp.float32)
    mu = jnp.mean(xf, axis=-1, keepdims=True)
    var = jnp.mean(jnp.square(xf - mu), axis=-1, keepdims=True)
    y = (xf - mu) * lax.rsqrt(var + LN_EPS)
    return (y * g.astype(jnp.float32) + b.astype(jnp.float32)).astype(x.dtype)

def rope_tables(length):
    inv = 1.0 / (ROPE_THETA ** (jnp.arange(0, MLA_ROPE_DIM, 2, dtype=jnp.float32) / MLA_ROPE_DIM))
    ang = jnp.arange(length, dtype=jnp.float32)[:, None] * inv[None, :]
    return jnp.cos(ang), jnp.sin(ang)

def apply_rope(x, cos, sin):
    shape = (1, x.shape[1]) + (1,) * (x.ndim - 3) + (cos.shape[-1],)
    c = cos.reshape(shape)
    s = sin.reshape(shape)
    xf = x.astype(jnp.float32)
    x1, x2 = jnp.split(xf, 2, axis=-1)
    return jnp.concatenate([x1 * c - x2 * s, x1 * s + x2 * c], axis=-1).astype(x.dtype)

def chunk_causal_sweep(attend, qs, kvs):
    n_real = qs[0].shape[1] - N_META

    def cut(ts, a, b):
        return tuple(t[:, a:b] for t in ts)

    outs = [attend(*cut(qs, 0, N_META), *cut(kvs, 0, N_META), np.ones((N_META, N_META), bool))]
    for blk in range(n_real // Q_BLOCK):
        q0 = blk * Q_BLOCK
        q1 = q0 + Q_BLOCK
        q_chunk = np.arange(q0, q1) // CHUNK
        k_chunk = np.arange(q1) // CHUNK
        mask = np.concatenate([np.ones((Q_BLOCK, N_META), bool),
                               k_chunk[None, :] <= q_chunk[:, None]], axis=1)
        outs.append(attend(*cut(qs, N_META + q0, N_META + q1), *cut(kvs, 0, N_META + q1), mask))
    return jnp.concatenate(outs, axis=1)

def swa_sink_mixer(h, w_in, sinks, w_out):
    B, L, _ = h.shape
    S = L - N_META
    nc = S // CHUNK
    G, R, dh = SWA_KV_HEADS, SWA_GROUP, SWA_HEAD_DIM
    qkv = h @ w_in
    q, k, v = jnp.split(qkv, [SWA_HEADS * dh, SWA_HEADS * dh + G * dh], axis=-1)
    q = q.reshape(B, L, G, R, dh)
    k = k.reshape(B, L, G, dh)
    v = v.reshape(B, L, G, dh)
    sink = sinks.reshape(G, R).astype(jnp.float32)
    scale = dh ** -0.5

    def attend(qb, kb, vb, mask):
        s = jnp.einsum('...qgrd,...kgd->...grqk', qb, kb).astype(jnp.float32) * scale
        s = jnp.where(mask, s, -jnp.inf)
        sink_col = jnp.broadcast_to(sink[:, :, None, None], s.shape[:-1] + (1,))
        p = jax.nn.softmax(jnp.concatenate([s, sink_col], axis=-1), axis=-1)[..., :-1]
        return jnp.einsum('...grqk,...kgd->...qgrd', p.astype(vb.dtype), vb)

    out_meta = attend(q[:, :N_META], k[:, :N_META], v[:, :N_META], np.ones((N_META, N_META), bool))

    W = SWA_WINDOW_CHUNKS
    qc = q[:, N_META:].reshape(B, nc, CHUNK, G, R, dh)
    kc = k[:, N_META:].reshape(B, nc, CHUNK, G, dh)
    vc = v[:, N_META:].reshape(B, nc, CHUNK, G, dh)
    pad = ((0, 0), (W - 1, 0), (0, 0), (0, 0), (0, 0))
    kpad = jnp.pad(kc, pad)
    vpad = jnp.pad(vc, pad)
    k_meta = jnp.broadcast_to(k[:, None, :N_META], (B, nc, N_META, G, dh))
    v_meta = jnp.broadcast_to(v[:, None, :N_META], (B, nc, N_META, G, dh))
    shifts = range(W - 1, -1, -1)
    kw = jnp.concatenate([k_meta] + [kpad[:, W - 1 - w: W - 1 - w + nc] for w in shifts], axis=2)
    vw = jnp.concatenate([v_meta] + [vpad[:, W - 1 - w: W - 1 - w + nc] for w in shifts], axis=2)
    c_idx = np.arange(nc)[:, None]
    band = np.concatenate([np.ones((nc, N_META), bool)] +
                          [np.broadcast_to(c_idx - w >= 0, (nc, CHUNK)) for w in shifts], axis=1)
    out_real = attend(qc, kw, vw, band[None, :, None, None, None, :])

    out = jnp.concatenate([out_meta.reshape(B, N_META, SWA_HEADS * dh),
                           out_real.reshape(B, S, SWA_HEADS * dh)], axis=1)
    return out @ w_out

def diff_attn_mixer(h, w_in, lam_q1, lam_k1, lam_q2, lam_k2, subln_g, w_out, lambda_init):
    B, L, _ = h.shape
    H, d = DIFF_HEADS, DIFF_HEAD_DIM
    qkv = h @ w_in
    q, k, v = jnp.split(qkv, 3, axis=-1)
    q = q.reshape(B, L, H, 2, d)
    k = k.reshape(B, L, H, 2, d)
    v = v.reshape(B, L, H, 2 * d)
    f32 = jnp.float32
    lam = (jnp.exp(jnp.sum(lam_q1.astype(f32) * lam_k1.astype(f32)))
           - jnp.exp(jnp.sum(lam_q2.astype(f32) * lam_k2.astype(f32))) + lambda_init)
    scale = d ** -0.5

    def attend(qb, kb, vb, mask):
        s = jnp.einsum('bqhid,bkhid->bihqk', qb, kb).astype(f32) * scale
        p = jax.nn.softmax(jnp.where(mask, s, -jnp.inf), axis=-1)
        diff = p[:, 0] - lam * p[:, 1]
        return jnp.einsum('bhqk,bkhe->bqhe', diff.astype(vb.dtype), vb)

    o = chunk_causal_sweep(attend, (q,), (k, v))
    o = rms_norm(o, subln_g, eps=LN_EPS) * (1.0 - lambda_init)
    return o.reshape(B, L, H * 2 * d) @ w_out

def conformer_conv_mixer(h, w_pw1, b_pw1, w_dw, b_dw, ln_g, ln_b, w_pw2, b_pw2):
    a = h @ w_pw1 + b_pw1
    a1, a2 = jnp.split(a, 2, axis=-1)
    u = a1 * jax.nn.sigmoid(a2)
    D = u.shape[-1]
    y = lax.conv_general_dilated(
        u, w_dw[:, None, :].astype(u.dtype), window_strides=(1,),
        padding=[(CONV_WIDTH - 1, 0)], dimension_numbers=('NWC', 'WIO', 'NWC'),
        feature_group_count=D) + b_dw
    y = jax.nn.silu(layer_norm(y, ln_g, ln_b))
    return y @ w_pw2 + b_pw2

def mla_mixer(h, w_in, q_norm_g, kv_norm_g, w_uq, w_ukv, w_out, cos, sin):
    B, L, _ = h.shape
    H = MLA_HEADS
    a = h @ w_in
    c_q, c_kv, k_rope = jnp.split(a, [MLA_Q_RANK, MLA_Q_RANK + MLA_KV_RANK], axis=-1)
    c_q = rms_norm(c_q, q_norm_g)
    c_kv = rms_norm(c_kv, kv_norm_g)
    q = (c_q @ w_uq).reshape(B, L, H, MLA_NOPE_DIM + MLA_ROPE_DIM)
    q_nope, q_rope = jnp.split(q, [MLA_NOPE_DIM], axis=-1)
    q_rope = apply_rope(q_rope, cos, sin)
    k_rope = apply_rope(k_rope, cos, sin)
    kv = (c_kv @ w_ukv).reshape(B, L, H, MLA_NOPE_DIM + MLA_V_DIM)
    k_nope, v = jnp.split(kv, [MLA_NOPE_DIM], axis=-1)
    scale = (MLA_NOPE_DIM + MLA_ROPE_DIM) ** -0.5

    def attend(qn, qr, kn, kr, vb, mask):
        s = (jnp.einsum('bqhd,bkhd->bhqk', qn, kn).astype(jnp.float32)
             + jnp.einsum('bqhd,bkd->bhqk', qr, kr).astype(jnp.float32)) * scale
        p = jax.nn.softmax(jnp.where(mask, s, -jnp.inf), axis=-1)
        return jnp.einsum('bhqk,bkhd->bqhd', p.astype(vb.dtype), vb)

    o = chunk_causal_sweep(attend, (q_nope, q_rope), (k_nope, k_rope, v))
    return o.reshape(B, L, H * MLA_V_DIM) @ w_out

def sq_relu_mlp(h, w1, w2):
    return jnp.square(jax.nn.relu(h @ w1)) @ w2

def setup_inputs(seed: int = 0) -> dict:
    key = jax.random.key(seed)
    ks = iter(jax.random.split(key, 40))
    D = D_MODEL

    def nrm(shape, scale):
        return jax.random.normal(next(ks), shape, jnp.float32) * scale

    def gain(shape):
        return 1.0 + nrm(shape, 0.01)

    return {
        "x": nrm((BATCH, SEQ, D), 1.0),
        "meta_tokens": nrm((N_META, D), 1.0),
        "mix_pre_g": gain((DEPTH, D)),
        "mix_post_g": gain((DEPTH, D)),
        "ffn_pre_g": gain((DEPTH, D)),
        "ffn_post_g": gain((DEPTH, D)),
        "swa_w_in": nrm((N_SWA_LAYERS, D, (SWA_HEADS + 2 * SWA_KV_HEADS) * SWA_HEAD_DIM), D ** -0.5),
        "swa_sinks": nrm((N_SWA_LAYERS, SWA_HEADS), 0.5),
        "swa_w_out": nrm((N_SWA_LAYERS, SWA_HEADS * SWA_HEAD_DIM, D), (SWA_HEADS * SWA_HEAD_DIM) ** -0.5),
        "diff_w_in": nrm((N_DIFF_LAYERS, D, 3 * DIFF_HEADS * 2 * DIFF_HEAD_DIM), D ** -0.5),
        "diff_lam_q1": nrm((N_DIFF_LAYERS, DIFF_HEAD_DIM), 0.1),
        "diff_lam_k1": nrm((N_DIFF_LAYERS, DIFF_HEAD_DIM), 0.1),
        "diff_lam_q2": nrm((N_DIFF_LAYERS, DIFF_HEAD_DIM), 0.1),
        "diff_lam_k2": nrm((N_DIFF_LAYERS, DIFF_HEAD_DIM), 0.1),
        "diff_subln_g": gain((N_DIFF_LAYERS, 2 * DIFF_HEAD_DIM)),
        "diff_w_out": nrm((N_DIFF_LAYERS, DIFF_HEADS * 2 * DIFF_HEAD_DIM, D), (DIFF_HEADS * 2 * DIFF_HEAD_DIM) ** -0.5),
        "conv_w_pw1": nrm((N_CONV_LAYERS, D, 2 * D), D ** -0.5),
        "conv_b_pw1": nrm((N_CONV_LAYERS, 2 * D), 0.01),
        "conv_w_dw": nrm((N_CONV_LAYERS, CONV_WIDTH, D), CONV_WIDTH ** -0.5),
        "conv_b_dw": nrm((N_CONV_LAYERS, D), 0.01),
        "conv_ln_g": gain((N_CONV_LAYERS, D)),
        "conv_ln_b": nrm((N_CONV_LAYERS, D), 0.01),
        "conv_w_pw2": nrm((N_CONV_LAYERS, D, D), D ** -0.5),
        "conv_b_pw2": nrm((N_CONV_LAYERS, D), 0.01),
        "mla_w_in": nrm((N_MLA_LAYERS, D, MLA_Q_RANK + MLA_KV_RANK + MLA_ROPE_DIM), D ** -0.5),
        "mla_q_norm_g": gain((N_MLA_LAYERS, MLA_Q_RANK)),
        "mla_kv_norm_g": gain((N_MLA_LAYERS, MLA_KV_RANK)),
        "mla_w_uq": nrm((N_MLA_LAYERS, MLA_Q_RANK, MLA_HEADS * (MLA_NOPE_DIM + MLA_ROPE_DIM)), MLA_Q_RANK ** -0.5),
        "mla_w_ukv": nrm((N_MLA_LAYERS, MLA_KV_RANK, MLA_HEADS * (MLA_NOPE_DIM + MLA_V_DIM)), MLA_KV_RANK ** -0.5),
        "mla_w_out": nrm((N_MLA_LAYERS, MLA_HEADS * MLA_V_DIM, D), (MLA_HEADS * MLA_V_DIM) ** -0.5),
        "ffn_w1": nrm((DEPTH, D, D_FF), D ** -0.5),
        "ffn_w2": nrm((DEPTH, D_FF, D), D_FF ** -0.5),
    }

def reference(x, meta_tokens, mix_pre_g, mix_post_g, ffn_pre_g, ffn_post_g,
              swa_w_in, swa_sinks, swa_w_out,
              diff_w_in, diff_lam_q1, diff_lam_k1, diff_lam_q2, diff_lam_k2, diff_subln_g, diff_w_out,
              conv_w_pw1, conv_b_pw1, conv_w_dw, conv_b_dw, conv_ln_g, conv_ln_b, conv_w_pw2, conv_b_pw2,
              mla_w_in, mla_q_norm_g, mla_kv_norm_g, mla_w_uq, mla_w_ukv, mla_w_out,
              ffn_w1, ffn_w2):
    B = x.shape[0]
    meta = jnp.broadcast_to(meta_tokens.astype(x.dtype)[None], (B, N_META, x.shape[-1]))
    h = jnp.concatenate([meta, x], axis=1)
    cos, sin = rope_tables(h.shape[1])

    for i in range(DEPTH):
        kind = i % N_MIXERS
        j = i // N_MIXERS
        u = rms_norm(h, mix_pre_g[i])
        if kind == 0:
            m = swa_sink_mixer(u, swa_w_in[j], swa_sinks[j], swa_w_out[j])
        elif kind == 1:
            lambda_init = 0.8 - 0.6 * math.exp(-0.3 * i)
            m = diff_attn_mixer(u, diff_w_in[j], diff_lam_q1[j], diff_lam_k1[j], diff_lam_q2[j],
                                diff_lam_k2[j], diff_subln_g[j], diff_w_out[j], lambda_init)
        elif kind == 2:
            m = conformer_conv_mixer(u, conv_w_pw1[j], conv_b_pw1[j], conv_w_dw[j], conv_b_dw[j],
                                     conv_ln_g[j], conv_ln_b[j], conv_w_pw2[j], conv_b_pw2[j])
        else:
            m = mla_mixer(u, mla_w_in[j], mla_q_norm_g[j], mla_kv_norm_g[j], mla_w_uq[j],
                          mla_w_ukv[j], mla_w_out[j], cos, sin)
        h = h + rms_norm(m, mix_post_g[i])
        f = sq_relu_mlp(rms_norm(h, ffn_pre_g[i]), ffn_w1[i], ffn_w2[i])
        h = h + rms_norm(f, ffn_post_g[i])

    return h[:, N_META:]


_drawn_inputs = setup_inputs


def setup_inputs(seed=0):
    import zlib

    import numpy as np

    out = dict(_drawn_inputs(seed))
    spreads = {}
    factors = {'mix_pre_g': 3.884,
     'mix_post_g': 5.834,
     'ffn_pre_g': 6.682,
     'ffn_post_g': 7.07,
     'swa_sinks': 49.967,
     'diff_subln_g': 64.0}
    for name, (base, spread) in spreads.items():
        noise = np.random.default_rng([zlib.crc32(name.encode()), seed]).standard_normal(out[name].shape)
        drawn = base * np.exp(spread * noise) if base else spread * noise
        out[name] = jnp.asarray(drawn.astype(out[name].dtype))
    for name, factor in factors.items():
        out[name] = (out[name] * factor).astype(out[name].dtype)
    return out
```

```python
from contextlib import ExitStack, contextmanager
import math

import numpy as np
import concourse.bass as bass
from concourse import mybir
from concourse.alu_op_type import AluOpType as ALU

F32 = mybir.dt.float32
F32R = mybir.dt.float32r
ACT = mybir.ActivationFunctionType
AX = mybir.AxisListType

P = 128
D = 2048
SEQ = 256
META = 16
L = META + SEQ
KC = D // P
D_FF = 4 * D
NORM_EPS = 1e-6
LN_EPS = 1e-5
CHUNK = 64
NQ = SEQ // CHUNK

UNITS = 4
UK = KC // UNITS
GW = 256
GT = GW // P

SWA_DH = 64
SWA_PAIRS = 4
SWA_WIN = 2 * CHUNK
SWA_KEYS = META + SWA_WIN
DIFF_HEADS = 8
PANEL = D // GW
BLOCKS = D_FF // D

G_SWA = 0
G_WOUT0 = G_SWA + 3 * SWA_PAIRS
G_FFN0 = G_WOUT0 + PANEL
G_DIFF = G_FFN0 + 2 * PANEL * BLOCKS
G_WOUT1 = G_DIFF + 3 * DIFF_HEADS
G_FFN1 = G_WOUT1 + PANEL
GROUPS = G_FFN1 + 2 * PANEL * BLOCKS

LAMBDA_INIT = 0.8 - 0.6 * math.exp(-0.3)
SMALL_LOADS = 4 + 4 + 1 + 1
MIX_PRE, MIX_POST, FFN_PRE, FFN_POST = range(4)

ATT0, ATT1, AUX, STAT = 4, 5, 6, 7

SWA_N = [META + CHUNK] + [SWA_KEYS] * 3
SWA_OFF = [0, 80, 224, 368]
DIFF_N = [META + CHUNK * (c + 1) for c in range(NQ)]
DIFF_BANK = [ATT0, ATT1, ATT1, ATT0]
DIFF_OFF = [0, 0, DIFF_N[1], DIFF_N[0]]
DIFF_PAD = [META + P, META + P, META + 2 * P, META + 2 * P]
DIFF_AT = [0, 144, 288, 560]
DIFF_P = 832


def column(which, layer, c):
    return which * 2 * KC + layer * KC + c


class Tally:

    def __init__(self, eng, sem):
        self.eng, self.sem, self.value, self.marks = eng, sem, 0, 0

    def mark(self, instruction):
        instruction.then_inc(self.sem, 1)
        self.value = self.value + 1
        self.marks += 1

    def wait(self):
        self.eng.wait_ge(self.sem, self.value)

    @contextmanager
    def turns(self, i, count, per):
        before, marks = self.value, self.marks
        self.value = before + i * per
        yield
        assert self.marks - marks == per, (self.marks - marks, per)
        self.value, self.marks = before + count * per, marks + count * per


def trunk(nc, a, out):
    ctx = ExitStack()
    with ctx:
        def sb(name, shape, dt=F32):
            return ctx.enter_context(nc.sbuf_tensor(name, shape, dt))

        def sem(name):
            return ctx.enter_context(nc.semaphore(name))

        ps = ctx.enter_context(nc.psum_tensor("ps", [P, 8, 512], F32))

        raw = sb("raw", [P, UNITS, UK, GW])
        w_hi = sb("w_hi", [P, UNITS, UK, GW], F32R)
        w_lo = sb("w_lo", [P, UNITS, UK, GW], F32R)
        h = sb("h", [P, KC, L])
        x_hi = sb("x_hi", [P, KC, L], F32R)
        x_lo = sb("x_lo", [P, KC, L], F32R)
        y = sb("y", [P, KC, L])
        z_hi = sb("z_hi", [P, KC, L], F32R)
        z_lo = sb("z_lo", [P, KC, L], F32R)
        rows = sb("rows", [P, 2, D])
        rstd = sb("rstd", [P, L])
        std = sb("std", [P, L])
        rpost = sb("rpost", [P, L])
        pre_sum = sb("pre_sum", [P, L])
        sq = sb("sq", [P, GT, L])
        sq_sum = sb("sq_sum", [P, GT, L])
        relu = sb("relu", [P, GT, L])
        ident = sb("ident", [P, P])
        ones = sb("ones", [P, P])
        fold = sb("fold", [P, CHUNK])
        gain_rows = sb("gain_rows", [P, P])
        gains = sb("gains", [P, P])
        lam_rows = sb("lam_rows", [6, P])
        lam_cols = sb("lam_cols", [P, 6])
        lam_prod = sb("lam_prod", [P, 2])
        lam_exp = sb("lam_exp", [P, 2])
        map_sign = sb("map_sign", [P, 1])
        sub_gain = sb("sub_gain", [P, 2])
        sink = sb("sink", [P, KC])
        sink_rows = sb("sink_rows", [P, 2 * KC])
        row_tile = sb("row_tile", [P, 2])
        sink_part = sb("sink_part", [P, SWA_PAIRS])
        sink_meta = sb("sink_meta", [P, SWA_PAIRS])
        q = sb("q", [P, 4, L])
        q_meta = sb("q_meta", [P, 4 * META])
        k = sb("k", [P, 2, L])
        vt = sb("vt", [P, 2, L])
        v = sb("v", [P, 2, GW])
        vm = sb("vm", [META, GW])
        vw = v[:, :, :].rearrange("p a b -> p (a b)")[:, 0:3 * P].rearrange("p (w d) -> p w d", w=3)
        vwm = vm[:, 0:P]
        p_win = sb("p_win", [P, 2, NQ, SWA_KEYS])
        p_diff = p_win[:, :, :, :].rearrange("p a b c -> p (a b c)")[:, 0:DIFF_P]
        p_meta = sb("p_meta", [P, META])
        mx = sb("mx", [P, 2, NQ])
        top = sb("top", [P, 2, NQ])
        neg = sb("neg", [P, 2, NQ])
        total = sb("total", [P, 2, NQ])
        e_sink = sb("e_sink", [P, 2, NQ])
        denom = sb("denom", [P, 2, NQ])
        inv = sb("inv", [P, 2, NQ])
        eps = sb("eps", [P, 2])
        mq = sb("mq", [P, 7])
        coef = sb("coef", [P, NQ, CHUNK])
        pt_win = sb("pt_win", [P, 2, 512])
        pt_meta = sb("pt_meta", [META, 2, 512])
        pt_mq = sb("pt_mq", [META, P])
        o_norm = sq[:, :, 0:SEQ]
        o_sq = relu[:, :, 0:SEQ]
        o_inv = rpost[:, 0:SEQ]

        landed = [sem(f"landed{s}") for s in range(UNITS)]
        v_landed = [sem(f"v_landed{s}") for s in range(UNITS)]
        small_in = sem("small_in")
        rows_in = sem("rows_in")
        stored = sem("stored")
        consts = sem("consts")
        y_zeroed = sem("y_zeroed")
        pads_zeroed = sem("pads_zeroed")
        hi_ready = sem("hi_ready")
        lo_ready = sem("lo_ready")
        units_used = sem("units_used")
        drained = sem("drained")
        vec = sem("vec")
        sca = sem("sca")
        eps_ready = sem("eps_ready")
        cols_done = sem("cols_done")
        sinks_ready = sem("sinks_ready")
        cols_ready = sem("cols_ready")
        lam_ready = sem("lam_ready")
        turned = sem("turned")
        h_ready = sem("h_ready")
        x_hi_ready = sem("x_hi_ready")
        x_ready = sem("x_ready")
        h_sq_ready = sem("h_sq_ready")
        pre_sum_ready = sem("pre_sum_ready")
        pre_stat = sem("pre_stat")
        pre_std = sem("pre_std")
        y_ready = sem("y_ready")
        y_sq_ready = sem("y_sq_ready")
        y_sum_ready = sem("y_sum_ready")
        post_stat = sem("post_stat")
        post_std = sem("post_std")
        relu_ready = sem("relu_ready")
        z_hi_ready = sem("z_hi_ready")
        z_ready = sem("z_ready")
        kv_ready = sem("kv_ready")
        q_ready = sem("q_ready")
        v_turned = sem("v_turned")
        v_ready = sem("v_ready")
        scores_begun = sem("scores_begun")
        s_done = sem("s_done")
        neg_ready = sem("neg_ready")
        p_ready = sem("p_ready")
        pn_ready = sem("pn_ready")
        pt_done = sem("pt_done")
        pt_win_ready = sem("pt_win_ready")
        pt_meta_ready = sem("pt_meta_ready")
        pv_done = sem("pv_done")
        o_hi_ready = sem("o_hi_ready")
        o_ready = sem("o_ready")
        ms_done = sem("ms_done")
        mneg_ready = sem("mneg_ready")
        mp_ready = sem("mp_ready")
        mpn_ready = sem("mpn_ready")
        mpt_done = sem("mpt_done")
        mpt_ready = sem("mpt_ready")
        mpv_done = sem("mpv_done")
        mo_hi_ready = sem("mo_hi_ready")
        mo_ready = sem("mo_ready")
        dk_ready = sem("dk_ready")
        dq_ready = sem("dq_ready")
        dvt_ready = sem("dvt_ready")
        dv_turned = sem("dv_turned")
        dv_ready = sem("dv_ready")
        ds_done = sem("ds_done")
        dneg_ready = sem("dneg_ready")
        dp_ready = sem("dp_ready")
        coef_ready = sem("coef_ready")
        dt_done = sem("dt_done")
        dt_win_ready = sem("dt_win_ready")
        dt_meta_ready = sem("dt_meta_ready")
        dpv_done = sem("dpv_done")
        o_sq_ready = sem("o_sq_ready")
        o_stat = sem("o_stat")
        o_std = sem("o_std")
        on_ready = sem("on_ready")
        do_hi_ready = sem("do_hi_ready")
        do_ready = sem("do_ready")
        out_turned = sem("out_turned")
        out_ready = sem("out_ready")

        block = ctx.enter_context(nc.Block())
        X = slice(META, L)
        A = slice(0, L)

        @block.sync
        def _(sp):
            def load(G, src, first=False, v_src=None):
                for s in range(UNITS):
                    if not first:
                        sp.wait_ge(lo_ready, UNITS * (G - 1) + s + 1)
                    chunks = slice(UK * s, UK * (s + 1))
                    if v_src is None:
                        sp.dma_start(raw[:, s], src[:, chunks]).then_inc(landed[s], 16)
                    else:
                        sp.dma_start(raw[:, s, :, 0:P], src[:, chunks]).then_inc(landed[s], 16)
                        sp.dma_start(raw[:, s, :, P:GW], v_src[:, chunks]).then_inc(v_landed[s], 16)

            swa_in = a["swa_w_in"][0].rearrange("(k p) n -> p k n", p=P)

            def load_kv(G, j, first=False):
                load(G, swa_in[:, :, bass.ds(D + j * P, P)], first,
                     swa_in[:, :, bass.ds(D + SWA_PAIRS * P + j * P, P)])

            def load_q(G, col):
                load(G, swa_in[:, :, bass.ds(col, GW)])

            load_kv(0, 0, first=True)
            with sp.Fori(0, SWA_PAIRS - 1) as j:
                load_q(3 * j + 1, 2 * GW * j)
                load_q(3 * j + 2, 2 * GW * j + GW)
                load_kv(3 * j + 3, j + 1)
            j = SWA_PAIRS - 1
            load_q(3 * j + 1, 2 * GW * j)
            load_q(3 * j + 2, 2 * GW * j + GW)

            def panel(G, src, col=0):
                with sp.Fori(0, PANEL) as i:
                    load(G + i, src[:, :, bass.ds(col + i * GW, GW)])

            def mlp(G, layer):
                w1 = a["ffn_w1"][layer].rearrange("(k p) n -> p k n", p=P)
                w2 = a["ffn_w2"][layer].rearrange("(b k p) n -> p (b k) n", p=P, b=BLOCKS)
                with sp.Fori(0, BLOCKS) as b:
                    panel(G + 2 * PANEL * b, w1, b * D)
                    panel(G + 2 * PANEL * b + PANEL, w2[:, bass.ds(b * KC, KC), :])

            panel(G_WOUT0, a["swa_w_out"][0].rearrange("(k p) n -> p k n", p=P))
            mlp(G_FFN0, 0)

            diff_in = a["diff_w_in"][0].rearrange("(k p) n -> p k n", p=P)

            def load_diff(G, part, hd):
                load(G, diff_in[:, :, bass.ds(part * D + hd * GW, GW)])

            load_diff(G_DIFF, 2, 0)
            load_diff(G_DIFF + 1, 1, 0)
            with sp.Fori(0, DIFF_HEADS - 1) as hd:
                load_diff(G_DIFF + 2 + 3 * hd, 0, hd)
                load_diff(G_DIFF + 3 + 3 * hd, 2, hd + 1)
                load_diff(G_DIFF + 4 + 3 * hd, 1, hd + 1)
            load_diff(G_DIFF + 2 + 3 * (DIFF_HEADS - 1), 0, DIFF_HEADS - 1)
            panel(G_WOUT1, a["diff_w_out"][0].rearrange("(k p) n -> p k n", p=P))
            mlp(G_FFN1, 1)

            for n in range(2 * 4):
                c4, r = n // 2, n % 2
                sp.wait_ge(out_ready, n + 1)
                sp.dma_start(out[0, P * r:P * (r + 1), 512 * c4:512 * (c4 + 1)],
                             rows[:, r, 512 * c4:512 * (c4 + 1)]).then_inc(stored, 16)
            sp.wait_ge(stored, 16 * 8)

        @block.gpsimd
        def _(pool):
            pool.memset(ident[:, :], 0.0).then_inc(consts, 1)
            pool.memset(ones[:, :], 1.0).then_inc(consts, 1)
            pool.memset(fold[:, :], 0.0).then_inc(consts, 1)
            pool.memset(p_win[:, :, 0, META + CHUNK:], 0.0).then_inc(consts, 1)
            pool.wait_ge(consts, 4)
            pool.affine_select(out=ident[:, :], in_=ident[:, :], compare_op=ALU.not_equal, fill=1.0,
                               base=0, pattern=[[-1, P]], channel_multiplier=1).then_inc(consts, 1)
            pool.affine_select(out=fold[:, :], in_=fold[:, :], compare_op=ALU.not_equal, fill=1.0,
                               base=0, pattern=[[-1, CHUNK]], channel_multiplier=1).then_inc(consts, 1)
            pool.wait_ge(consts, 6)
            pool.affine_select(out=fold[:, :], in_=fold[:, :], compare_op=ALU.not_equal, fill=1.0,
                               base=-CHUNK, pattern=[[-1, CHUNK]], channel_multiplier=1).then_inc(consts, 1)
            for layer, B in ((0, 1), (1, 3)):
                pool.wait_ge(pre_sum_ready, B + 1)
                pool.memset(y[:, :, :], 0.0).then_inc(y_zeroed, 1)
                if layer == 0:
                    pool.memset(p_diff[:, DIFF_N[0]:DIFF_PAD[0]], 0.0).then_inc(pads_zeroed, 1)
                    pool.memset(p_diff[:, DIFF_AT[2] + DIFF_N[2]:DIFF_AT[3]], 0.0).then_inc(pads_zeroed, 1)

        @block.tensor
        def _(pe):
            def group(G, pair, lag, hi, lo, tok, ready=None, at=None):
                n = tok.stop - tok.start
                if not isinstance(G, int) or G - lag + 1 > 0:
                    pe.wait_ge(drained, G - lag + 1)
                for s in range(UNITS):
                    pe.wait_ge(lo_ready, UNITS * G + s + 1)
                    if ready:
                        ready(s)
                    for kk in range(UK):
                        c = UK * s + kk
                        for m in range(GT):
                            acc = ps[:, 2 * pair + m, 0:n]
                            cols = slice(P * m, P * (m + 1))
                            pe.matmul(acc, w_hi[:, s, kk, cols], hi[:, c, tok], start=(c == 0), stop=False)
                            pe.matmul(acc, w_hi[:, s, kk, cols], lo[:, c, tok], start=False, stop=False)
                            last = pe.matmul(acc, w_lo[:, s, kk, cols], hi[:, c, tok], start=False,
                                             stop=(c == KC - 1))
                    last.then_inc(units_used, 1)
                    for work in (at or {}).get(s, ()):
                        work()

            def x_units(B):
                return lambda s: pe.wait_ge(x_ready, KC * B + UK * (s + 1))

            def pre_stat_sum(B, n=L):
                pe.wait_ge(pre_sum_ready, B + 1)
                pe.matmul(ps[:, STAT, 0:n], ones[:, :], pre_sum[:, L - n:L], start=True,
                          stop=True).then_inc(pre_stat, 1)

            def post_stat_sum(p, tok):
                pe.wait_ge(y_sum_ready, PANEL * (p + 1))
                n = tok.stop - tok.start
                for m in range(GT):
                    last = pe.matmul(ps[:, STAT, 0:n], ones[:, :], sq_sum[:, m, tok], start=(m == 0),
                                     stop=(m == GT - 1))
                last.then_inc(post_stat, 1)

            pe.wait_ge(consts, 7)
            pe.wait_ge(small_in, 16 * SMALL_LOADS)
            pe.transpose(ps[:, ATT0, 0:P], gain_rows[:, :], ident[:, :]).then_inc(cols_done, 1)
            pe.transpose(ps[:, ATT1, 0:6], lam_rows[:, :], ident[0:6, 0:6]).then_inc(cols_done, 1)
            pe.wait_ge(rows_in, 16 * 3)
            meta_rows = y[0:META].rearrange("p c t -> p (c t)")
            for c in range(KC):
                if c >= 4:
                    pe.wait_ge(h_ready, c - 3)
                f = slice(P * c, P * (c + 1))
                pe.transpose(ps[:, c % 4, 0:META], meta_rows[:, f], ident[0:META, 0:META])
                for r in range(2):
                    last = pe.transpose(ps[:, c % 4, META + P * r:META + P * (r + 1)], rows[:, r, f],
                                        ident[:, :])
                last.then_inc(turned, 1)
            pe.wait_ge(cols_ready, 3)
            pe.matmul(ps[:, ATT0, 0:2], ones[:, :], lam_prod[:, :], start=True, stop=True).then_inc(cols_done, 1)
            pe.wait_ge(h_ready, KC)

            def v_turn(j):
                pe.wait_ge(kv_ready, j + 1)
                pe.transpose(ps[0:META, AUX, 3 * P:4 * P], vt[:, 0, 0:META], ident[:, :])
                for w in range(3):
                    t0 = META + CHUNK * w
                    last = pe.transpose(ps[:, AUX, P * w:P * (w + 1)], vt[:, 0, t0:t0 + P], ident[:, :])
                last.then_inc(v_turned, 1)

            def swa_scores(j, g):
                pe.wait_ge(q_ready, 2 * j + g + 1)
                pe.sem_inc(scores_begun, 1)
                for t in range(2):
                    for e in range(2):
                        half = slice(CHUNK * e, CHUNK * (e + 1))
                        for c in range(NQ):
                            qc = q[half, 2 * g + t, META + CHUNK * c:META + CHUNK * (c + 1)]
                            keys = [(0, SWA_N[c])] if c < 2 else [(0, META), (META + CHUNK * (c - 1), SWA_WIN)]
                            col = SWA_OFF[c]
                            for k0, nk in keys:
                                last = pe.matmul(ps[half, ATT0 + t, col:col + nk], qc, k[half, g, k0:k0 + nk],
                                                 start=True, stop=True)
                                col += nk
                    last.then_inc(s_done, 1)

            def meta_scores(j):
                for g in range(2):
                    for e in range(2):
                        half = slice(CHUNK * e, CHUNK * (e + 1))
                        r = 32 * (2 * g + e)
                        last = pe.matmul(ps[r:r + 32, AUX, 0:META], q_meta[half, 32 * g:32 * (g + 1)],
                                         k[half, g, 0:META], start=True, stop=True)
                last.then_inc(ms_done, 1)

            def swa_turn(n):
                for t in range(2):
                    pe.wait_ge(pn_ready, n + t + 1)
                    for c in range(NQ):
                        cols = slice(P * c, P * (c + 1))
                        pe.transpose(ps[:, ATT0 + t, cols], p_win[:, t, c, META:], ident[:, :])
                        last = pe.transpose(ps[0:META, AUX + t, cols], p_win[:, t, c, 0:META], ident[:, :])
                    last.then_inc(pt_done, 1)

            def swa_values(n, g):
                for t in range(2):
                    pe.wait_ge(pt_win_ready, n + t + 1)
                    pe.wait_ge(pt_meta_ready, n + t + 1)
                    for e in range(2):
                        half = slice(CHUNK * e, CHUNK * (e + 1))
                        dv = slice(SWA_DH * g, SWA_DH * (g + 1))
                        pm = pt_meta[:, t, :].rearrange("p (c r) -> p c r", c=NQ)[:, :, half]
                        pe.matmul(ps[half, ATT0 + t, 0:SEQ], vwm[:, dv], pm, start=True, stop=False)
                        for c in range(NQ):
                            nk = CHUNK if c == 0 else SWA_WIN
                            r = P * c + CHUNK * e
                            last = pe.matmul(ps[half, ATT0 + t, CHUNK * c:CHUNK * (c + 1)],
                                             vw[0:nk, max(c - 1, 0), dv], pt_win[0:nk, t, r:r + CHUNK],
                                             start=False, stop=(c == NQ - 1))
                    last.then_inc(pv_done, 1)

            def meta_turn(j):
                pe.wait_ge(pt_meta_ready, 4 * j + 3)
                pe.transpose(ps[0:META, AUX, 0:P], p_meta[:, :], ident[:, :]).then_inc(mpt_done, 1)

            def meta_values(j):
                pe.wait_ge(mpt_ready, j + 1)
                for g in range(2):
                    for e in range(2):
                        r = 32 * (2 * g + e)
                        last = pe.matmul(ps[CHUNK * e:CHUNK * (e + 1), STAT, 32 * g:32 * (g + 1)],
                                         vwm[:, SWA_DH * g:SWA_DH * (g + 1)], pt_mq[:, r:r + 32],
                                         start=True, stop=True)
                last.then_inc(mpv_done, 1)

            def first(j):
                return {0: [lambda: swa_scores(j, 0)], 2: [lambda: swa_turn(4 * j)],
                        3: [lambda: swa_values(4 * j, 0)]}

            def second(j):
                n = 4 * j + 2
                return {0: [lambda: swa_scores(j, 1), lambda: meta_scores(j)],
                        2: [lambda: pe.wait_ge(mpn_ready, j + 1), lambda: swa_turn(n)],
                        3: [lambda: meta_turn(j), lambda: swa_values(n, 1), lambda: meta_values(j)]}

            group(G_SWA, 0, 2, x_hi, x_lo, A, x_units(0), {3: [lambda: pre_stat_sum(0)]})

            def pair(j, more):
                group(3 * j + 1, 1, 1, x_hi, x_lo, A, at={0: [lambda: v_turn(j)]})
                group(3 * j + 2, 0, 2, x_hi, x_lo, A, at=first(j))
                if more:
                    group(3 * j + 3, 1, 2, x_hi, x_lo, A, at=second(j))
                else:
                    for works in second(j).values():
                        for work in works:
                            work()

            with pe.Fori(0, SWA_PAIRS - 1) as j:
                pair(j, True)
            pair(SWA_PAIRS - 1, False)

            def panel(G, pair, hi, lo, tok, ready=None, at=None):
                group(G, pair, 2, hi, lo, tok, ready, at)
                group(G + 1, 1 - pair, 2, hi, lo, tok, ready)
                with pe.Fori(1, PANEL // 2) as i:
                    group(G + 2 * i, pair, 2, hi, lo, tok)
                    group(G + 2 * i + 1, 1 - pair, 2, hi, lo, tok)

            def mlp(G, layer, pair, tok, B):
                n = tok.stop - tok.start
                def blocks(b, ready=None, at=None):
                    panel(G + 2 * PANEL * b, pair, x_hi, x_lo, tok, ready, at)
                    z0 = PANEL * (BLOCKS * layer + b)
                    panel(G + 2 * PANEL * b + PANEL, pair, z_hi, z_lo, tok,
                          lambda s: pe.wait_ge(z_ready, z0 + 2 * (s + 1)))
                blocks(0, x_units(B), {3: [lambda: pre_stat_sum(B, n)]})
                with pe.Fori(1, BLOCKS) as b:
                    blocks(b)

            pe.wait_ge(o_ready, 4 * SWA_PAIRS)
            pe.wait_ge(mo_ready, SWA_PAIRS)
            panel(G_WOUT0, 1, z_hi, z_lo, A)
            post_stat_sum(0, A)
            mlp(G_FFN0, 0, 1, A, 1)
            post_stat_sum(1, A)

            def dv_turn(hd):
                pe.wait_ge(dvt_ready, hd + 1)
                for f in range(2):
                    cols = slice(P * f, P * (f + 1))
                    pe.transpose(ps[0:META, ATT1, cols], vt[:, f, 0:META], ident[:, :])
                    for r in range(2):
                        last = pe.transpose(ps[:, AUX, GW * r + P * f:GW * r + P * (f + 1)],
                                            vt[:, f, META + P * r:META + P * (r + 1)], ident[:, :])
                last.then_inc(dv_turned, 1)

            def diff_scores(hd):
                pe.wait_ge(dq_ready, hd + 1)
                for m in range(2):
                    half = slice(CHUNK * m, CHUNK * (m + 1))
                    for c in range(NQ):
                        last = pe.matmul(ps[half, DIFF_BANK[c], DIFF_OFF[c]:DIFF_OFF[c] + DIFF_N[c]],
                                         q[:, m, META + CHUNK * c:META + CHUNK * (c + 1)],
                                         k[:, m, 0:DIFF_N[c]], start=True, stop=True)
                last.then_inc(ds_done, 1)

            def diff_turn(hd):
                pe.wait_ge(coef_ready, hd + 1)
                for c in range(NQ):
                    cols = slice(CHUNK * c, CHUNK * (c + 1))
                    at = DIFF_AT[c]
                    pe.matmul(ps[:, ATT1, cols], p_diff[:, at + META:at + META + P], coef[:, c, :],
                              start=True, stop=True)
                    last = pe.matmul(ps[0:META, ATT0, cols], p_diff[:, at:at + META], coef[:, c, :],
                                     start=True, stop=True)
                    if c >= 2:
                        last = pe.matmul(ps[:, ATT0, GW + CHUNK * (c - 2):GW + CHUNK * (c - 1)],
                                         p_diff[:, at + META + P:at + META + 2 * P], coef[:, c, :],
                                         start=True, stop=True)
                last.then_inc(dt_done, 1)

            def diff_values(hd):
                pe.wait_ge(dt_win_ready, hd + 1)
                pe.wait_ge(dt_meta_ready, hd + 1)
                pe.wait_ge(dv_ready, hd + 1)
                for f in range(2):
                    cols = slice(P * f, P * (f + 1))
                    o = ps[:, STAT, SEQ * f:SEQ * (f + 1)]
                    pe.matmul(o, vm[:, cols], pt_meta[:, 0, 0:SEQ], start=True, stop=False)
                    pe.matmul(o, v[:, 0, cols], pt_win[:, 0, 0:SEQ], start=False, stop=False)
                    last = pe.matmul(ps[:, STAT, SEQ * f + 2 * CHUNK:SEQ * (f + 1)], v[:, 1, cols],
                                     pt_win[:, 1, 0:2 * CHUNK], start=False, stop=True)
                last.then_inc(dpv_done, 1)

            def diff_stat(hd):
                pe.wait_ge(o_sq_ready, hd + 1)
                for f in range(2):
                    last = pe.matmul(ps[:, ATT0, 0:SEQ], ones[:, :], o_sq[:, f, :], start=(f == 0), stop=(f == 1))
                last.then_inc(o_stat, 1)

            pe.wait_ge(pads_zeroed, 2)
            group(G_DIFF, 1, 2, x_hi, x_lo, A, x_units(2), {3: [lambda: pre_stat_sum(2)]})
            group(G_DIFF + 1, 0, 2, x_hi, x_lo, A, at={1: [lambda: dv_turn(0)]})

            def head(hd, more):
                group(G_DIFF + 2 + 3 * hd, 1, 1, x_hi, x_lo, X)
                first = {0: [lambda: diff_scores(hd)], 2: [lambda: diff_turn(hd)], 3: [lambda: diff_values(hd)]}
                second = {0: [lambda: diff_stat(hd)]}
                if more:
                    group(G_DIFF + 3 + 3 * hd, 0, 2, x_hi, x_lo, A, at=first)
                    second[1] = [lambda: dv_turn(hd + 1)]
                    group(G_DIFF + 4 + 3 * hd, 1, 2, x_hi, x_lo, A, at=second)
                else:
                    for works in (*first.values(), *second.values()):
                        for work in works:
                            work()

            with pe.Fori(0, DIFF_HEADS - 1) as hd:
                head(hd, True)
            head(DIFF_HEADS - 1, False)

            pe.wait_ge(do_ready, DIFF_HEADS)
            panel(G_WOUT1, 0, z_hi, z_lo, X)
            post_stat_sum(2, X)
            mlp(G_FFN1, 1, 0, X, 3)
            post_stat_sum(3, X)

            for n in range(8):
                c4, r = n // 2, n % 2
                pe.wait_ge(h_ready, KC * 4 + 4 * (c4 + 1))
                if n >= 4:
                    pe.wait_ge(out_ready, n - 3)
                for i in range(4):
                    last = pe.transpose(ps[:, n % 4, P * i:P * (i + 1)],
                                        h[:, 4 * c4 + i, META + P * r:META + P * (r + 1)], ident[:, :])
                last.then_inc(out_turned, 1)

        @block.scalar
        def _(act):
            own = Tally(act, sca)

            def split_hi(G, s, kv=None):
                act.wait_ge(landed[s], 16 * (G + 1))
                if kv is not None:
                    act.wait_ge(v_landed[s], 16 * (kv + 1))
                if not isinstance(G, int) or G > 0:
                    act.wait_ge(units_used, UNITS * (G - 1) + s + 1)
                act.activation(w_hi[:, s], raw[:, s], ACT.Copy).then_inc(hi_ready, 1)

            def slot(G, at=None, following=True, kv=None):
                for s in range(UNITS):
                    if following:
                        split_hi(G + 1, s, kv)
                    for work in (at or {}).get(s, ()):
                        work()

            def x_split(B, c, gain):
                act.wait_ge(h_ready, KC * B + c + 1)
                act.activation(x_hi[:, c, :], h[:, c, :], ACT.Copy,
                               scale=gains[:, gain + c:gain + c + 1]).then_inc(x_hi_ready, 1)

            def h_square(c):
                act.activation(y[:, c, :], h[:, c, :], ACT.Square).then_inc(h_sq_ready, 1)

            def pre_root(B, n=L):
                act.wait_ge(pre_stat, B + 1)
                act.activation(std[:, L - n:L], ps[:, STAT, 0:n], ACT.Sqrt, bias=eps_norm,
                               scale=1.0 / D).then_inc(pre_std, 1)

            eps_norm = eps[:, 0:1]
            eps_ln = eps[:, 1:2]

            for i, name in enumerate(("mix_pre_g", "mix_post_g", "ffn_pre_g", "ffn_post_g")):
                act.dma_start(gain_rows[2 * KC * i:2 * KC * (i + 1), :],
                              a[name].rearrange("l (c p) -> (l c) p", p=P)).then_inc(small_in, 16)
            for i, name in enumerate(("diff_lam_q1", "diff_lam_k1", "diff_lam_q2", "diff_lam_k2")):
                act.dma_start(lam_rows[i:i + 1, :], a[name]).then_inc(small_in, 16)
            act.dma_start(lam_rows[4:6, :], a["diff_subln_g"][0].rearrange("(c p) -> c p", p=P)).then_inc(small_in, 16)
            act.dma_start(y[0:META].rearrange("p c t -> p (c t)")[:, 0:D], a["meta_tokens"]).then_inc(rows_in, 16)
            for r in range(2):
                act.dma_start(rows[:, r, :], a["x"][0, P * r:P * (r + 1), :]).then_inc(rows_in, 16)
            act.dma_start(sink_rows[:, :], a["swa_sinks"].broadcast_to([P, 2 * KC])).then_inc(small_in, 16)

            for s in range(UNITS):
                split_hi(0, s, 0)
            act.wait_ge(eps_ready, 2)
            act.wait_ge(cols_ready, 1)
            for c in range(KC):
                x_split(0, c, column(MIX_PRE, 0, 0))
            act.wait_ge(turned, KC)
            for c in range(KC):
                h_square(c)
            act.wait_ge(sinks_ready, 1)
            act.wait_ge(cols_done, 3)
            act.activation(lam_exp[:, :], ps[:, ATT0, 0:2], ACT.Exp).then_inc(lam_ready, 1)

            def swa_exp(n):
                for t in range(2):
                    act.wait_ge(neg_ready, n + t + 1)
                    for c in range(NQ):
                        act.activation(p_win[:, t, c, 0:SWA_N[c]],
                                       ps[:, ATT0 + t, SWA_OFF[c]:SWA_OFF[c] + SWA_N[c]], ACT.Exp,
                                       bias=neg[:, t, c:c + 1], scale=SWA_DH ** -0.5,
                                       accum_out=total[:, t, c:c + 1])
                    act.activation(e_sink[:, t, :], neg[:, t, :], ACT.Exp,
                                   bias=sink_at(n, t)).then_inc(p_ready, 1)

            def sink_at(n, t):
                return sink[:, bass.ds(n + t, 1)]

            def meta_exp(j):
                act.wait_ge(mneg_ready, j + 1)
                act.activation(p_meta[:, :], ps[:, AUX, 0:META], ACT.Exp, bias=mq[:, 2:3],
                               scale=SWA_DH ** -0.5, accum_out=mq[:, 3:4])
                act.activation(mq[:, 4:5], mq[:, 2:3], ACT.Exp,
                               bias=sink_meta[:, bass.ds(j, 1)]).then_inc(mp_ready, 1)

            def swa_pt_meta(n):
                for t in range(2):
                    act.wait_ge(pt_done, n + t + 1)
                    act.activation(pt_meta[:, t, :], ps[0:META, AUX + t, :], ACT.Copy).then_inc(pt_meta_ready, 1)

            def swa_o_hi(n):
                for t in range(2):
                    act.wait_ge(pv_done, n + t + 1)
                    act.activation(z_hi[:, bass.ds(n + t, 1), X], ps[:, ATT0 + t, 0:SEQ].unsqueeze(1),
                                   ACT.Copy).then_inc(o_hi_ready, 1)

            def meta_o_hi(j):
                act.wait_ge(mpv_done, j + 1)
                act.activation(z_hi[:, bass.ds(4 * j, 4), 0:META],
                               ps[:, STAT, 0:4 * META].rearrange("p (t q) -> p t q", t=4),
                               ACT.Copy).then_inc(mo_hi_ready, 1)

            def first(j):
                n = 4 * j
                return {0: [lambda: swa_exp(n)], 2: [lambda: swa_pt_meta(n)], 3: [lambda: swa_o_hi(n)]}

            def second(j):
                n = 4 * j + 2
                return {0: [lambda: swa_exp(n), lambda: meta_exp(j)], 2: [lambda: swa_pt_meta(n)],
                        3: [lambda: swa_o_hi(n), lambda: meta_o_hi(j)]}

            slot(G_SWA)
            pre_root(0)

            def pair(j, more):
                slot(3 * j + 1)
                slot(3 * j + 2, first(j), kv=j + 1 if more else None)
                if more:
                    slot(3 * j + 3, second(j))
                else:
                    for works in second(j).values():
                        for work in works:
                            work()

            with act.Fori(0, SWA_PAIRS - 1) as j:
                pair(j, True)
            pair(SWA_PAIRS - 1, False)

            def y_square(p, i):
                act.wait_ge(y_ready, PANEL * p + i + 1)
                act.activation(sq[:, :, :], y[:, bass.ds(GT * i, GT), :], ACT.Square).then_inc(y_sq_ready, 1)

            def final_panel(G, p, following=True):
                with act.Fori(0, PANEL - 1) as i:
                    slot(G + i)
                    y_square(p, i)
                slot(G + PANEL - 1, following=following)
                y_square(p, PANEL - 1)

            def post_root(p, tok):
                act.wait_ge(post_stat, p + 1)
                n = tok.stop - tok.start
                act.activation(std[:, tok], ps[:, STAT, 0:n], ACT.Sqrt, bias=eps_norm,
                               scale=1.0 / D).then_inc(post_std, 1)

            def mlp(G, layer, p, B, n, following):
                def hidden(b, i):
                    act.wait_ge(relu_ready, PANEL * (BLOCKS * layer + b) + i + 1)
                    own.mark(act.activation(sq[:, :, :], relu[:, :, :], ACT.Square))
                    own.wait()
                    act.activation(z_hi[:, bass.ds(GT * i, GT), :], sq[:, :, :], ACT.Copy).then_inc(z_hi_ready, 1)

                def up(b, i0=0):
                    G1 = G + 2 * PANEL * b
                    with act.Fori(i0, PANEL) as i, own.turns(i - i0, PANEL - i0, 1):
                        slot(G1 + i)
                        hidden(b, i)

                slot(G)
                pre_root(B, n)
                hidden(0, 0)
                up(0, 1)
                with act.Fori(0, PANEL) as i:
                    slot(G + PANEL + i)
                with act.Fori(1, BLOCKS - 1) as b, own.turns(b - 1, BLOCKS - 2, PANEL):
                    up(b)
                    with act.Fori(0, PANEL) as i:
                        slot(G + 2 * PANEL * b + PANEL + i)
                up(BLOCKS - 1)
                final_panel(G + (2 * BLOCKS - 1) * PANEL, p, following)

            def boundary(B, p, gain):
                post_root(p, A if p < 2 else X)
                for c in range(KC):
                    x_split(B, c, gain)
                    h_square(c)

            final_panel(G_WOUT0, 0)
            boundary(1, 0, column(FFN_PRE, 0, 0))
            mlp(G_FFN0, 0, 1, 1, L, True)
            boundary(2, 1, column(MIX_PRE, 1, 0))

            def diff_exp(hd):
                act.wait_ge(dneg_ready, hd + 1)
                for c in range(NQ):
                    last = act.activation(p_diff[:, DIFF_AT[c]:DIFF_AT[c] + DIFF_N[c]],
                                          ps[:, DIFF_BANK[c], DIFF_OFF[c]:DIFF_OFF[c] + DIFF_N[c]], ACT.Exp,
                                          bias=neg[:, 0, c:c + 1], scale=P ** -0.5,
                                          accum_out=total[:, 0, c:c + 1])
                last.then_inc(dp_ready, 1)

            def diff_pt_meta(hd):
                act.wait_ge(dt_done, hd + 1)
                act.activation(pt_meta[:, 0, 0:SEQ], ps[0:META, ATT0, 0:SEQ], ACT.Copy)
                act.activation(pt_win[:, 1, 0:2 * CHUNK], ps[:, ATT0, SEQ:SEQ + 2 * CHUNK],
                               ACT.Copy).then_inc(dt_meta_ready, 1)

            def diff_square(hd):
                act.wait_ge(dpv_done, hd + 1)
                act.activation(o_sq, ps[:, STAT, :].rearrange("p (f t) -> p f t", f=2),
                               ACT.Square).then_inc(o_sq_ready, 1)

            def diff_root(hd):
                act.wait_ge(o_stat, hd + 1)
                act.activation(std[:, 0:SEQ], ps[:, ATT0, 0:SEQ], ACT.Sqrt, bias=eps_ln,
                               scale=1.0 / GW).then_inc(o_std, 1)

            def diff_o_hi(hd):
                act.wait_ge(on_ready, hd + 1)
                act.activation(z_hi[:, bass.ds(2 * hd, 2), X], o_norm, ACT.Copy).then_inc(do_hi_ready, 1)

            slot(G_DIFF)
            pre_root(2)
            slot(G_DIFF + 1)

            def head(hd, more):
                slot(G_DIFF + 2 + 3 * hd)
                first = {0: [lambda: diff_exp(hd)], 2: [lambda: diff_pt_meta(hd)], 3: [lambda: diff_square(hd)]}
                second = {0: [lambda: diff_root(hd)], 1: [lambda: diff_o_hi(hd)]}
                if more:
                    slot(G_DIFF + 3 + 3 * hd, first)
                    slot(G_DIFF + 4 + 3 * hd, second)
                else:
                    for works in (*first.values(), *second.values()):
                        for work in works:
                            work()

            with act.Fori(0, DIFF_HEADS - 1) as hd:
                head(hd, True)
            head(DIFF_HEADS - 1, False)

            final_panel(G_WOUT1, 2)
            boundary(3, 2, column(FFN_PRE, 1, 0))
            mlp(G_FFN1, 1, 3, 3, SEQ, False)
            post_root(3, X)
            for n in range(8):
                c4, r = n // 2, n % 2
                act.wait_ge(out_turned, n + 1)
                act.activation(rows[:, r, 512 * c4:512 * (c4 + 1)], ps[:, n % 4, :], ACT.Copy).then_inc(out_ready, 1)

        @block.vector
        def _(dve):
            own = Tally(dve, vec)

            def split_lo(G, s):
                dve.wait_ge(hi_ready, UNITS * G + s + 1)
                dve.tensor_tensor(w_lo[:, s], raw[:, s], w_hi[:, s].bitcast(F32), ALU.subtract).then_inc(lo_ready, 1)

            def slot(G, at=None, following=True):
                for s in range(UNITS):
                    if following:
                        split_lo(G + 1, s)
                    for work in (at or {}).get(s, ()):
                        work()

            def group_done(G):
                dve.wait_ge(units_used, UNITS * (G + 1))

            def scaled(out_, pair, tok):
                n = tok.stop - tok.start
                return dve.tensor_tensor(out_, ps[:, 2 * pair:2 * pair + 2, 0:n],
                                         rstd[:, tok].unsqueeze(1).broadcast_to([P, 2, n]), ALU.mult)

            def x_lo_split(B, c, gain):
                dve.wait_ge(x_hi_ready, KC * B + c + 1)
                dve.scalar_tensor_tensor(x_lo[:, c, :], h[:, c, :], gains[:, gain + c:gain + c + 1],
                                         x_hi[:, c, :].bitcast(F32), ALU.mult, ALU.subtract).then_inc(x_ready, 1)

            def h_sum(B):
                dve.wait_ge(h_sq_ready, KC * (B + 1))
                dve.tensor_reduce(pre_sum[:, :], y[:, :, :].rearrange("p c t -> p t c"), AX.X,
                                  ALU.add).then_inc(pre_sum_ready, 1)

            def pre_inverse(B):
                dve.wait_ge(pre_std, B + 1)
                own.mark(dve.reciprocal(rstd[:, :], std[:, :]))
                own.wait()

            dve.memset(eps[:, 0:1], NORM_EPS).then_inc(eps_ready, 1)
            dve.memset(eps[:, 1:2], LN_EPS).then_inc(eps_ready, 1)
            own.mark(dve.memset(map_sign[:, :], 1.0))
            dve.wait_ge(cols_done, 1)
            dve.tensor_copy(gains[:, :], ps[:, ATT0, 0:P]).then_inc(cols_ready, 1)
            dve.wait_ge(cols_done, 2)
            dve.tensor_copy(lam_cols[:, :], ps[:, ATT1, 0:6]).then_inc(cols_ready, 1)
            dve.wait_ge(cols_ready, 2)
            own.mark(dve.tensor_scalar(sub_gain[:, :], lam_cols[:, 4:6], 1.0 - LAMBDA_INIT, None, ALU.mult))
            dve.tensor_tensor(lam_prod[:, :], lam_cols[:, 0:4:2], lam_cols[:, 1:4:2], ALU.mult).then_inc(cols_ready, 1)
            dve.wait_ge(small_in, 16 * SMALL_LOADS)
            for e in range(2):
                half = slice(CHUNK * e, CHUNK * (e + 1))
                own.mark(dve.tensor_copy(sink[half, :], sink_rows[half, e:2 * KC:2]))
            dve.wait_ge(consts, 7)
            own.mark(dve.tensor_reduce(row_tile[:, :], ident[:, :].rearrange("p (a t b) -> p t a b", a=4, t=2),
                                       AX.XY, ALU.add))
            own.wait()
            for g in range(2):
                for e in range(2):
                    r = slice(32 * (2 * g + e), 32 * (2 * g + e) + 32)
                    of_tile = [sink_rows[r, 4 * g + 2 * t + e:2 * KC:8] for t in range(2)]
                    own.mark(dve.tensor_scalar(sink_part[r, :], of_tile[0], row_tile[r, 0:1], None, ALU.mult))
                    own.wait()
                    own.mark(dve.scalar_tensor_tensor(sink_meta[r, :], of_tile[1], row_tile[r, 1:2],
                                                      sink_part[r, :], ALU.mult, ALU.add))
            own.wait()
            dve.sem_inc(sinks_ready, 1)
            for s in range(UNITS):
                split_lo(0, s)
            for c in range(KC):
                dve.wait_ge(turned, c + 1)
                dve.tensor_copy(h[:, c, :], ps[:, c % 4, 0:L]).then_inc(h_ready, 1)
                if c:
                    x_lo_split(0, c - 1, column(MIX_PRE, 0, 0))
            x_lo_split(0, KC - 1, column(MIX_PRE, 0, 0))
            h_sum(0)
            dve.wait_ge(lam_ready, 1)
            own.wait()
            own.mark(dve.scalar_tensor_tensor(map_sign[CHUNK:P, :], lam_exp[CHUNK:P, 1:2], -LAMBDA_INIT,
                                              lam_exp[CHUNK:P, 0:1], ALU.add, ALU.subtract))

            def kv_out(G, j, pair):
                group_done(G)
                b = 2 * pair
                for g in range(2):
                    src = slice(CHUNK * g, CHUNK * (g + 1))
                    for e in range(2):
                        dve.tensor_tensor(k[CHUNK * e:CHUNK * (e + 1), g, :], ps[src, b, 0:L], rstd[src, :], ALU.mult)
                dve.tensor_tensor(vt[:, 0, :], ps[:, b + 1, 0:L], rstd[:, :], ALU.mult).then_inc(kv_ready, 1)
                free(kv_ready, j + 1)

            def free(made, value):
                dve.wait_ge(made, value)
                dve.sem_inc(drained, 1)

            def q_out(G, j, g, pair):
                group_done(G)
                dve.tensor_tensor(q_meta[:, 32 * g:32 * (g + 1)].rearrange("p (t q) -> p t q", t=2),
                                  ps[:, 2 * pair:2 * pair + 2, 0:META],
                                  rstd[:, 0:META].unsqueeze(1).broadcast_to([P, 2, META]), ALU.mult)
                scaled(q[:, 2 * g:2 * g + 2, :], pair, A).then_inc(q_ready, 1)
                free(q_ready, 2 * j + g + 1)

            def v_out(j):
                dve.wait_ge(v_turned, j + 1)
                dve.tensor_copy(vw, ps[:, AUX, 0:3 * P].rearrange("p (w d) -> p w d", w=3))
                dve.tensor_copy(vwm, ps[0:META, AUX, 3 * P:4 * P]).then_inc(v_ready, 1)

            def swa_max(n):
                for t in range(2):
                    dve.wait_ge(s_done, n + t + 1)
                    b = ATT0 + t
                    dve.tensor_reduce(mx[:, t, 0:1], ps[:, b, 0:SWA_N[0]], AX.X, ALU.max)
                    own.mark(dve.tensor_reduce(mx[:, t, 1:NQ],
                                               ps[:, b, SWA_N[0]:].rearrange("p (c k) -> p c k", k=SWA_KEYS),
                                               AX.X, ALU.max))
                    own.wait()
                    own.mark(dve.tensor_scalar(top[:, t, :], mx[:, t, :], SWA_DH ** -0.5,
                                               sink[:, bass.ds(n + t, 1)], ALU.mult, ALU.max))
                    own.wait()
                    dve.tensor_scalar(neg[:, t, :], top[:, t, :], -1.0, None, ALU.mult).then_inc(neg_ready, 1)

            def meta_max(j):
                dve.wait_ge(ms_done, j + 1)
                own.mark(dve.tensor_reduce(mq[:, 0:1], ps[:, AUX, 0:META], AX.X, ALU.max))
                own.wait()
                own.mark(dve.tensor_scalar(mq[:, 1:2], mq[:, 0:1], SWA_DH ** -0.5,
                                           sink_meta[:, bass.ds(j, 1)], ALU.mult, ALU.max))
                own.wait()
                dve.tensor_scalar(mq[:, 2:3], mq[:, 1:2], -1.0, None, ALU.mult).then_inc(mneg_ready, 1)

            def swa_norm(n):
                for t in range(2):
                    dve.wait_ge(p_ready, n + t + 1)
                    own.mark(dve.tensor_tensor(denom[:, t, :], total[:, t, :], e_sink[:, t, :], ALU.add))
                    own.wait()
                    own.mark(dve.reciprocal(inv[:, t, :], denom[:, t, :]))
                    own.wait()
                    for c in range(NQ):
                        last = dve.tensor_scalar(p_win[:, t, c, 0:SWA_N[c]], p_win[:, t, c, 0:SWA_N[c]],
                                                 inv[:, t, c:c + 1], None, ALU.mult)
                    last.then_inc(pn_ready, 1)

            def meta_norm(j):
                dve.wait_ge(mp_ready, j + 1)
                own.mark(dve.tensor_tensor(mq[:, 5:6], mq[:, 3:4], mq[:, 4:5], ALU.add))
                own.wait()
                own.mark(dve.reciprocal(mq[:, 6:7], mq[:, 5:6]))
                own.wait()
                dve.tensor_scalar(p_meta[:, :], p_meta[:, :], mq[:, 6:7], None, ALU.mult).then_inc(mpn_ready, 1)

            def swa_pt_win(n):
                for t in range(2):
                    dve.wait_ge(pt_done, n + t + 1)
                    dve.tensor_copy(pt_win[:, t, :], ps[:, ATT0 + t, :]).then_inc(pt_win_ready, 1)

            def meta_pt(j):
                dve.wait_ge(mpt_done, j + 1)
                dve.tensor_copy(pt_mq[:, :], ps[0:META, AUX, 0:P]).then_inc(mpt_ready, 1)

            def swa_o_lo(n):
                for t in range(2):
                    dve.wait_ge(o_hi_ready, n + t + 1)
                    tile = bass.ds(n + t, 1)
                    dve.tensor_tensor(z_lo[:, tile, X], ps[:, ATT0 + t, 0:SEQ].unsqueeze(1),
                                      z_hi[:, tile, X].bitcast(F32), ALU.subtract).then_inc(o_ready, 1)

            def meta_o_lo(j):
                dve.wait_ge(mo_hi_ready, j + 1)
                tiles = bass.ds(4 * j, 4)
                dve.tensor_tensor(z_lo[:, tiles, 0:META], ps[:, STAT, 0:4 * META].rearrange("p (t q) -> p t q", t=4),
                                  z_hi[:, tiles, 0:META].bitcast(F32), ALU.subtract).then_inc(mo_ready, 1)

            def first(j):
                n = 4 * j
                return {0: [lambda: swa_max(n)], 1: [lambda: swa_norm(n)], 2: [lambda: swa_pt_win(n)],
                        3: [lambda: swa_o_lo(n)]}

            def second(j):
                n = 4 * j + 2
                return {0: [lambda: swa_max(n), lambda: meta_max(j)], 1: [lambda: swa_norm(n), lambda: meta_norm(j)],
                        2: [lambda: swa_pt_win(n)], 3: [lambda: meta_pt(j), lambda: swa_o_lo(n), lambda: meta_o_lo(j)]}

            slot(G_SWA)
            pre_inverse(0)
            kv_out(G_SWA, 0, 0)

            def pair(j, more):
                slot(3 * j + 1, {0: [lambda: v_out(j)]})
                q_out(3 * j + 1, j, 0, 1)
                slot(3 * j + 2, first(j))
                q_out(3 * j + 2, j, 1, 0)
                if more:
                    slot(3 * j + 3, second(j))
                    kv_out(3 * j + 3, j + 1, 1)
                else:
                    for works in second(j).values():
                        for work in works:
                            work()

            SWA_STEPS = 20
            with dve.Fori(0, SWA_PAIRS - 1) as j, own.turns(j, SWA_PAIRS - 1, SWA_STEPS):
                pair(j, True)
            pair(SWA_PAIRS - 1, False)

            def clear_sum():
                own.mark(dve.memset(sq_sum[:, :, :], 0.0))

            def y_sum(p, i):
                dve.wait_ge(y_sq_ready, PANEL * p + i + 1)
                own.wait()
                own.mark(dve.tensor_tensor(sq_sum[:, :, :], sq_sum[:, :, :], sq[:, :, :], ALU.add))
                own.wait()
                dve.sem_inc(y_sum_ready, 1)

            def tiles_of(i):
                return bass.ds(GT * i, GT)

            def columns(tok):
                return tok.stop - tok.start

            def final_panel(G, p, tok, bank0, add, following=True):
                def out_(i, pair):
                    group_done(G + i)
                    src = ps[:, 2 * pair:2 * pair + 2, 0:columns(tok)]
                    dst = y[:, tiles_of(i), tok]
                    if add:
                        dve.tensor_tensor(dst, dst, src, ALU.add).then_inc(y_ready, 1)
                    else:
                        dve.tensor_copy(dst, src).then_inc(y_ready, 1)
                    free(y_ready, PANEL * p + i + 1)
                    y_sum(p, i)
                clear_sum()
                with dve.Fori(0, PANEL // 2 - 1) as i, own.turns(i, PANEL // 2 - 1, 2):
                    for o in range(2):
                        slot(G + 2 * i + o)
                        out_(2 * i + o, bank0 ^ o)
                for o in range(2):
                    i = PANEL - 2 + o
                    slot(G + i, following=following or o == 0)
                    out_(i, bank0 ^ o)

            def boundary(B, p, post, pre, tok):
                dve.wait_ge(post_std, p + 1)
                own.mark(dve.reciprocal(rpost[:, tok], std[:, tok]))
                own.wait()
                scaled_y = []
                for c in range(KC + 2):
                    if c < KC:
                        own.mark(dve.scalar_tensor_tensor(y[:, c, tok], y[:, c, tok], gains[:, post + c:post + c + 1],
                                                          rpost[:, tok], ALU.mult, ALU.mult))
                        scaled_y.append(own.value)
                    if 1 <= c <= KC:
                        dve.wait_ge(vec, scaled_y[c - 1])
                        dve.tensor_tensor(h[:, c - 1, tok], h[:, c - 1, tok], y[:, c - 1, tok],
                                          ALU.add).then_inc(h_ready, 1)
                    if c >= 2 and pre is not None:
                        x_lo_split(B, c - 2, pre)
                if pre is not None:
                    h_sum(B)

            def mlp(G, layer, p, B, tok, bank0, following):
                n = columns(tok)

                def up_out(b, i, pair):
                    group_done(G + 2 * PANEL * b + i)
                    number = PANEL * (BLOCKS * layer + b) + i + 1
                    dve.scalar_tensor_tensor(relu[:, :, tok], ps[:, 2 * pair:2 * pair + 2, 0:n], 0.0,
                                             rstd[:, tok].unsqueeze(1).broadcast_to([P, 2, n]), ALU.max,
                                             ALU.mult).then_inc(relu_ready, 1)
                    free(relu_ready, number)
                    dve.wait_ge(z_hi_ready, number)
                    dve.tensor_tensor(z_lo[:, tiles_of(i), :], sq[:, :, :], z_hi[:, tiles_of(i), :].bitcast(F32),
                                      ALU.subtract).then_inc(z_ready, 1)

                def up(b, start=0):
                    with dve.Fori(start, PANEL // 2) as i:
                        for o in range(2):
                            slot(G + 2 * PANEL * b + 2 * i + o)
                            up_out(b, 2 * i + o, bank0 ^ o)

                def down(b):
                    G2 = G + 2 * PANEL * b + PANEL
                    with dve.Fori(0, PANEL // 2) as i, own.turns(i, PANEL // 2, 2):
                        for o in range(2):
                            slot(G2 + 2 * i + o)
                            group_done(G2 + 2 * i + o)
                            dst = y[:, tiles_of(2 * i + o), tok]
                            own.mark(dve.tensor_tensor(dst, dst, ps[:, 2 * (bank0 ^ o):2 * (bank0 ^ o) + 2, 0:n], ALU.add))
                            own.wait()
                            dve.sem_inc(drained, 1)

                slot(G)
                pre_inverse(B)
                up_out(0, 0, bank0)
                slot(G + 1)
                up_out(0, 1, bank0 ^ 1)
                up(0, 1)
                dve.wait_ge(y_zeroed, layer + 1)
                down(0)
                with dve.Fori(1, BLOCKS - 1) as b, own.turns(b - 1, BLOCKS - 2, PANEL):
                    up(b)
                    down(b)
                up(BLOCKS - 1)
                final_panel(G + (2 * BLOCKS - 1) * PANEL, p, tok, bank0, True, following)

            final_panel(G_WOUT0, 0, A, 1, False)
            boundary(1, 0, column(MIX_POST, 0, 0), column(FFN_PRE, 0, 0), A)
            mlp(G_FFN0, 0, 1, 1, A, 1, True)
            boundary(2, 1, column(FFN_POST, 0, 0), column(MIX_PRE, 1, 0), A)

            def tiles_out(G, dst, pair, tok, made, value):
                group_done(G)
                scaled(dst, pair, tok).then_inc(made, 1)
                free(made, value)

            def dv_out(hd):
                dve.wait_ge(dv_turned, hd + 1)
                dve.tensor_copy(v[:, :, :], ps[:, AUX, :].rearrange("p (r f) -> p r f", r=2))
                dve.tensor_copy(vm[:, :], ps[0:META, ATT1, 0:GW]).then_inc(dv_ready, 1)

            def diff_max(hd):
                dve.wait_ge(ds_done, hd + 1)
                for c in range(NQ):
                    last = dve.tensor_reduce(mx[:, 0, c:c + 1],
                                             ps[:, DIFF_BANK[c], DIFF_OFF[c]:DIFF_OFF[c] + DIFF_N[c]], AX.X, ALU.max)
                own.mark(last)
                own.wait()
                dve.tensor_scalar(neg[:, 0, :], mx[:, 0, :], -(P ** -0.5), None, ALU.mult).then_inc(dneg_ready, 1)

            def diff_coef(hd):
                dve.wait_ge(dp_ready, hd + 1)
                own.mark(dve.reciprocal(inv[:, 0, :], total[:, 0, :]))
                own.wait()
                for c in range(NQ):
                    last = dve.tensor_scalar(coef[:, c, :], fold[:, :], inv[:, 0, c:c + 1], map_sign[:, 0:1],
                                             ALU.mult, ALU.mult)
                last.then_inc(coef_ready, 1)

            def diff_pt_win(hd):
                dve.wait_ge(dt_done, hd + 1)
                dve.tensor_copy(pt_win[:, 0, 0:SEQ], ps[:, ATT1, 0:SEQ]).then_inc(dt_win_ready, 1)

            def diff_norm(hd):
                dve.wait_ge(o_std, hd + 1)
                own.mark(dve.reciprocal(o_inv, std[:, 0:SEQ]))
                own.wait()
                for f in range(2):
                    last = dve.scalar_tensor_tensor(o_norm[:, f, :], ps[:, STAT, SEQ * f:SEQ * (f + 1)],
                                                    sub_gain[:, f:f + 1], o_inv, ALU.mult, ALU.mult)
                last.then_inc(on_ready, 1)

            def diff_o_lo(hd):
                dve.wait_ge(do_hi_ready, hd + 1)
                dve.tensor_tensor(z_lo[:, bass.ds(2 * hd, 2), X], o_norm, z_hi[:, bass.ds(2 * hd, 2), X].bitcast(F32),
                                  ALU.subtract).then_inc(do_ready, 1)

            dve.wait_ge(consts, 7)
            slot(G_DIFF)
            pre_inverse(2)
            tiles_out(G_DIFF, vt[:, :, :], 1, A, dvt_ready, 1)
            slot(G_DIFF + 1, {1: [lambda: dv_out(0)]})
            tiles_out(G_DIFF + 1, k[:, :, :], 0, A, dk_ready, 1)

            def head(hd, more):
                G = G_DIFF + 2 + 3 * hd
                slot(G)
                tiles_out(G, q[:, 0:2, X], 1, X, dq_ready, hd + 1)
                first = {0: [lambda: diff_max(hd)], 1: [lambda: diff_coef(hd)], 2: [lambda: diff_pt_win(hd)]}
                second = {0: [lambda: diff_norm(hd)], 1: [lambda: diff_o_lo(hd)]}
                if more:
                    slot(G + 1, first)
                    tiles_out(G + 1, vt[:, :, :], 0, A, dvt_ready, hd + 2)
                    second[1].append(lambda: dv_out(hd + 1))
                    slot(G + 2, second)
                    tiles_out(G + 2, k[:, :, :], 1, A, dk_ready, hd + 2)
                else:
                    for works in (*first.values(), *second.values()):
                        for work in works:
                            work()

            DIFF_STEPS = 3
            with dve.Fori(0, DIFF_HEADS - 1) as hd, own.turns(hd, DIFF_HEADS - 1, DIFF_STEPS):
                head(hd, True)
            head(DIFF_HEADS - 1, False)

            final_panel(G_WOUT1, 2, X, 0, False)
            boundary(3, 2, column(MIX_POST, 1, 0), column(FFN_PRE, 1, 0), X)
            mlp(G_FFN1, 1, 3, 3, X, 0, False)
            boundary(4, 3, column(FFN_POST, 1, 0), None, X)


INPUTS = ["x", "meta_tokens", "mix_pre_g", "mix_post_g", "ffn_pre_g", "ffn_post_g", "swa_w_in", "swa_sinks",
          "swa_w_out", "diff_w_in", "diff_lam_q1", "diff_lam_k1", "diff_lam_q2", "diff_lam_k2", "diff_subln_g",
          "diff_w_out", "ffn_w1", "ffn_w2"]


def kernel(**inputs):
    import concourse.bacc as bacc
    from concourse.bass_utils import run_bass_kernel_spmd

    nc = bacc.Bacc("TRN2", target_bir_lowering=False, num_devices=1)
    arrays, args = {}, {}
    for name in INPUTS:
        value = np.ascontiguousarray(inputs[name])
        arrays[name] = value
        args[name] = nc.dram_tensor(name, value.shape, mybir.dt.from_np(value.dtype), kind="ExternalInput").ap()
    out = nc.dram_tensor("out", (1, SEQ, D), F32, kind="ExternalOutput").ap()
    trunk(nc, args, out)
    result = run_bass_kernel_spmd(nc, [arrays], core_ids=[0])
    return result.results[0]["out"]
```

```python
from contextlib import ExitStack, contextmanager
import math

import numpy as np
import concourse.bass as bass
from concourse import mybir
from concourse.alu_op_type import AluOpType as ALU

F32 = mybir.dt.float32
F32R = mybir.dt.float32r
ACT = mybir.ActivationFunctionType
AX = mybir.AxisListType

P = 128
D = 2048
SEQ = 256
META = 16
L = META + SEQ
KC = D // P
D_FF = 4 * D
NORM_EPS = 1e-6
LN_EPS = 1e-5
CHUNK = 64
NQ = SEQ // CHUNK

UNITS = 4
UK = KC // UNITS
GW = 256
GT = GW // P

SWA_DH = 64
SWA_KV = 8
SWA_PAIRS = SWA_KV // 2
KV_GROUPS = 2 * SWA_KV * SWA_DH // GW
META_PAD = 32
SWA_WIN = 2 * CHUNK
SWA_KEYS = META + SWA_WIN
DIFF_HEADS = 8
PANEL = D // GW
BLOCKS = D_FF // D

G_SWA = 0
G_SWA_Q = G_SWA + KV_GROUPS
G_WOUT0 = G_SWA_Q + PANEL
G_FFN0 = G_WOUT0 + PANEL
G_DIFF = G_FFN0 + 2 * PANEL * BLOCKS
G_WOUT1 = G_DIFF + 3 * DIFF_HEADS
G_FFN1 = G_WOUT1 + PANEL
GROUPS = G_FFN1 + 2 * PANEL * BLOCKS

LAMBDA_INIT = 0.8 - 0.6 * math.exp(-0.3)
GAIN_LOADS = 4
SMALL_LOADS = 4 + 1 + 1
MIX_PRE, MIX_POST, FFN_PRE, FFN_POST = range(4)

ATT0, ATT1, AUX, STAT = 4, 5, 6, 7

SWA_N = [META + CHUNK] + [SWA_KEYS] * 3
SWA_OFF = [0, 80, 224, 368]
DIFF_N = [META + CHUNK * (c + 1) for c in range(NQ)]
DIFF_BANK = [ATT0, ATT1, ATT1, ATT0]
DIFF_OFF = [0, 0, DIFF_N[1], DIFF_N[0]]
DIFF_PAD = [META + P, META + P, META + 2 * P, META + 2 * P]
DIFF_AT = [0, 144, 288, 560]
DIFF_P = 832

Y_STEPS = PANEL + 1


BY_CHUNK = [(g, s) for s in range(UNITS) for g in range(2)]
LATE_LAST = [(g, s) for g in range(2) for s in range(UNITS - 1)] + [(0, UNITS - 1), (1, UNITS - 1)]
FIRST_DONE = 6

SPLITS = {7: [4], 11: [5, 6], 15: [7]}
FIRST_SPLITS = {5: [0], 7: [1], 9: [2], 11: [3], 13: [4], 15: [5, 6, 7]}


def column(which, layer, c):
    return which * 2 * KC + layer * KC + c


class Tally:

    def __init__(self, eng, sem):
        self.eng, self.sem, self.value, self.marks = eng, sem, 0, 0

    def mark(self, instruction):
        instruction.then_inc(self.sem, 1)
        self.value = self.value + 1
        self.marks += 1

    def wait(self):
        self.eng.wait_ge(self.sem, self.value)

    @contextmanager
    def turns(self, i, count, per):
        before, marks = self.value, self.marks
        self.value = before + i * per
        yield
        assert self.marks - marks == per, (self.marks - marks, per)
        self.value, self.marks = before + count * per, marks + count * per


def trunk(nc, a, out):
    ctx = ExitStack()
    with ctx:
        def sb(name, shape, dt=F32):
            return ctx.enter_context(nc.sbuf_tensor(name, shape, dt))

        def sem(name):
            return ctx.enter_context(nc.semaphore(name))

        ps = ctx.enter_context(nc.psum_tensor("ps", [P, 8, 512], F32))

        raw = sb("raw", [P, UNITS, UK, GW])
        w_hi = sb("w_hi", [P, UNITS, UK, GW], F32R)
        w_lo = sb("w_lo", [P, UNITS, UK, GW], F32R)
        h = sb("h", [P, KC, L])
        x_hi = sb("x_hi", [P, KC, L], F32R)
        x_lo = sb("x_lo", [P, KC, L], F32R)
        y = sb("y", [P, KC, L])
        z_hi = sb("z_hi", [P, KC, L], F32R)
        z_lo = sb("z_lo", [P, KC, L], F32R)
        rows = sb("rows", [P, 2, D])
        rstd = sb("rstd", [P, L])
        std = sb("std", [P, L])
        rpost = sb("rpost", [P, L])
        pre_sum = sb("pre_sum", [P, L])
        sq = sb("sq", [P, GT, L])
        sq_sum = sb("sq_sum", [P, GT, L])
        relu = sb("relu", [P, GT, L])
        ident = sb("ident", [P, P])
        ones = sb("ones", [P, P])
        fold = sb("fold", [P, CHUNK])
        gain_rows = sb("gain_rows", [P, P])
        gains = sb("gains", [P, P])
        lam_rows = sb("lam_rows", [6, P])
        lam_cols = sb("lam_cols", [P, 6])
        lam_prod = sb("lam_prod", [P, 2])
        lam_exp = sb("lam_exp", [P, 2])
        map_sign = sb("map_sign", [P, 1])
        sub_gain = sb("sub_gain", [P, 2])
        sink = sb("sink", [P, KC])
        sink_rows = sb("sink_rows", [P, 2 * KC])
        row_tile = sb("row_tile", [P, 2])
        sink_part = sb("sink_part", [P, SWA_PAIRS])
        sink_meta = sb("sink_meta", [P, SWA_PAIRS])
        q = sb("q", [P, 2 * NQ * P])
        dq = q[:, 0:2 * SEQ].rearrange("p (m t) -> p m t", m=2)
        qz = q[:, :].rearrange("p (t c e r) -> p t c e r", t=2, c=NQ, e=2)
        q_meta = sb("q_meta", [P, P])
        kv = sb("kv", [P, 2 * L + 2 * L + 2 * GW])
        k = kv[:, 0:2 * L].rearrange("p (m t) -> p m t", m=2)
        vt = kv[:, 2 * L:4 * L].rearrange("p (m t) -> p m t", m=2)
        v = kv[:, 4 * L:4 * L + 2 * GW].rearrange("p (r f) -> p r f", r=2)
        vm = sb("vm", [META, GW])
        y_flat = y[:, :, :].rearrange("p c t -> p (c t)")
        k_all = y_flat[:, 0:SWA_KV * L]
        k_heads = k_all.rearrange("p (h t) -> p h t", h=SWA_KV)
        v_meta = y_flat[:, SWA_KV * L:SWA_KV * L + SWA_PAIRS * P]
        v_wins = kv[:, 0:3 * SWA_PAIRS * P]
        own_v = y_flat[:, SWA_KV * L + SWA_PAIRS * P:SWA_KV * L + SWA_PAIRS * P + (NQ + 3) * P]
        vz = own_v[:, 0:NQ * P].rearrange("p (c d) -> p c d", c=NQ)
        vw = own_v[:, NQ * P:]
        chunk_rows = sb("chunk_rows", [P, NQ])
        p_win = sb("p_win", [P, 2, NQ, SWA_KEYS])
        p_diff = p_win[:, :, :, :].rearrange("p a b c -> p (a b c)")[:, 0:DIFF_P]
        p_keys = sb("p_keys", [P, 2, NQ, META_PAD])
        p_meta = sb("p_meta", [P, META])
        mx = sb("mx", [P, 2, NQ])
        top = sb("top", [P, 2, NQ])
        neg = sb("neg", [P, 2, NQ])
        total = sb("total", [P, 2, NQ])
        e_sink = sb("e_sink", [P, 2, NQ])
        denom = sb("denom", [P, 2, NQ])
        inv = sb("inv", [P, 2, NQ])
        table = sb("table", [P, 2])
        eps = sb("eps", [P, 2])
        mq = sb("mq", [P, 7])
        coef = sb("coef", [P, NQ, CHUNK])
        pt_win = sb("pt_win", [P, 2, 512])
        pt_meta = sb("pt_meta", [META, SEQ])
        pt_keys = sb("pt_keys", [P, 2, P])
        pt_mq = sb("pt_mq", [P, P])
        def v_tiles(j):
            return (relu, sq)[j // 2][:, j % 2, :]

        v_first = sq_sum[:, :, :].rearrange("p m t -> p (m t)")[:, 0:SWA_PAIRS * P]

        meta_rows = [pt_win[0:META, :, :].rearrange("p t k -> p (t k)"), kv[0:META, 0:D // 2]]

        def swa_o(t, e):
            return ps[0:SWA_DH, ATT0 + t, :].rearrange("p (c e r) -> p c e r", c=NQ, e=2)[:, :, e, :]

        def swa_z(z, e, tile):
            return z[CHUNK * e:CHUNK * (e + 1), tile, META:L].rearrange("p o (c r) -> p (o c) r", c=NQ)

        def meta_o(e):
            return ps[0:SWA_DH, STAT, 2 * P:3 * P].rearrange("p (g e t r) -> p g e t r", g=2, e=2, t=2)[:, :, e, :, :]

        def meta_z(z, e, tiles):
            return z[CHUNK * e:CHUNK * (e + 1), tiles, 0:META].rearrange("p (g t) r -> p g t r", g=2)

        o_norm = sq[:, :, 0:SEQ]
        o_sq = relu[:, :, 0:SEQ]
        o_inv = rpost[:, 0:SEQ]

        landed = [sem(f"landed{s}") for s in range(UNITS)]
        gains_in = sem("gains_in")
        small_in = sem("small_in")
        rows_in = [sem(f"rows_in{f}") for f in range(2)]
        stored = sem("stored")
        consts = sem("consts")
        zeroed = sem("zeroed")
        pads_zeroed = sem("pads_zeroed")
        hi_ready = sem("hi_ready")
        lo_ready = sem("lo_ready")
        units_used = sem("units_used")
        drained = sem("drained")
        vec = sem("vec")
        sca = sem("sca")
        eps_ready = sem("eps_ready")
        cols_done = sem("cols_done")
        sinks_ready = sem("sinks_ready")
        cols_ready = sem("cols_ready")
        lam_ready = sem("lam_ready")
        turned = sem("turned")
        h_ready = sem("h_ready")
        x_hi_ready = sem("x_hi_ready")
        x_ready = sem("x_ready")
        h_sq_ready = sem("h_sq_ready")
        summed = sem("summed")
        pre_sum_ready = sem("pre_sum_ready")
        pre_stat = sem("pre_stat")
        pre_std = sem("pre_std")
        y_ready = sem("y_ready")
        y_sq_ready = sem("y_sq_ready")
        y_sum_ready = sem("y_sum_ready")
        post_stat = sem("post_stat")
        post_std = sem("post_std")
        relu_ready = sem("relu_ready")
        z_hi_ready = sem("z_hi_ready")
        z_ready = sem("z_ready")
        k_ready = sem("k_ready")
        v_out_ready = sem("v_out_ready")
        q_ready = sem("q_ready")
        begun = sem("begun")
        v_turned = sem("v_turned")
        v_ready = sem("v_ready")
        pair_begun = sem("pair_begun")
        pair_v_ready = sem("pair_v_ready")
        s_done = sem("s_done")
        neg_ready = sem("neg_ready")
        p_ready = sem("p_ready")
        pn_ready = sem("pn_ready")
        pt_done = sem("pt_done")
        pk_done = sem("pk_done")
        pt_win_ready = sem("pt_win_ready")
        pt_keys_ready = sem("pt_keys_ready")
        pv_done = sem("pv_done")
        o_hi_ready = sem("o_hi_ready")
        o_ready = sem("o_ready")
        ms_done = sem("ms_done")
        mneg_ready = sem("mneg_ready")
        mp_ready = sem("mp_ready")
        mpn_ready = sem("mpn_ready")
        mpt_done = sem("mpt_done")
        mpt_ready = sem("mpt_ready")
        mpv_done = sem("mpv_done")
        mo_hi_ready = sem("mo_hi_ready")
        mo_ready = sem("mo_ready")
        dk_ready = sem("dk_ready")
        dq_ready = sem("dq_ready")
        dvt_ready = sem("dvt_ready")
        dv_turned = sem("dv_turned")
        dv_ready = sem("dv_ready")
        ds_done = sem("ds_done")
        dneg_ready = sem("dneg_ready")
        dp_ready = sem("dp_ready")
        coef_ready = sem("coef_ready")
        dt_done = sem("dt_done")
        dt_win_ready = sem("dt_win_ready")
        dt_meta_ready = sem("dt_meta_ready")
        dpv_done = sem("dpv_done")
        o_sq_ready = sem("o_sq_ready")
        o_stat = sem("o_stat")
        o_std = sem("o_std")
        on_ready = sem("on_ready")
        do_hi_ready = sem("do_hi_ready")
        do_ready = sem("do_ready")
        out_turned = sem("out_turned")
        out_ready = sem("out_ready")

        block = ctx.enter_context(nc.Block())
        X = slice(META, L)
        A = slice(0, L)

        @block.sync
        def _(sp):
            def load_unit(u, src, s):
                slot = u % UNITS if isinstance(u, int) else s
                if not isinstance(u, int) or u >= UNITS:
                    sp.wait_ge(lo_ready, u - UNITS + 1)
                sp.dma_start(raw[:, slot], src[:, UK * s:UK * (s + 1)]).then_inc(landed[slot], 16)

            def load(G, src):
                for s in range(UNITS):
                    load_unit(UNITS * G + s, src, s)

            def load_two(G, srcs, order):
                for i, (g, s) in enumerate(order):
                    load_unit(UNITS * G + i, srcs[g], s)

            for f in range(2):
                cols = slice(D // 2 * f, D // 2 * (f + 1))
                sp.dma_start(meta_rows[f], a["meta_tokens"][:, cols]).then_inc(rows_in[f], 16)
                for r in range(2):
                    sp.dma_start(rows[:, r, cols], a["x"][0, P * r:P * (r + 1), cols]).then_inc(rows_in[f], 16)

            swa_in = a["swa_w_in"][0].rearrange("(k p) n -> p k n", p=P)

            def swa_cols(col):
                return swa_in[:, :, bass.ds(col, GW)]

            load_two(G_SWA, [swa_cols(D), swa_cols(D + GW)], BY_CHUNK)
            load(G_SWA + 2, swa_cols(D + 2 * GW))
            load(G_SWA + 3, swa_cols(D + 3 * GW))
            with sp.Fori(0, PANEL) as i:
                load(G_SWA_Q + i, swa_cols(i * GW))

            def panel(G, src, col=0, order=None):
                if order:
                    load_two(G, [src[:, :, bass.ds(col + g * GW, GW)] for g in range(2)], order)
                with sp.Fori(2 if order else 0, PANEL) as i:
                    load(G + i, src[:, :, bass.ds(col + i * GW, GW)])

            def mlp(G, layer):
                w1 = a["ffn_w1"][layer].rearrange("(k p) n -> p k n", p=P)
                w2 = a["ffn_w2"][layer].rearrange("(b k p) n -> p (b k) n", p=P, b=BLOCKS)
                panel(G, w1, 0, BY_CHUNK)
                panel(G + PANEL, w2[:, 0:KC, :])
                with sp.Fori(1, BLOCKS) as b:
                    panel(G + 2 * PANEL * b, w1, b * D)
                    panel(G + 2 * PANEL * b + PANEL, w2[:, bass.ds(b * KC, KC), :])

            panel(G_WOUT0, a["swa_w_out"][0].rearrange("(k p) n -> p k n", p=P), 0, LATE_LAST)
            mlp(G_FFN0, 0)

            diff_in = a["diff_w_in"][0].rearrange("(k p) n -> p k n", p=P)

            def diff_cols(part, hd):
                return diff_in[:, :, bass.ds(part * D + hd * GW, GW)]

            load_two(G_DIFF, [diff_cols(2, 0), diff_cols(1, 0)], BY_CHUNK)
            with sp.Fori(0, DIFF_HEADS - 1) as hd:
                load(G_DIFF + 2 + 3 * hd, diff_cols(0, hd))
                load(G_DIFF + 3 + 3 * hd, diff_cols(2, hd + 1))
                load(G_DIFF + 4 + 3 * hd, diff_cols(1, hd + 1))
            load(G_DIFF + 2 + 3 * (DIFF_HEADS - 1), diff_cols(0, DIFF_HEADS - 1))
            panel(G_WOUT1, a["diff_w_out"][0].rearrange("(k p) n -> p k n", p=P), 0, LATE_LAST)
            mlp(G_FFN1, 1)

            for n in range(2 * 4):
                c4, r = n // 2, n % 2
                sp.wait_ge(out_ready, n + 1)
                sp.dma_start(out[0, P * r:P * (r + 1), 512 * c4:512 * (c4 + 1)],
                             rows[:, r, 512 * c4:512 * (c4 + 1)]).then_inc(stored, 16)
            sp.wait_ge(stored, 16 * 8)

        @block.gpsimd
        def _(pool):
            pool.memset(ident[:, :], 0.0).then_inc(consts, 1)
            pool.wait_ge(consts, 1)
            pool.affine_select(out=ident[:, :], in_=ident[:, :], compare_op=ALU.not_equal, fill=1.0,
                               base=0, pattern=[[-1, P]], channel_multiplier=1).then_inc(consts, 1)
            pool.memset(ones[:, :], 1.0).then_inc(consts, 1)
            pool.memset(fold[:, :], 0.0).then_inc(consts, 1)
            pool.wait_ge(consts, 4)
            pool.affine_select(out=fold[:, :], in_=fold[:, :], compare_op=ALU.not_equal, fill=1.0,
                               base=0, pattern=[[-1, CHUNK]], channel_multiplier=1).then_inc(consts, 1)
            pool.wait_ge(consts, 5)
            pool.affine_select(out=fold[:, :], in_=fold[:, :], compare_op=ALU.not_equal, fill=1.0,
                               base=-CHUNK, pattern=[[-1, CHUNK]], channel_multiplier=1).then_inc(consts, 1)
            pool.memset(q[:, :], 0.0).then_inc(zeroed, 1)
            pool.memset(q_meta[:, :], 0.0).then_inc(zeroed, 1)
            pool.memset(p_win[:, :, 0, META + CHUNK:], 0.0).then_inc(zeroed, 1)
            pool.memset(p_keys[:, :, :, :], 0.0).then_inc(zeroed, 1)
            pool.memset(pt_mq[:, :], 0.0).then_inc(zeroed, 1)

            def h_sum(B):
                pool.wait_ge(h_sq_ready, KC * B + 2)
                pool.tensor_tensor(pre_sum[:, :], y[:, 0, :], y[:, 1, :], ALU.add).then_inc(summed, 1)
                for c in range(2, KC):
                    pool.wait_ge(h_sq_ready, KC * B + c + 1)
                    pool.wait_ge(summed, (KC - 1) * B + c - 1)
                    pool.tensor_tensor(pre_sum[:, :], pre_sum[:, :], y[:, c, :], ALU.add).then_inc(summed, 1)
                pool.wait_ge(summed, (KC - 1) * (B + 1))
                pool.sem_inc(pre_sum_ready, 1)

            h_sum(0)

            def pair_v(j):
                pool.tensor_tensor(vz, v_meta[:, bass.ds(P * j, P)].unsqueeze(1).broadcast_to([P, NQ, P]),
                                   chunk_rows[:, :].unsqueeze(2).broadcast_to([P, NQ, P]), ALU.mult
                                   ).then_inc(pair_v_ready, 1)
                pool.tensor_copy(vw, v_wins[:, bass.ds(3 * P * j, 3 * P)]).then_inc(pair_v_ready, 1)

            pool.wait_ge(v_ready, 1)
            pair_v(0)
            pool.wait_ge(v_ready, SWA_PAIRS)
            with pool.Fori(1, SWA_PAIRS) as j:
                pool.wait_ge(pv_done, 4 * j)
                pool.sem_inc(pair_begun, 1)
                pool.wait_ge(mpv_done, j)
                pool.sem_inc(pair_begun, 1)
                pair_v(j)

            h_sum(1)
            pool.memset(p_diff[:, DIFF_N[0]:DIFF_PAD[0]], 0.0).then_inc(pads_zeroed, 1)
            pool.memset(p_diff[:, DIFF_AT[2] + DIFF_N[2]:DIFF_AT[3]], 0.0).then_inc(pads_zeroed, 1)
            h_sum(2)
            h_sum(3)

        @block.tensor
        def _(pe):
            def unit(u, slot, G, s, parity, hi, lo, tok, ready=None):
                n = tok.stop - tok.start
                if s == 0 and (not isinstance(G, int) or G > 1):
                    pe.wait_ge(drained, G - 1)
                pe.wait_ge(lo_ready, u + 1)
                for kk in range(UK):
                    c = UK * s + kk
                    if ready:
                        ready(c)
                    for m in range(GT):
                        acc = ps[:, 2 * parity + m, 0:n]
                        cols = slice(P * m, P * (m + 1))
                        pe.matmul(acc, w_hi[:, slot, kk, cols], hi[:, c, tok], start=(c == 0), stop=False)
                        pe.matmul(acc, w_hi[:, slot, kk, cols], lo[:, c, tok], start=False, stop=False)
                        last = pe.matmul(acc, w_lo[:, slot, kk, cols], hi[:, c, tok], start=False,
                                         stop=(c == KC - 1))
                last.then_inc(units_used, 1)

            def group(G, parity, hi, lo, tok, ready=None, at=None):
                for s in range(UNITS):
                    unit(UNITS * G + s, s, G, s, parity, hi, lo, tok, ready)
                    for work in (at or {}).get(s, ()):
                        work()

            def two_groups(G, order, hi, lo, tok, ready, at=None):
                for i, (g, s) in enumerate(order):
                    unit(UNITS * G + i, i % UNITS, G + g, s, g, hi, lo, tok, ready)
                    for work in (at or {}).get(i, ()):
                        work()

            def x_chunk(B):
                return lambda c: pe.wait_ge(x_ready, KC * B + c + 1)

            def pre_stat_sum(B, n=L):
                pe.wait_ge(pre_sum_ready, B + 1)
                pe.matmul(ps[:, STAT, 0:n], ones[:, :], pre_sum[:, L - n:L], start=True,
                          stop=True).then_inc(pre_stat, 1)

            def post_stat_sum(p, tok, ended):
                n = tok.stop - tok.start
                if not ended:
                    pe.wait_ge(y_sum_ready, (PANEL - 1) * (p + 1))
                for m in range(GT):
                    if ended:
                        pe.wait_ge(y_sq_ready, Y_STEPS * p + PANEL + m)
                    src = sq if ended else sq_sum
                    last = pe.matmul(ps[:, STAT, 0:n], ones[:, :], src[:, m, tok], start=(m == 0 and not ended),
                                     stop=(m == GT - 1 and ended))
                if ended:
                    last.then_inc(post_stat, 1)

            pe.wait_ge(consts, 6)
            pe.wait_ge(gains_in, 16 * GAIN_LOADS)
            pe.transpose(ps[:, 0, 0:P], gain_rows[:, :], ident[:, :]).then_inc(cols_done, 1)

            def x_turn(chunks):
                for c in chunks:
                    half, c_half = c // (KC // 2), c % (KC // 2)
                    if c_half == 0:
                        pe.wait_ge(rows_in[half], 16 * 3)
                    if c >= 4:
                        pe.wait_ge(h_ready, c - 3)
                    b = 4 + c % 4
                    pe.transpose(ps[:, b, 0:META], meta_rows[half][:, P * c_half:P * (c_half + 1)],
                                 ident[0:META, 0:META])
                    for r in range(2):
                        last = pe.transpose(ps[:, b, META + P * r:META + P * (r + 1)],
                                            rows[:, r, P * c:P * (c + 1)], ident[:, :])
                    last.then_inc(turned, 1)

            def lambda_turn():
                pe.wait_ge(small_in, 16 * SMALL_LOADS)
                pe.wait_ge(h_ready, KC)
                pe.transpose(ps[:, ATT1, 0:6], lam_rows[:, :], ident[0:6, 0:6]).then_inc(cols_done, 1)

            def lambda_sums():
                pe.wait_ge(cols_ready, 3)
                pe.wait_ge(h_ready, KC)
                pe.matmul(ps[:, ATT0, 0:2], ones[:, :], lam_prod[:, :], start=True, stop=True).then_inc(cols_done, 1)

            x_turn(range(0, 10))

            def v_turn(j):
                pe.wait_ge(v_out_ready, j // 2 + 1)
                src = v_tiles(j)
                for w in range(3):
                    t0 = META + CHUNK * w
                    pe.transpose(ps[:, ATT0 + j, P * w:P * (w + 1)], src[:, t0:t0 + P], ident[:, :])
                last = pe.transpose(ps[:, ATT0 + j, 3 * P:4 * P], v_first[:, P * j:P * (j + 1)], ident[:, :])
                last.then_inc(v_turned, 1)

            def swa_scores(j, g):
                pe.wait_ge(q_ready, 2 * j + g + 1)
                n = 4 * j + 2 * g
                if not isinstance(n, int) or n > 0:
                    pe.wait_ge(o_ready, n)
                k0 = (2 * j + g) * L
                for t in range(2):
                    for c in range(NQ):
                        qc = q[:, P * (NQ * t + c):P * (NQ * t + c + 1)]
                        keys = [(0, SWA_N[c])] if c < 2 else [(0, META), (META + CHUNK * (c - 1), SWA_WIN)]
                        col = SWA_OFF[c]
                        for at, nk in keys:
                            last = pe.matmul(ps[:, ATT0 + t, col:col + nk], qc, k_all[:, bass.ds(k0 + at, nk)],
                                             start=True, stop=True)
                            col += nk
                    last.then_inc(s_done, 1)

            def meta_scores(j):
                for g in range(2):
                    last = pe.matmul(ps[:, STAT, META * g:META * (g + 1)], q_meta[:, :],
                                     k_all[:, bass.ds((2 * j + g) * L, META)], start=True, stop=True)
                last.then_inc(ms_done, 1)

            def swa_turn(n):
                for t in range(2):
                    pe.wait_ge(pn_ready, n + t + 1)
                    for c in range(NQ):
                        last = pe.transpose(ps[:, ATT0 + t, P * c:P * (c + 1)], p_win[:, t, c, META:], ident[:, :])
                    last.then_inc(pt_done, 1)
                for t in range(2):
                    last = pe.transpose(ps[:, AUX, P * t:P * (t + 1)], p_keys[:, t].rearrange("p c k -> p (c k)"),
                                        ident[:, :])
                last.then_inc(pk_done, 1)

            def swa_values(j, g):
                n = 4 * j + 2 * g
                pe.wait_ge(pair_v_ready, 2 * (j + 1))
                pe.wait_ge(pt_keys_ready, 2 * j + g + 1)
                for t in range(2):
                    pe.wait_ge(pt_win_ready, n + t + 1)
                    pe.sem_inc(begun, 1)
                    for c in range(NQ):
                        cols = slice(P * c, P * (c + 1))
                        o = ps[0:SWA_DH, ATT0 + t, cols]
                        dv = slice(SWA_DH * g, SWA_DH * (g + 1))
                        pe.matmul(o, vz[:, c, dv], pt_keys[:, t, :],
                                  start=True, stop=False)
                        win = slice(P * max(c - 1, 0) + SWA_DH * g, P * max(c - 1, 0) + SWA_DH * (g + 1))
                        last = pe.matmul(o, vw[:, win], pt_win[:, t, cols], start=False, stop=True)
                    last.then_inc(pv_done, 1)

            def meta_turn(j):
                pe.wait_ge(mpn_ready, j + 1)
                pe.transpose(ps[0:META, STAT, P:2 * P], p_meta[:, :], ident[:, :]).then_inc(mpt_done, 1)

            def meta_values(j):
                pe.wait_ge(mpt_ready, j + 1)
                pe.sem_inc(begun, 1)
                for g in range(2):
                    last = pe.matmul(ps[0:SWA_DH, STAT, 2 * P + CHUNK * g:2 * P + CHUNK * (g + 1)],
                                     vz[:, 0, SWA_DH * g:SWA_DH * (g + 1)],
                                     pt_mq[:, CHUNK * g:CHUNK * (g + 1)], start=True, stop=True)
                last.then_inc(mpv_done, 1)

            def first(j):
                return {0: [lambda: swa_scores(j, 0)], 2: [lambda: swa_turn(4 * j)],
                        3: [lambda: swa_values(j, 0)]}

            def second(j):
                return {0: [lambda: swa_scores(j, 1), lambda: meta_scores(j)],
                        2: [lambda: swa_turn(4 * j + 2), lambda: meta_turn(j)],
                        3: [lambda: swa_values(j, 1), lambda: meta_values(j)]}

            two_groups(G_SWA, BY_CHUNK, x_hi, x_lo, A, x_chunk(0), {
                0: [lambda: x_turn(range(10, 12))], 1: [lambda: x_turn(range(12, 16))],
                6: [lambda: pre_stat_sum(0)], 7: [lambda_turn]})
            group(G_SWA + 2, 0, x_hi, x_lo, A, at={0: [lambda_sums]})
            group(G_SWA + 3, 1, x_hi, x_lo, A, at={1: [lambda: v_turn(0)], 2: [lambda: v_turn(1)]})
            group(G_SWA_Q, 0, x_hi, x_lo, A, at={1: [lambda: v_turn(2)], 2: [lambda: v_turn(3)]})
            pe.wait_ge(v_ready, SWA_PAIRS)
            group(G_SWA_Q + 1, 1, x_hi, x_lo, A, at=first(0))
            with pe.Fori(1, SWA_PAIRS) as j:
                group(G_SWA_Q + 2 * j, 0, x_hi, x_lo, A, at=second(j - 1))
                group(G_SWA_Q + 2 * j + 1, 1, x_hi, x_lo, A, at=first(j))

            def panel(G, hi, lo, tok, ready=None, order=None, at=None):
                if order:
                    two_groups(G, order, hi, lo, tok, ready, at)
                else:
                    group(G, 0, hi, lo, tok, ready)
                    group(G + 1, 1, hi, lo, tok)
                with pe.Fori(1, PANEL // 2 - 1) as i:
                    group(G + 2 * i, 0, hi, lo, tok)
                    group(G + 2 * i + 1, 1, hi, lo, tok)
                group(G + PANEL - 2, 0, hi, lo, tok)

            def mlp(G, layer, tok, B, p):
                n = tok.stop - tok.start

                def z_chunk(b):
                    z0 = PANEL * (BLOCKS * layer + b)
                    return lambda c: pe.wait_ge(z_ready, z0 + c // GT + 1) if c % GT == 0 else None

                def blocks(b, ready=None, order=None, at=None):
                    G1 = G + 2 * PANEL * b
                    panel(G1, x_hi, x_lo, tok, ready, order, at)
                    group(G1 + PANEL - 1, 1, x_hi, x_lo, tok)
                    panel(G1 + PANEL, z_hi, z_lo, tok, z_chunk(b))

                blocks(0, x_chunk(B), BY_CHUNK, {6: [lambda: pre_stat_sum(B, n)]})
                group(G + 2 * PANEL - 1, 1, z_hi, z_lo, tok)
                with pe.Fori(1, BLOCKS - 1) as b:
                    blocks(b)
                    group(G + 2 * PANEL * b + 2 * PANEL - 1, 1, z_hi, z_lo, tok)
                blocks(BLOCKS - 1)
                last_group(G + 2 * PANEL * BLOCKS - 1, tok, p)

            def last_group(G, tok, p):
                group(G, 1, z_hi, z_lo, tok, at={2: [lambda: post_stat_sum(p, tok, False)]})
                post_stat_sum(p, tok, True)

            def z_parts(c):
                pe.wait_ge(o_ready, c + 1)
                pe.wait_ge(mo_ready, c // 4 + 1)

            at = second(SWA_PAIRS - 1)
            panel(G_WOUT0, z_hi, z_lo, A, z_parts, LATE_LAST, at)
            last_group(G_WOUT0 + PANEL - 1, A, 0)
            mlp(G_FFN0, 0, A, 1, 1)

            def dv_turn(hd):
                pe.wait_ge(dvt_ready, hd + 1)
                for f in range(2):
                    cols = slice(P * f, P * (f + 1))
                    pe.transpose(ps[0:META, ATT1, cols], vt[:, f, 0:META], ident[:, :])
                    for r in range(2):
                        last = pe.transpose(ps[:, AUX, GW * r + P * f:GW * r + P * (f + 1)],
                                            vt[:, f, META + P * r:META + P * (r + 1)], ident[:, :])
                last.then_inc(dv_turned, 1)

            def diff_scores(hd):
                pe.wait_ge(dq_ready, hd + 1)
                for m in range(2):
                    half = slice(CHUNK * m, CHUNK * (m + 1))
                    for c in range(NQ):
                        last = pe.matmul(ps[half, DIFF_BANK[c], DIFF_OFF[c]:DIFF_OFF[c] + DIFF_N[c]],
                                         dq[:, m, CHUNK * c:CHUNK * (c + 1)],
                                         k[:, m, 0:DIFF_N[c]], start=True, stop=True)
                last.then_inc(ds_done, 1)

            def diff_turn(hd):
                pe.wait_ge(coef_ready, hd + 1)
                for c in range(NQ):
                    cols = slice(CHUNK * c, CHUNK * (c + 1))
                    at = DIFF_AT[c]
                    pe.matmul(ps[:, ATT1, cols], p_diff[:, at + META:at + META + P], coef[:, c, :],
                              start=True, stop=True)
                    last = pe.matmul(ps[0:META, ATT0, cols], p_diff[:, at:at + META], coef[:, c, :],
                                     start=True, stop=True)
                    if c >= 2:
                        last = pe.matmul(ps[:, ATT0, GW + CHUNK * (c - 2):GW + CHUNK * (c - 1)],
                                         p_diff[:, at + META + P:at + META + 2 * P], coef[:, c, :],
                                         start=True, stop=True)
                last.then_inc(dt_done, 1)

            def diff_values(hd):
                pe.wait_ge(dt_win_ready, hd + 1)
                pe.wait_ge(dt_meta_ready, hd + 1)
                pe.wait_ge(dv_ready, hd + 1)
                for f in range(2):
                    cols = slice(P * f, P * (f + 1))
                    o = ps[:, STAT, SEQ * f:SEQ * (f + 1)]
                    pe.matmul(o, vm[:, cols], pt_meta[:, :], start=True, stop=False)
                    pe.matmul(o, v[:, 0, cols], pt_win[:, 0, 0:SEQ], start=False, stop=False)
                    last = pe.matmul(ps[:, STAT, SEQ * f + 2 * CHUNK:SEQ * (f + 1)], v[:, 1, cols],
                                     pt_win[:, 1, 0:2 * CHUNK], start=False, stop=True)
                last.then_inc(dpv_done, 1)

            def diff_stat(hd):
                pe.wait_ge(o_sq_ready, hd + 1)
                for f in range(2):
                    last = pe.matmul(ps[:, ATT0, 0:SEQ], ones[:, :], o_sq[:, f, :], start=(f == 0), stop=(f == 1))
                last.then_inc(o_stat, 1)

            pe.wait_ge(pads_zeroed, 2)
            two_groups(G_DIFF, BY_CHUNK, x_hi, x_lo, A, x_chunk(2), {6: [lambda: pre_stat_sum(2)]})

            first = lambda hd: {0: [lambda: diff_scores(hd)], 2: [lambda: diff_turn(hd)], 3: [lambda: diff_values(hd)]}
            second = lambda hd: {0: [lambda: diff_stat(hd)]}

            def head(hd, o, at=None):
                G = G_DIFF + 2 + 3 * hd
                group(G, o, x_hi, x_lo, X, at=at)
                group(G + 1, 1 - o, x_hi, x_lo, A, at=first(hd))
                group(G + 2, o, x_hi, x_lo, A, at={**second(hd), 1: [lambda: dv_turn(hd + 1)]})

            head(0, 0, {0: [lambda: dv_turn(0)]})
            with pe.Fori(0, (DIFF_HEADS - 2) // 2) as i:
                head(2 * i + 1, 1)
                head(2 * i + 2, 0)
            hd = DIFF_HEADS - 1
            group(G_DIFF + 2 + 3 * hd, 1, x_hi, x_lo, X)

            def diff_z(c):
                pe.wait_ge(do_ready, c // 2 + 1)

            at = {**first(hd), UNITS: second(hd)[0]}
            panel(G_WOUT1, z_hi, z_lo, X, diff_z, LATE_LAST, at)
            last_group(G_WOUT1 + PANEL - 1, X, 2)
            mlp(G_FFN1, 1, X, 3, 3)

            for n in range(8):
                c4, r = n // 2, n % 2
                pe.wait_ge(h_ready, KC * 4 + 4 * (c4 + 1))
                if n >= 4:
                    pe.wait_ge(out_ready, n - 3)
                for i in range(4):
                    last = pe.transpose(ps[:, n % 4, P * i:P * (i + 1)],
                                        h[:, 4 * c4 + i, META + P * r:META + P * (r + 1)], ident[:, :])
                last.then_inc(out_turned, 1)

        @block.scalar
        def _(act):
            own = Tally(act, sca)

            def split_hi(G, s):
                act.wait_ge(landed[s], 16 * (G + 1))
                if not isinstance(G, int) or G > 0:
                    act.wait_ge(units_used, UNITS * (G - 1) + s + 1)
                act.activation(w_hi[:, s], raw[:, s], ACT.Copy).then_inc(hi_ready, 1)

            def slot(G, at=None, following=True, ended=None):
                for s in range(UNITS):
                    if s == UNITS - 1 and ended:
                        ended()
                    if following:
                        split_hi(G + 1, s)
                    for work in (at or {}).get(s, ()):
                        work()

            def two_slots(G, at):
                slot(G, at)
                slot(G + 1, {i - UNITS: work for i, work in at.items()})

            def x_split(B, c, gain):
                act.wait_ge(h_ready, KC * B + c + 1)
                act.activation(x_hi[:, c, :], h[:, c, :], ACT.Copy,
                               scale=gains[:, gain + c:gain + c + 1]).then_inc(x_hi_ready, 1)

            def operand(B, G, gain):
                for c in range(KC):
                    x_split(B, c, gain)
                    h_square(c)
                    for u in (SPLITS if B else FIRST_SPLITS).get(c, ()):
                        split_hi(G + u // UNITS, u % UNITS)

            def use_table(func):
                act.activation(table[:, 0:1], table[:, 1:2], func)

            def h_square(c):
                act.activation(y[:, c, :], h[:, c, :], ACT.Square).then_inc(h_sq_ready, 1)

            def pre_root(B, n=L):
                act.wait_ge(pre_stat, B + 1)
                act.activation(std[:, L - n:L], ps[:, STAT, 0:n], ACT.Sqrt, bias=eps_norm,
                               scale=1.0 / D).then_inc(pre_std, 1)

            eps_norm = eps[:, 0:1]
            eps_ln = eps[:, 1:2]

            for i, name in enumerate(("mix_pre_g", "mix_post_g", "ffn_pre_g", "ffn_post_g")):
                act.dma_start(gain_rows[2 * KC * i:2 * KC * (i + 1), :],
                              a[name].rearrange("l (c p) -> (l c) p", p=P)).then_inc(gains_in, 16)
            for i, name in enumerate(("diff_lam_q1", "diff_lam_k1", "diff_lam_q2", "diff_lam_k2")):
                act.dma_start(lam_rows[i:i + 1, :], a[name]).then_inc(small_in, 16)
            act.dma_start(lam_rows[4:6, :], a["diff_subln_g"][0].rearrange("(c p) -> c p", p=P)).then_inc(small_in, 16)
            act.dma_start(sink_rows[:, :], a["swa_sinks"].broadcast_to([P, 2 * KC])).then_inc(small_in, 16)

            act.wait_ge(eps_ready, 3)
            act.wait_ge(cols_ready, 1)
            operand(0, G_SWA, column(MIX_PRE, 0, 0))
            def swa_exp(n):
                for t in range(2):
                    act.wait_ge(neg_ready, n + t + 1)
                    for c in range(NQ):
                        act.activation(p_win[:, t, c, 0:SWA_N[c]],
                                       ps[:, ATT0 + t, SWA_OFF[c]:SWA_OFF[c] + SWA_N[c]], ACT.Exp,
                                       bias=neg[:, t, c:c + 1], scale=SWA_DH ** -0.5,
                                       accum_out=total[:, t, c:c + 1])
                    act.activation(e_sink[:, t, :], neg[:, t, :], ACT.Exp,
                                   bias=sink_at(n, t)).then_inc(p_ready, 1)

            def sink_at(n, t):
                return sink[:, bass.ds(n + t, 1)]

            def meta_exp(j):
                act.wait_ge(mneg_ready, j + 1)
                for g in range(2):
                    half = slice(CHUNK * g, CHUNK * (g + 1))
                    act.activation(p_meta[half, :], ps[half, STAT, META * g:META * (g + 1)], ACT.Exp,
                                   bias=mq[half, 2:3], scale=SWA_DH ** -0.5, accum_out=mq[half, 3:4])
                act.activation(mq[:, 4:5], mq[:, 2:3], ACT.Exp,
                               bias=sink_meta[:, bass.ds(j, 1)]).then_inc(mp_ready, 1)

            def swa_pt_keys(i):
                act.wait_ge(pk_done, i + 1)
                act.activation(pt_keys[:, :, :], ps[:, AUX, 0:2 * P].rearrange("p (t r) -> p t r", t=2),
                               ACT.Copy).then_inc(pt_keys_ready, 1)

            def swa_o_hi(n):
                for t in range(2):
                    act.wait_ge(pv_done, n + t + 1)
                    for e in range(2):
                        last = act.activation(swa_z(z_hi, e, bass.ds(n + t, 1)), swa_o(t, e), ACT.Copy)
                    last.then_inc(o_hi_ready, 1)

            def meta_o_hi(j):
                act.wait_ge(mpv_done, j + 1)
                for e in range(2):
                    last = act.activation(meta_z(z_hi, e, bass.ds(4 * j, 4)), meta_o(e), ACT.Copy)
                last.then_inc(mo_hi_ready, 1)

            def first(j):
                n = 4 * j
                return {0: [lambda: swa_exp(n)], 2: [lambda: swa_pt_keys(2 * j)], 3: [lambda: swa_o_hi(n)]}

            def second(j):
                n = 4 * j + 2
                return {0: [lambda: swa_exp(n), lambda: meta_exp(j)], 2: [lambda: swa_pt_keys(2 * j + 1)],
                        3: [lambda: swa_o_hi(n), lambda: meta_o_hi(j)]}

            slot(G_SWA + 1, {2: [lambda: pre_root(0), lambda: use_table(ACT.Exp)]})
            act.wait_ge(cols_done, 3)
            act.activation(lam_exp[:, :], ps[:, ATT0, 0:2], ACT.Exp).then_inc(lam_ready, 1)
            act.wait_ge(sinks_ready, 1)

            slot(G_SWA + 2)
            slot(G_SWA + 3)
            slot(G_SWA_Q)
            slot(G_SWA_Q + 1, first(0))
            with act.Fori(1, SWA_PAIRS) as j:
                slot(G_SWA_Q + 2 * j, second(j - 1))
                slot(G_SWA_Q + 2 * j + 1, first(j))

            def y_square(p, i):
                act.wait_ge(y_ready, Y_STEPS * p + i + 1)
                act.activation(sq[:, :, :], y[:, bass.ds(GT * i, GT), :], ACT.Square).then_inc(y_sq_ready, 1)

            def final_panel(G, p, following=True, at=None):
                if at is not None:
                    two_slots(G, {**at, FIRST_DONE + 1: [lambda: y_square(p, 0)]})
                    y_square(p, 1)
                with act.Fori(2 if at is not None else 0, PANEL - 1) as i:
                    slot(G + i)
                    y_square(p, i)

                def last_tiles():
                    use_table(ACT.Sqrt)
                    for m in range(GT):
                        act.wait_ge(y_ready, Y_STEPS * p + PANEL + m)
                        act.activation(sq[:, m, :], y[:, KC - GT + m, :], ACT.Square).then_inc(y_sq_ready, 1)

                slot(G + PANEL - 1, ended=last_tiles, following=following)

            def post_root(p, tok):
                act.wait_ge(post_stat, p + 1)
                n = tok.stop - tok.start
                act.activation(std[:, tok], ps[:, STAT, 0:n], ACT.Sqrt, bias=eps_norm,
                               scale=1.0 / D).then_inc(post_std, 1)

            def mlp(G, layer, p, B, n, following):
                def hidden(b, i):
                    act.wait_ge(relu_ready, PANEL * (BLOCKS * layer + b) + i + 1)
                    own.mark(act.activation(sq[:, :, :], relu[:, :, :], ACT.Square))
                    own.wait()
                    act.activation(z_hi[:, bass.ds(GT * i, GT), :], sq[:, :, :], ACT.Copy).then_inc(z_hi_ready, 1)

                def up(b, i0=0):
                    G1 = G + 2 * PANEL * b
                    with act.Fori(i0, PANEL) as i, own.turns(i - i0, PANEL - i0, 1):
                        slot(G1 + i)
                        hidden(b, i)

                slot(G + 1, {2: [lambda: pre_root(B, n), lambda: hidden(0, 0)]})
                hidden(0, 1)
                up(0, 2)
                with act.Fori(0, PANEL) as i:
                    slot(G + PANEL + i)
                with act.Fori(1, BLOCKS - 1) as b, own.turns(b - 1, BLOCKS - 2, PANEL):
                    up(b)
                    with act.Fori(0, PANEL) as i:
                        slot(G + 2 * PANEL * b + PANEL + i)
                up(BLOCKS - 1)
                final_panel(G + (2 * BLOCKS - 1) * PANEL, p, following)

            def boundary(B, G, p, gain):
                post_root(p, A if p < 2 else X)
                operand(B, G, gain)

            final_panel(G_WOUT0, 0, at=second(SWA_PAIRS - 1))
            boundary(1, G_FFN0, 0, column(FFN_PRE, 0, 0))
            mlp(G_FFN0, 0, 1, 1, L, True)
            boundary(2, G_DIFF, 1, column(MIX_PRE, 1, 0))

            def diff_exp(hd):
                act.wait_ge(dneg_ready, hd + 1)
                for c in range(NQ):
                    last = act.activation(p_diff[:, DIFF_AT[c]:DIFF_AT[c] + DIFF_N[c]],
                                          ps[:, DIFF_BANK[c], DIFF_OFF[c]:DIFF_OFF[c] + DIFF_N[c]], ACT.Exp,
                                          bias=neg[:, 0, c:c + 1], scale=P ** -0.5,
                                          accum_out=total[:, 0, c:c + 1])
                last.then_inc(dp_ready, 1)

            def diff_pt_meta(hd):
                act.wait_ge(dt_done, hd + 1)
                act.activation(pt_meta[:, :], ps[0:META, ATT0, 0:SEQ], ACT.Copy)
                act.activation(pt_win[:, 1, 0:2 * CHUNK], ps[:, ATT0, SEQ:SEQ + 2 * CHUNK],
                               ACT.Copy).then_inc(dt_meta_ready, 1)

            def diff_square(hd):
                act.wait_ge(dpv_done, hd + 1)
                act.activation(o_sq, ps[:, STAT, :].rearrange("p (f t) -> p f t", f=2),
                               ACT.Square).then_inc(o_sq_ready, 1)

            def diff_root(hd):
                act.wait_ge(o_stat, hd + 1)
                act.activation(std[:, 0:SEQ], ps[:, ATT0, 0:SEQ], ACT.Sqrt, bias=eps_ln,
                               scale=1.0 / GW).then_inc(o_std, 1)

            def diff_o_hi(hd):
                act.wait_ge(on_ready, hd + 1)
                act.activation(z_hi[:, bass.ds(2 * hd, 2), X], o_norm, ACT.Copy).then_inc(do_hi_ready, 1)

            slot(G_DIFF + 1, {2: [lambda: pre_root(2), lambda: use_table(ACT.Exp)]})
            first = lambda hd: {0: [lambda: diff_exp(hd), lambda: use_table(ACT.Sqrt)], 2: [lambda: diff_pt_meta(hd)],
                                3: [lambda: diff_square(hd)]}
            second = lambda hd: {0: [lambda: diff_root(hd), lambda: use_table(ACT.Exp), lambda: diff_o_hi(hd)]}

            def head(hd):
                slot(G_DIFF + 2 + 3 * hd)
                slot(G_DIFF + 3 + 3 * hd, first(hd))
                slot(G_DIFF + 4 + 3 * hd, second(hd))

            with act.Fori(0, DIFF_HEADS - 1) as hd:
                head(hd)
            hd = DIFF_HEADS - 1
            slot(G_DIFF + 2 + 3 * hd)
            final_panel(G_WOUT1, 2, at={**first(hd), **{UNITS + i: work for i, work in second(hd).items()}})
            boundary(3, G_FFN1, 2, column(FFN_PRE, 1, 0))
            mlp(G_FFN1, 1, 3, 3, SEQ, False)
            post_root(3, X)
            for n in range(8):
                c4, r = n // 2, n % 2
                act.wait_ge(out_turned, n + 1)
                act.activation(rows[:, r, 512 * c4:512 * (c4 + 1)], ps[:, n % 4, :], ACT.Copy).then_inc(out_ready, 1)

        @block.vector
        def _(dve):
            own = Tally(dve, vec)

            def split_lo(G, s):
                dve.wait_ge(hi_ready, UNITS * G + s + 1)
                dve.tensor_tensor(w_lo[:, s], raw[:, s], w_hi[:, s].bitcast(F32), ALU.subtract).then_inc(lo_ready, 1)

            def slot(G, ended=None, at=None, following=True):
                for s in range(UNITS):
                    if s == UNITS - 1 and ended:
                        group_done(G)
                        ended()
                    if following:
                        split_lo(G + 1, s)
                    for work in (at or {}).get(s, ()):
                        work()

            def two_slots(G, first_ended, second_ended, at):
                slot(G, at=at)
                late = {i - UNITS: list(work) for i, work in at.items()}
                late.setdefault(FIRST_DONE - UNITS, []).extend([lambda: first_done(G), first_ended])
                slot(G + 1, second_ended, late)

            def first_done(G):
                dve.wait_ge(units_used, UNITS * G + FIRST_DONE + 1)

            def group_done(G):
                dve.wait_ge(units_used, UNITS * (G + 1))

            def scaled(out_, pair, tok):
                n = tok.stop - tok.start
                return dve.tensor_tensor(out_, ps[:, 2 * pair:2 * pair + 2, 0:n],
                                         rstd[:, tok].unsqueeze(1).broadcast_to([P, 2, n]), ALU.mult)

            def x_lo_split(B, c, gain):
                dve.wait_ge(x_hi_ready, KC * B + c + 1)
                dve.scalar_tensor_tensor(x_lo[:, c, :], h[:, c, :], gains[:, gain + c:gain + c + 1],
                                         x_hi[:, c, :].bitcast(F32), ALU.mult, ALU.subtract).then_inc(x_ready, 1)

            def pre_inverse(B):
                dve.wait_ge(pre_std, B + 1)
                own.mark(dve.reciprocal(rstd[:, :], std[:, :]))
                own.wait()

            dve.memset(eps[:, 0:1], NORM_EPS).then_inc(eps_ready, 1)
            dve.memset(eps[:, 1:2], LN_EPS).then_inc(eps_ready, 1)
            dve.memset(table[:, :], 1.0).then_inc(eps_ready, 1)
            own.mark(dve.memset(map_sign[:, :], 1.0))
            dve.wait_ge(cols_done, 1)
            dve.tensor_copy(gains[:, :], ps[:, 0, 0:P]).then_inc(cols_ready, 1)
            for c in range(KC + 1):
                if c < KC:
                    dve.wait_ge(turned, c + 1)
                    dve.tensor_copy(h[:, c, :], ps[:, 4 + c % 4, 0:L]).then_inc(h_ready, 1)
                if c:
                    x_lo_split(0, c - 1, column(MIX_PRE, 0, 0))
                    for u in FIRST_SPLITS.get(c - 1, ()):
                        split_lo(u // UNITS, u % UNITS)

            def sinks():
                dve.wait_ge(cols_done, 2)
                dve.tensor_copy(lam_cols[:, :], ps[:, ATT1, 0:6]).then_inc(cols_ready, 1)
                dve.wait_ge(cols_ready, 2)
                own.mark(dve.tensor_scalar(sub_gain[:, :], lam_cols[:, 4:6], 1.0 - LAMBDA_INIT, None, ALU.mult))
                dve.tensor_tensor(lam_prod[:, :], lam_cols[:, 0:4:2], lam_cols[:, 1:4:2], ALU.mult).then_inc(cols_ready, 1)
                dve.wait_ge(small_in, 16 * SMALL_LOADS)
                for e in range(2):
                    half = slice(CHUNK * e, CHUNK * (e + 1))
                    own.mark(dve.tensor_copy(sink[half, :], sink_rows[half, e:2 * KC:2]))
                dve.wait_ge(consts, 6)
                own.mark(dve.tensor_reduce(chunk_rows[:, :], ident[:, :].rearrange("p (c k) -> p c k", c=NQ)[:, :, 0:META],
                                           AX.X, ALU.add))
                own.mark(dve.tensor_reduce(row_tile[:, :], ident[:, :].rearrange("p (a t b) -> p t a b", a=4, t=2),
                                           AX.XY, ALU.add))
                own.wait()
                for g in range(2):
                    for e in range(2):
                        r = slice(32 * (2 * g + e), 32 * (2 * g + e) + 32)
                        of_tile = [sink_rows[r, 4 * g + 2 * t + e:2 * KC:8] for t in range(2)]
                        own.mark(dve.tensor_scalar(sink_part[r, :], of_tile[0], row_tile[r, 0:1], None, ALU.mult))
                        own.wait()
                        own.mark(dve.scalar_tensor_tensor(sink_meta[r, :], of_tile[1], row_tile[r, 1:2],
                                                          sink_part[r, :], ALU.mult, ALU.add))
                own.wait()
                dve.sem_inc(sinks_ready, 1)
                dve.wait_ge(lam_ready, 1)
                own.mark(dve.scalar_tensor_tensor(map_sign[CHUNK:P, :], lam_exp[CHUNK:P, 1:2], -LAMBDA_INIT,
                                                  lam_exp[CHUNK:P, 0:1], ALU.add, ALU.subtract))

            def k_out(i):
                for g in range(2):
                    src = slice(CHUNK * g, CHUNK * (g + 1))
                    for e in range(2):
                        dst = k_heads[CHUNK * e:CHUNK * (e + 1), 4 * i + g:4 * i + g + 3:2, :]
                        last = dve.tensor_tensor(dst, ps[src, 2 * i:2 * i + 2, 0:L],
                                                 rstd[src, :].unsqueeze(1).broadcast_to([CHUNK, 2, L]), ALU.mult)
                last.then_inc(k_ready, 1)
                free(k_ready, i + 1)

            def v_out(i):
                first_v = v_first.rearrange("p (j c k) -> p j c k", j=SWA_PAIRS, c=NQ)[:, 2 * i:2 * i + 2]
                wide = [P, 2, NQ, META_PAD]
                dve.tensor_tensor(first_v, ps[:, 2 * i:2 * i + 2, 0:META_PAD].unsqueeze(2).broadcast_to(wide),
                                  rstd[:, 0:META_PAD].unsqueeze(1).unsqueeze(1).broadcast_to(wide), ALU.mult)
                scaled((relu, sq)[i][:, :, :], i, A).then_inc(v_out_ready, 1)
                free(v_out_ready, i + 1)

            def free(made, value):
                dve.wait_ge(made, value)
                dve.sem_inc(drained, 1)

            def q_out(i, parity):
                for e in range(2):
                    half = slice(CHUNK * e, CHUNK * (e + 1))
                    src = ps[half, 2 * parity:2 * parity + 2, :]
                    qm = q_meta[half, CHUNK * parity:CHUNK * (parity + 1)].rearrange("p (e t r) -> p t e r", e=2, t=2)
                    dve.tensor_tensor(qm[:, :, e, :], src[:, :, 0:META],
                                      rstd[half, 0:META].unsqueeze(1).broadcast_to([CHUNK, 2, META]), ALU.mult)
                    for t in range(2):
                        last = dve.tensor_tensor(qz[half, t, :, e, :],
                                                 src[:, t, META:L].rearrange("p (c r) -> p c r", c=NQ),
                                                 rstd[half, META:L].rearrange("p (c r) -> p c r", c=NQ), ALU.mult)
                last.then_inc(q_ready, 1)
                free(q_ready, i + 1)

            def v_turn_out(j):
                dve.wait_ge(v_turned, j + 1)
                dve.tensor_copy(v_wins[:, 3 * P * j:3 * P * (j + 1)], ps[:, ATT0 + j, 0:3 * P])
                dve.tensor_copy(v_meta[:, P * j:P * (j + 1)], ps[:, ATT0 + j, 3 * P:4 * P]).then_inc(v_ready, 1)

            def swa_max(n):
                for t in range(2):
                    dve.wait_ge(s_done, n + t + 1)
                    b = ATT0 + t
                    dve.tensor_reduce(mx[:, t, 0:1], ps[:, b, 0:SWA_N[0]], AX.X, ALU.max)
                    own.mark(dve.tensor_reduce(mx[:, t, 1:NQ],
                                               ps[:, b, SWA_N[0]:].rearrange("p (c k) -> p c k", k=SWA_KEYS),
                                               AX.X, ALU.max))
                    own.wait()
                    own.mark(dve.tensor_scalar(top[:, t, :], mx[:, t, :], SWA_DH ** -0.5,
                                               sink[:, bass.ds(n + t, 1)], ALU.mult, ALU.max))
                    own.wait()
                    dve.tensor_scalar(neg[:, t, :], top[:, t, :], -1.0, None, ALU.mult).then_inc(neg_ready, 1)

            def meta_max(j):
                dve.wait_ge(ms_done, j + 1)
                for g in range(2):
                    half = slice(CHUNK * g, CHUNK * (g + 1))
                    own.mark(dve.tensor_reduce(mq[half, 0:1], ps[half, STAT, META * g:META * (g + 1)], AX.X, ALU.max))
                own.wait()
                own.mark(dve.tensor_scalar(mq[:, 1:2], mq[:, 0:1], SWA_DH ** -0.5,
                                           sink_meta[:, bass.ds(j, 1)], ALU.mult, ALU.max))
                own.wait()
                dve.tensor_scalar(mq[:, 2:3], mq[:, 1:2], -1.0, None, ALU.mult).then_inc(mneg_ready, 1)

            def swa_norm(n):
                for t in range(2):
                    dve.wait_ge(p_ready, n + t + 1)
                    own.mark(dve.tensor_tensor(denom[:, t, :], total[:, t, :], e_sink[:, t, :], ALU.add))
                    own.wait()
                    own.mark(dve.reciprocal(inv[:, t, :], denom[:, t, :]))
                    own.wait()
                    win = p_win[:, t, :, META:]
                    dve.tensor_tensor(win, win, inv[:, t, :].unsqueeze(2).broadcast_to([P, NQ, SWA_WIN]), ALU.mult)
                    dve.tensor_tensor(p_keys[:, t, :, 0:META], p_win[:, t, :, 0:META],
                                      inv[:, t, :].unsqueeze(2).broadcast_to([P, NQ, META]),
                                      ALU.mult).then_inc(pn_ready, 1)

            def meta_norm(j):
                dve.wait_ge(mp_ready, j + 1)
                own.mark(dve.tensor_tensor(mq[:, 5:6], mq[:, 3:4], mq[:, 4:5], ALU.add))
                own.wait()
                own.mark(dve.reciprocal(mq[:, 6:7], mq[:, 5:6]))
                own.wait()
                dve.tensor_scalar(p_meta[:, :], p_meta[:, :], mq[:, 6:7], None, ALU.mult).then_inc(mpn_ready, 1)

            def swa_pt_win(n):
                for t in range(2):
                    dve.wait_ge(pt_done, n + t + 1)
                    dve.tensor_copy(pt_win[:, t, :], ps[:, ATT0 + t, :]).then_inc(pt_win_ready, 1)

            def meta_pt(j):
                dve.wait_ge(mpt_done, j + 1)
                dve.tensor_copy(pt_mq[0:META, :], ps[0:META, STAT, P:2 * P]).then_inc(mpt_ready, 1)

            def swa_o_lo(n):
                for t in range(2):
                    dve.wait_ge(o_hi_ready, n + t + 1)
                    for e in range(2):
                        tile = bass.ds(n + t, 1)
                        last = dve.tensor_tensor(swa_z(z_lo, e, tile), swa_o(t, e), swa_z(z_hi, e, tile).bitcast(F32),
                                                 ALU.subtract)
                    last.then_inc(o_ready, 1)

            def meta_o_lo(j):
                dve.wait_ge(mo_hi_ready, j + 1)
                for e in range(2):
                    tiles = bass.ds(4 * j, 4)
                    last = dve.tensor_tensor(meta_z(z_lo, e, tiles), meta_o(e), meta_z(z_hi, e, tiles).bitcast(F32),
                                             ALU.subtract)
                last.then_inc(mo_ready, 1)

            def first(j):
                n = 4 * j
                return {0: [lambda: swa_max(n), lambda: swa_norm(n)], 2: [lambda: swa_pt_win(n)],
                        3: [lambda: swa_o_lo(n)]}

            def second(j):
                n = 4 * j + 2
                return {0: [lambda: swa_max(n), lambda: meta_max(j), lambda: swa_norm(n), lambda: meta_norm(j)],
                        2: [lambda: swa_pt_win(n), lambda: meta_pt(j)], 3: [lambda: swa_o_lo(n), lambda: meta_o_lo(j)]}

            dve.wait_ge(zeroed, 5)
            slot(G_SWA + 1, lambda: k_out(1),
                 {2: [lambda: pre_inverse(0), lambda: first_done(G_SWA), lambda: k_out(0)]})
            sinks()
            slot(G_SWA + 2, lambda: v_out(0))
            slot(G_SWA + 3, lambda: v_out(1), {1: [lambda: v_turn_out(0)], 2: [lambda: v_turn_out(1)]})
            slot(G_SWA_Q, lambda: q_out(0, 0), {1: [lambda: v_turn_out(2)], 2: [lambda: v_turn_out(3)]})
            slot(G_SWA_Q + 1, lambda: q_out(1, 1), first(0))
            SWA_STEPS = 21
            with dve.Fori(1, SWA_PAIRS) as j, own.turns(j - 1, SWA_PAIRS - 1, SWA_STEPS):
                slot(G_SWA_Q + 2 * j, lambda: q_out(2 * j, 0), second(j - 1))
                slot(G_SWA_Q + 2 * j + 1, lambda: q_out(2 * j + 1, 1), first(j))

            def y_sum(p, i):
                dve.wait_ge(y_sq_ready, Y_STEPS * p + i + 1)
                own.wait()
                own.mark(dve.tensor_tensor(sq_sum[:, :, :], sq_sum[:, :, :], sq[:, :, :], ALU.add))
                own.wait()
                dve.sem_inc(y_sum_ready, 1)

            def tiles_of(i):
                return bass.ds(GT * i, GT)

            def columns(tok):
                return tok.stop - tok.start

            def final_panel(G, p, tok, add, following=True, at=None):
                def y_out(i, parity):
                    dst, src = y[:, tiles_of(i), tok], ps[:, 2 * parity:2 * parity + 2, 0:columns(tok)]
                    if add:
                        dve.tensor_tensor(dst, dst, src, ALU.add).then_inc(y_ready, 1)
                    else:
                        dve.tensor_copy(dst, src).then_inc(y_ready, 1)
                    free(y_ready, Y_STEPS * p + i + 1)

                own.mark(dve.memset(sq_sum[:, :, :], 0.0))
                if at is not None:
                    two_slots(G, lambda: (y_out(0, 0), y_sum(p, 0)), lambda: y_out(1, 1), at)
                    y_sum(p, 1)
                start = 1 if at is not None else 0
                with dve.Fori(start, PANEL // 2 - 1) as i, own.turns(i - start, PANEL // 2 - 1 - start, 2):
                    for o in range(2):
                        slot(G + 2 * i + o, lambda: y_out(2 * i + o, o))
                        y_sum(p, 2 * i + o)
                slot(G + PANEL - 2, lambda: y_out(PANEL - 2, 0))
                y_sum(p, PANEL - 2)

                def last_tiles():
                    for m in range(GT):
                        dst, src = y[:, KC - GT + m, tok], ps[:, 2 + m, 0:columns(tok)]
                        if add:
                            dve.tensor_tensor(dst, dst, src, ALU.add).then_inc(y_ready, 1)
                        else:
                            dve.tensor_copy(dst, src).then_inc(y_ready, 1)
                    free(y_ready, Y_STEPS * (p + 1))

                slot(G + PANEL - 1, last_tiles, following=following)

            def boundary(B, G, p, post, pre, tok):
                dve.wait_ge(post_std, p + 1)
                own.mark(dve.reciprocal(rpost[:, tok], std[:, tok]))
                own.wait()
                scaled_y = []
                for c in range(KC + 2):
                    if c < KC:
                        own.mark(dve.scalar_tensor_tensor(y[:, c, tok], y[:, c, tok], gains[:, post + c:post + c + 1],
                                                          rpost[:, tok], ALU.mult, ALU.mult))
                        scaled_y.append(own.value)
                    if 1 <= c <= KC:
                        dve.wait_ge(vec, scaled_y[c - 1])
                        dve.tensor_tensor(h[:, c - 1, tok], h[:, c - 1, tok], y[:, c - 1, tok],
                                          ALU.add).then_inc(h_ready, 1)
                    if c >= 2 and pre is not None:
                        x_lo_split(B, c - 2, pre)
                        for u in SPLITS.get(c - 2, ()):
                            split_lo(G + u // UNITS, u % UNITS)

            def mlp(G, layer, p, B, tok, following):
                n = columns(tok)

                def up_out(i, parity):
                    dve.scalar_tensor_tensor(relu[:, :, tok], ps[:, 2 * parity:2 * parity + 2, 0:n], 0.0,
                                             rstd[:, tok].unsqueeze(1).broadcast_to([P, 2, n]), ALU.max,
                                             ALU.mult).then_inc(relu_ready, 1)
                    free(relu_ready, i)

                def z_split(b, i):
                    dve.wait_ge(z_hi_ready, number(b, i))
                    dve.tensor_tensor(z_lo[:, tiles_of(i), :], sq[:, :, :], z_hi[:, tiles_of(i), :].bitcast(F32),
                                      ALU.subtract).then_inc(z_ready, 1)

                def number(b, i):
                    return PANEL * (BLOCKS * layer + b) + i + 1

                def up(b, start=0):
                    with dve.Fori(start, PANEL // 2) as i:
                        for o in range(2):
                            slot(G + 2 * PANEL * b + 2 * i + o, lambda: up_out(number(b, 2 * i + o), o))
                            z_split(b, 2 * i + o)

                def down(b):
                    G2 = G + 2 * PANEL * b + PANEL
                    def y_add(i, parity):
                        dst, src = y[:, tiles_of(i), tok], ps[:, 2 * parity:2 * parity + 2, 0:n]
                        if isinstance(b, int) and b == 0:
                            own.mark(dve.tensor_copy(dst, src))
                        else:
                            own.mark(dve.tensor_tensor(dst, dst, src, ALU.add))
                        own.wait()
                        dve.sem_inc(drained, 1)

                    with dve.Fori(0, PANEL // 2) as i, own.turns(i, PANEL // 2, 2):
                        for o in range(2):
                            slot(G2 + 2 * i + o, lambda: y_add(2 * i + o, o))

                slot(G + 1, lambda: up_out(number(0, 1), 1),
                     {2: [lambda: pre_inverse(B), lambda: first_done(G), lambda: up_out(number(0, 0), 0),
                          lambda: z_split(0, 0)]})
                z_split(0, 1)
                up(0, 1)
                down(0)
                with dve.Fori(1, BLOCKS - 1) as b, own.turns(b - 1, BLOCKS - 2, PANEL):
                    up(b)
                    down(b)
                up(BLOCKS - 1)
                final_panel(G + (2 * BLOCKS - 1) * PANEL, p, tok, True, following)

            final_panel(G_WOUT0, 0, A, False, at=second(SWA_PAIRS - 1))
            boundary(1, G_FFN0, 0, column(MIX_POST, 0, 0), column(FFN_PRE, 0, 0), A)
            mlp(G_FFN0, 0, 1, 1, A, True)
            boundary(2, G_DIFF, 1, column(FFN_POST, 0, 0), column(MIX_PRE, 1, 0), A)

            def tiles_out(dst, pair, tok, made, value):
                scaled(dst, pair, tok).then_inc(made, 1)
                free(made, value)

            def dv_out(hd):
                dve.wait_ge(dv_turned, hd + 1)
                dve.tensor_copy(v[:, :, :], ps[:, AUX, :].rearrange("p (r f) -> p r f", r=2))
                dve.tensor_copy(vm[:, :], ps[0:META, ATT1, 0:GW]).then_inc(dv_ready, 1)

            def diff_max(hd):
                dve.wait_ge(ds_done, hd + 1)
                for c in range(NQ):
                    last = dve.tensor_reduce(mx[:, 0, c:c + 1],
                                             ps[:, DIFF_BANK[c], DIFF_OFF[c]:DIFF_OFF[c] + DIFF_N[c]], AX.X, ALU.max)
                own.mark(last)
                own.wait()
                dve.tensor_scalar(neg[:, 0, :], mx[:, 0, :], -(P ** -0.5), None, ALU.mult).then_inc(dneg_ready, 1)

            def diff_coef(hd):
                dve.wait_ge(dp_ready, hd + 1)
                own.mark(dve.reciprocal(inv[:, 0, :], total[:, 0, :]))
                own.wait()
                for c in range(NQ):
                    last = dve.tensor_scalar(coef[:, c, :], fold[:, :], inv[:, 0, c:c + 1], map_sign[:, 0:1],
                                             ALU.mult, ALU.mult)
                last.then_inc(coef_ready, 1)

            def diff_pt_win(hd):
                dve.wait_ge(dt_done, hd + 1)
                dve.tensor_copy(pt_win[:, 0, 0:SEQ], ps[:, ATT1, 0:SEQ]).then_inc(dt_win_ready, 1)

            def diff_norm(hd):
                dve.wait_ge(o_std, hd + 1)
                own.mark(dve.reciprocal(o_inv, std[:, 0:SEQ]))
                own.wait()
                for f in range(2):
                    last = dve.scalar_tensor_tensor(o_norm[:, f, :], ps[:, STAT, SEQ * f:SEQ * (f + 1)],
                                                    sub_gain[:, f:f + 1], o_inv, ALU.mult, ALU.mult)
                last.then_inc(on_ready, 1)

            def diff_o_lo(hd):
                dve.wait_ge(do_hi_ready, hd + 1)
                dve.tensor_tensor(z_lo[:, bass.ds(2 * hd, 2), X], o_norm, z_hi[:, bass.ds(2 * hd, 2), X].bitcast(F32),
                                  ALU.subtract).then_inc(do_ready, 1)

            slot(G_DIFF + 1, lambda: tiles_out(k, 1, A, dk_ready, 1),
                 {2: [lambda: pre_inverse(2), lambda: first_done(G_DIFF), lambda: tiles_out(vt, 0, A, dvt_ready, 1)]})
            first = lambda hd: {0: [lambda: diff_max(hd), lambda: diff_coef(hd)], 2: [lambda: diff_pt_win(hd)]}
            second = lambda hd: {0: [lambda: diff_norm(hd), lambda: diff_o_lo(hd)]}

            def head(hd, o, at=None):
                G = G_DIFF + 2 + 3 * hd
                slot(G, lambda: tiles_out(dq, o, X, dq_ready, hd + 1), at)
                slot(G + 1, lambda: tiles_out(vt, 1 - o, A, dvt_ready, hd + 2), first(hd))
                slot(G + 2, lambda: tiles_out(k, o, A, dk_ready, hd + 2), {**second(hd), 1: [lambda: dv_out(hd + 1)]})

            DIFF_STEPS = 3
            head(0, 0, {0: [lambda: dv_out(0)]})
            with dve.Fori(0, (DIFF_HEADS - 2) // 2) as i, own.turns(i, (DIFF_HEADS - 2) // 2, 2 * DIFF_STEPS):
                head(2 * i + 1, 1)
                head(2 * i + 2, 0)
            hd = DIFF_HEADS - 1
            slot(G_DIFF + 2 + 3 * hd, lambda: tiles_out(dq, 1, X, dq_ready, hd + 1))

            final_panel(G_WOUT1, 2, X, False, at={**first(hd), **{UNITS + i: work for i, work in second(hd).items()}})
            boundary(3, G_FFN1, 2, column(MIX_POST, 1, 0), column(FFN_PRE, 1, 0), X)
            mlp(G_FFN1, 1, 3, 3, X, False)
            boundary(4, None, 3, column(FFN_POST, 1, 0), None, X)


INPUTS = ["x", "meta_tokens", "mix_pre_g", "mix_post_g", "ffn_pre_g", "ffn_post_g", "swa_w_in", "swa_sinks",
          "swa_w_out", "diff_w_in", "diff_lam_q1", "diff_lam_k1", "diff_lam_q2", "diff_lam_k2", "diff_subln_g",
          "diff_w_out", "ffn_w1", "ffn_w2"]


def kernel(**inputs):
    import concourse.bacc as bacc
    from concourse.bass_utils import run_bass_kernel_spmd

    nc = bacc.Bacc("TRN2", target_bir_lowering=False, num_devices=1)
    arrays, args = {}, {}
    for name in INPUTS:
        value = np.ascontiguousarray(inputs[name])
        arrays[name] = value
        args[name] = nc.dram_tensor(name, value.shape, mybir.dt.from_np(value.dtype), kind="ExternalInput").ap()
    out = nc.dram_tensor("out", (1, SEQ, D), F32, kind="ExternalOutput").ap()
    trunk(nc, args, out)
    result = run_bass_kernel_spmd(nc, [arrays], core_ids=[0])
    return result.results[0]["out"]
```

```python
from contextlib import ExitStack, contextmanager
import math

import numpy as np
import concourse.bass as bass
from concourse import mybir
from concourse.alu_op_type import AluOpType as ALU

F32 = mybir.dt.float32
F32R = mybir.dt.float32r
ACT = mybir.ActivationFunctionType
AX = mybir.AxisListType

P = 128
D = 2048
SEQ = 256
META = 16
L = META + SEQ
KC = D // P
D_FF = 4 * D
NORM_EPS = 1e-6
LN_EPS = 1e-5
CHUNK = 64
NQ = SEQ // CHUNK

UNITS = 4
UK = KC // UNITS
GW = 256
GT = GW // P

SWA_DH = 64
SWA_KV = 8
SWA_PAIRS = SWA_KV // 2
KV_GROUPS = 2 * SWA_KV * SWA_DH // GW
META_PAD = 32
SWA_WIN = 2 * CHUNK
SWA_KEYS = META + SWA_WIN
DIFF_HEADS = 8
PANEL = D // GW
BLOCKS = D_FF // D

G_SWA = 0
G_SWA_Q = G_SWA + KV_GROUPS
G_WOUT0 = G_SWA_Q + PANEL
G_FFN0 = G_WOUT0 + PANEL
G_DIFF = G_FFN0 + 2 * PANEL * BLOCKS
G_WOUT1 = G_DIFF + 3 * DIFF_HEADS
G_FFN1 = G_WOUT1 + PANEL
GROUPS = G_FFN1 + 2 * PANEL * BLOCKS

LAMBDA_INIT = 0.8 - 0.6 * math.exp(-0.3)
GAIN_LOADS = 4
SMALL_LOADS = 4 + 1 + 1
MIX_PRE, MIX_POST, FFN_PRE, FFN_POST = range(4)

ATT0, ATT1, AUX, STAT = 4, 5, 6, 7

SWA_N = [META + CHUNK] + [SWA_KEYS] * 3
SWA_OFF = [0, 80, 224, 368]
DIFF_N = [META + CHUNK * (c + 1) for c in range(NQ)]
DIFF_BANK = [ATT0, ATT1, ATT1, ATT0]
DIFF_OFF = [0, 0, DIFF_N[1], DIFF_N[0]]
DIFF_PAD = [P, 2 * P, 2 * P, L]
DIFF_AT = [0, P, 3 * P, 5 * P]
DIFF_P = DIFF_AT[3] + L

PRE_STAT_AT = 2 * KC - UK
FILLERS = 16
X_AHEAD = 6

H_BLOCKS = [(0, 1), (1, 2)] + [(c, c + 2) for c in range(2, KC, 2)]

POOL_BLOCKS = [H_BLOCKS[i] for i in (2, 4, 6)]

Y_STEPS = PANEL + 1

BY_CHUNK = [(g, s) for s in range(UNITS) for g in range(2)]
LATE_LAST = [(g, s) for g in range(2) for s in range(UNITS - 1)] + [(0, UNITS - 1), (1, UNITS - 1)]
FIRST_DONE = 6

SPLITS = {3: [3], 7: [4], 9: [5], 11: [6], 15: [7]}
FIRST_SPLITS = {1: [0], 5: [1], 8: [2], 10: [3], 12: [4], 15: [5, 6, 7]}


def column(which, layer, c):
    return which * 2 * KC + layer * KC + c


class Tally:

    def __init__(self, eng, sem):
        self.eng, self.sem, self.value, self.marks = eng, sem, 0, 0

    def mark(self, instruction):
        instruction.then_inc(self.sem, 1)
        self.value = self.value + 1
        self.marks += 1

    def wait(self):
        self.eng.wait_ge(self.sem, self.value)

    @contextmanager
    def turns(self, i, count, per):
        before, marks = self.value, self.marks
        self.value = before + i * per
        yield
        assert self.marks - marks == per, (self.marks - marks, per)
        self.value, self.marks = before + count * per, marks + count * per


def trunk(nc, a, out):
    ctx = ExitStack()
    with ctx:
        def sb(name, shape, dt=F32):
            return ctx.enter_context(nc.sbuf_tensor(name, shape, dt))

        def sem(name):
            return ctx.enter_context(nc.semaphore(name))

        ps = ctx.enter_context(nc.psum_tensor("ps", [P, 8, 512], F32))

        raw = sb("raw", [P, UNITS, UK, GW])
        w_hi = sb("w_hi", [P, UNITS, UK, GW], F32R)
        w_lo = sb("w_lo", [P, UNITS, UK, GW], F32R)
        h = sb("h", [P, KC, L])
        x_hi = sb("x_hi", [P, KC, L], F32R)
        x_lo = sb("x_lo", [P, KC, L], F32R)
        y = sb("y", [P, KC, L])
        z_hi = sb("z_hi", [P, KC, L], F32R)
        z_lo = sb("z_lo", [P, KC, L], F32R)
        rows = sb("rows", [P, 2, D])
        rstd = sb("rstd", [P, L])
        std = sb("std", [P, L])
        rpost = sb("rpost", [P, L])
        pre_sum = sb("pre_sum", [P, L])
        sq = sb("sq", [P, GT, L])
        sq_sum = sb("sq_sum", [P, GT, L])
        relu = sb("relu", [P, GT, L])
        ident = sb("ident", [P, P])
        ones = sb("ones", [P, P])
        fold = sb("fold", [P, CHUNK])
        gain_rows = sb("gain_rows", [P, P])
        gains = sb("gains", [P, P])
        lam_rows = sb("lam_rows", [6, P])
        lam_cols = sb("lam_cols", [P, 6])
        lam_prod = sb("lam_prod", [P, 2])
        lam_exp = sb("lam_exp", [P, 2])
        map_sign = sb("map_sign", [P, 1])
        sub_gain = sb("sub_gain", [P, 2])
        sink = sb("sink", [P, KC])
        sink_rows = sb("sink_rows", [P, 2 * KC])
        row_tile = sb("row_tile", [P, 2])
        sink_part = sb("sink_part", [P, SWA_PAIRS])
        sink_meta = sb("sink_meta", [P, SWA_PAIRS])
        q = sb("q", [P, 2 * NQ * P])
        dq = q[:, 0:2 * SEQ].rearrange("p (m t) -> p m t", m=2)
        qz = q[:, :].rearrange("p (t c e r) -> p t c e r", t=2, c=NQ, e=2)
        q_meta = sb("q_meta", [P, P])
        kv = sb("kv", [P, 2 * L + 2 * L + 2 * GW])
        k = kv[:, 0:2 * L].rearrange("p (m t) -> p m t", m=2)
        vt = kv[:, 2 * L:4 * L].rearrange("p (m t) -> p m t", m=2)
        v = kv[:, 4 * L:4 * L + 2 * GW].rearrange("p (r f) -> p r f", r=2)
        v_end = sb("v_end", [META, GW])
        y_flat = y[:, :, :].rearrange("p c t -> p (c t)")
        k_all = y_flat[:, 0:SWA_KV * L]
        k_heads = k_all.rearrange("p (h t) -> p h t", h=SWA_KV)
        v_meta = y_flat[:, SWA_KV * L:SWA_KV * L + SWA_PAIRS * P]
        v_wins = kv[:, 0:3 * SWA_PAIRS * P]
        own_v = y_flat[:, SWA_KV * L + SWA_PAIRS * P:SWA_KV * L + SWA_PAIRS * P + (NQ + 3) * P]
        vz = own_v[:, 0:NQ * P].rearrange("p (c d) -> p c d", c=NQ)
        vw = own_v[:, NQ * P:]
        chunk_rows = sb("chunk_rows", [P, NQ])
        p_win = sb("p_win", [P, 2, NQ, SWA_KEYS])
        p_diff = p_win[:, :, :, :].rearrange("p a b c -> p (a b c)")[:, 0:DIFF_P]
        p_keys = sb("p_keys", [P, 2, NQ, META_PAD])
        p_meta = sb("p_meta", [P, META])
        mx = sb("mx", [P, 2, NQ])
        top = sb("top", [P, 2, NQ])
        neg = sb("neg", [P, 2, NQ])
        total = sb("total", [P, 2, NQ])
        e_sink = sb("e_sink", [P, 2, NQ])
        denom = sb("denom", [P, 2, NQ])
        inv = sb("inv", [P, 2, NQ])
        mq = sb("mq", [P, 7])
        table = sb("table", [P, 2])
        eps = sb("eps", [P, 2])
        coef = sb("coef", [P, NQ, CHUNK])
        pt_win = sb("pt_win", [P, 2, 512])
        pt_end = sb("pt_end", [META, CHUNK])
        pt_keys = sb("pt_keys", [P, 2, P])
        pt_mq = sb("pt_mq", [P, P])

        def v_tiles(j):
            return (relu, sq)[j // 2][:, j % 2, :]

        v_first = sq_sum[:, :, :].rearrange("p m t -> p (m t)")[:, 0:SWA_PAIRS * P]

        meta_rows = [pt_win[0:META, :, :].rearrange("p t k -> p (t k)"), kv[0:META, 0:D // 2]]

        def k_of(i, g, e):
            return k_heads[CHUNK * e:CHUNK * (e + 1), 4 * i + g:4 * i + g + 3:2, :]

        def swa_o(t, e):
            return ps[0:SWA_DH, ATT0 + t, :].rearrange("p (c e r) -> p c e r", c=NQ, e=2)[:, :, e, :]

        def swa_z(z, e, tile):
            return z[CHUNK * e:CHUNK * (e + 1), tile, META:L].rearrange("p o (c r) -> p (o c) r", c=NQ)

        def meta_o(e):
            return ps[0:SWA_DH, STAT, 2 * P:3 * P].rearrange("p (g e t r) -> p g e t r", g=2, e=2, t=2)[:, :, e, :, :]

        def meta_z(z, e, tiles):
            return z[CHUNK * e:CHUNK * (e + 1), tiles, 0:META].rearrange("p (g t) r -> p g t r", g=2)

        o_norm = sq[:, :, 0:SEQ]
        o_sq = relu[:, :, 0:SEQ]
        o_inv = rpost[:, 0:SEQ]

        landed = [sem(f"landed{s}") for s in range(UNITS)]
        gains_in = sem("gains_in")
        small_in = sem("small_in")
        rows_in = [sem(f"rows_in{i}") for i in range(4)]
        stored = sem("stored")
        consts = sem("consts")
        zeroed = sem("zeroed")
        pool_split = sem("pool_split")
        h_pool_ready = sem("h_pool_ready")
        pads_zeroed = sem("pads_zeroed")
        hi_ready = sem("hi_ready")
        lo_ready = sem("lo_ready")
        units_used = sem("units_used")
        tile_done = sem("tile_done")
        drained = sem("drained")
        vec = sem("vec")
        sca = sem("sca")
        eps_ready = sem("eps_ready")
        cols_done = sem("cols_done")
        sinks_ready = sem("sinks_ready")
        cols_ready = sem("cols_ready")
        lam_ready = sem("lam_ready")
        turned = sem("turned")
        y_scaled = sem("y_scaled")
        h_ready = sem("h_ready")
        x_hi_ready = sem("x_hi_ready")
        x_ready = sem("x_ready")
        h_sq_ready = sem("h_sq_ready")
        summed = sem("summed")
        pre_sum_ready = sem("pre_sum_ready")
        pre_stat = sem("pre_stat")
        pre_std = sem("pre_std")
        y_ready = sem("y_ready")
        y_sq_ready = sem("y_sq_ready")
        y_gained = sem("y_gained")
        y_sum_ready = sem("y_sum_ready")
        post_stat = sem("post_stat")
        post_std = sem("post_std")
        relu_ready = sem("relu_ready")
        z_hi_ready = sem("z_hi_ready")
        z_ready = sem("z_ready")
        k_ready = sem("k_ready")
        k_both = sem("k_both")
        v_out_ready = sem("v_out_ready")
        q_ready = sem("q_ready")
        begun = sem("begun")
        v_turned = sem("v_turned")
        v_ready = sem("v_ready")
        pair_begun = sem("pair_begun")
        pair_v_ready = sem("pair_v_ready")
        s_done = sem("s_done")
        neg_ready = sem("neg_ready")
        p_ready = sem("p_ready")
        pn_ready = sem("pn_ready")
        pt_done = sem("pt_done")
        pk_done = sem("pk_done")
        pt_win_ready = sem("pt_win_ready")
        pt_keys_ready = sem("pt_keys_ready")
        pv_done = sem("pv_done")
        o_hi_ready = sem("o_hi_ready")
        o_ready = sem("o_ready")
        ms_done = sem("ms_done")
        mneg_ready = sem("mneg_ready")
        mp_ready = sem("mp_ready")
        mpn_ready = sem("mpn_ready")
        mpt_done = sem("mpt_done")
        mpt_ready = sem("mpt_ready")
        mpv_done = sem("mpv_done")
        mo_hi_ready = sem("mo_hi_ready")
        mo_ready = sem("mo_ready")
        dk_ready = sem("dk_ready")
        dq_ready = sem("dq_ready")
        dvt_ready = sem("dvt_ready")
        dv_turned = sem("dv_turned")
        dv_ready = sem("dv_ready")
        ds_done = sem("ds_done")
        dneg_ready = sem("dneg_ready")
        dp_ready = sem("dp_ready")
        coef_ready = sem("coef_ready")
        dt_done = sem("dt_done")
        dt_win_ready = sem("dt_win_ready")
        dt_end_ready = sem("dt_end_ready")
        dpv_done = sem("dpv_done")
        o_sq_ready = sem("o_sq_ready")
        o_stat = sem("o_stat")
        o_std = sem("o_std")
        on_ready = sem("on_ready")
        do_hi_ready = sem("do_hi_ready")
        do_ready = sem("do_ready")
        out_turned = sem("out_turned")
        out_ready = sem("out_ready")

        block = ctx.enter_context(nc.Block())
        X = slice(META, L)
        A = slice(0, L)

        @block.sync
        def _(sp):
            def load_unit(u, src, s):
                slot = u % UNITS if isinstance(u, int) else s
                if not isinstance(u, int) or u >= UNITS:
                    sp.wait_ge(lo_ready, u - UNITS + 1)
                sp.dma_start(raw[:, slot], src[:, UK * s:UK * (s + 1)]).then_inc(landed[slot], 16)

            def load(G, src):
                for s in range(UNITS):
                    load_unit(UNITS * G + s, src, s)

            def load_two(G, srcs, order):
                for i, (g, s) in enumerate(order):
                    if G == G_SWA and i <= UNITS:
                        load_rows(i) if i < UNITS else small_loads()
                    load_unit(UNITS * G + i, srcs[g], s)

            def small_loads():
                for i, name in enumerate(("diff_lam_q1", "diff_lam_k1", "diff_lam_q2", "diff_lam_k2")):
                    sp.dma_start(lam_rows[i:i + 1, :], a[name]).then_inc(small_in, 16)
                sp.dma_start(lam_rows[4:6, :],
                             a["diff_subln_g"][0].rearrange("(c p) -> c p", p=P)).then_inc(small_in, 16)
                sp.dma_start(sink_rows[:, :], a["swa_sinks"].broadcast_to([P, 2 * KC])).then_inc(small_in, 16)

            def load_rows(i):
                if i % 2 == 0:
                    half = slice(D // 4 * i, D // 4 * (i + 2))
                    sp.dma_start(meta_rows[i // 2], a["meta_tokens"][:, half]).then_inc(rows_in[i], 16)
                cols = slice(D // 4 * i, D // 4 * (i + 1))
                for r in range(2):
                    sp.dma_start(rows[:, r, cols], a["x"][0, P * r:P * (r + 1), cols]).then_inc(rows_in[i], 16)

            swa_in = a["swa_w_in"][0].rearrange("(k p) n -> p k n", p=P)

            def swa_cols(col):
                return swa_in[:, :, bass.ds(col, GW)]

            load_two(G_SWA, [swa_cols(D), swa_cols(D + GW)], BY_CHUNK)
            load(G_SWA + 2, swa_cols(D + 2 * GW))
            load(G_SWA + 3, swa_cols(D + 3 * GW))
            with sp.Fori(0, PANEL) as i:
                load(G_SWA_Q + i, swa_cols(i * GW))

            def panel(G, src, col=0, order=None):
                if order:
                    load_two(G, [src[:, :, bass.ds(col + g * GW, GW)] for g in range(2)], order)
                with sp.Fori(2 if order else 0, PANEL) as i:
                    load(G + i, src[:, :, bass.ds(col + i * GW, GW)])

            def mlp(G, layer):
                w1 = a["ffn_w1"][layer].rearrange("(k p) n -> p k n", p=P)
                w2 = a["ffn_w2"][layer].rearrange("(b k p) n -> p (b k) n", p=P, b=BLOCKS)
                panel(G, w1, 0, BY_CHUNK)
                panel(G + PANEL, w2[:, 0:KC, :])
                with sp.Fori(1, BLOCKS) as b:
                    panel(G + 2 * PANEL * b, w1, b * D)
                    panel(G + 2 * PANEL * b + PANEL, w2[:, bass.ds(b * KC, KC), :])

            panel(G_WOUT0, a["swa_w_out"][0].rearrange("(k p) n -> p k n", p=P), 0, LATE_LAST)
            mlp(G_FFN0, 0)

            diff_in = a["diff_w_in"][0].rearrange("(k p) n -> p k n", p=P)

            def diff_cols(part, hd):
                return diff_in[:, :, bass.ds(part * D + hd * GW, GW)]

            load_two(G_DIFF, [diff_cols(2, 0), diff_cols(1, 0)], BY_CHUNK)
            with sp.Fori(0, DIFF_HEADS - 1) as hd:
                load(G_DIFF + 2 + 3 * hd, diff_cols(0, hd))
                load(G_DIFF + 3 + 3 * hd, diff_cols(2, hd + 1))
                load(G_DIFF + 4 + 3 * hd, diff_cols(1, hd + 1))
            load(G_DIFF + 2 + 3 * (DIFF_HEADS - 1), diff_cols(0, DIFF_HEADS - 1))
            panel(G_WOUT1, a["diff_w_out"][0].rearrange("(k p) n -> p k n", p=P), 0, LATE_LAST)
            mlp(G_FFN1, 1)

            for n in range(2 * 4):
                c4, r = n // 2, n % 2
                sp.wait_ge(out_ready, n + 1)
                sp.dma_start(out[0, P * r:P * (r + 1), 512 * c4:512 * (c4 + 1)],
                             rows[:, r, 512 * c4:512 * (c4 + 1)]).then_inc(stored, 16)
            sp.wait_ge(stored, 16 * 8)

        @block.gpsimd
        def _(pool):
            pool.memset(ident[:, :], 0.0).then_inc(consts, 1)
            pool.wait_ge(consts, 1)
            pool.affine_select(out=ident[:, :], in_=ident[:, :], compare_op=ALU.not_equal, fill=1.0,
                               base=0, pattern=[[-1, P]], channel_multiplier=1).then_inc(consts, 1)
            pool.memset(ones[:, :], 1.0).then_inc(consts, 1)
            pool.memset(fold[:, :], 0.0).then_inc(consts, 1)
            pool.wait_ge(consts, 4)
            pool.affine_select(out=fold[:, :], in_=fold[:, :], compare_op=ALU.not_equal, fill=1.0,
                               base=0, pattern=[[-1, CHUNK]], channel_multiplier=1).then_inc(consts, 1)
            pool.wait_ge(consts, 5)
            pool.affine_select(out=fold[:, :], in_=fold[:, :], compare_op=ALU.not_equal, fill=1.0,
                               base=-CHUNK, pattern=[[-1, CHUNK]], channel_multiplier=1).then_inc(consts, 1)
            pool.memset(q[:, :], 0.0).then_inc(zeroed, 1)
            pool.memset(q_meta[:, :], 0.0).then_inc(zeroed, 1)
            pool.memset(p_win[:, :, 0, META + CHUNK:], 0.0).then_inc(zeroed, 1)
            pool.memset(p_keys[:, :, :, :], 0.0).then_inc(zeroed, 1)
            pool.memset(pt_mq[:, :], 0.0).then_inc(zeroed, 1)

            def h_sum(B):
                pool.wait_ge(h_sq_ready, KC * B + 2)
                pool.tensor_tensor(pre_sum[:, :], y[:, 0, :], y[:, 1, :], ALU.add).then_inc(summed, 1)
                for c in range(2, KC):
                    pool.wait_ge(h_sq_ready, KC * B + c + 1)
                    pool.wait_ge(summed, (KC - 1) * B + c - 1)
                    pool.tensor_tensor(pre_sum[:, :], pre_sum[:, :], y[:, c, :], ALU.add).then_inc(summed, 1)
                pool.wait_ge(summed, (KC - 1) * (B + 1))
                pool.sem_inc(pre_sum_ready, 1)

            h_sum(0)

            def pair_v(j):
                pool.tensor_tensor(vz, v_meta[:, bass.ds(P * j, P)].unsqueeze(1).broadcast_to([P, NQ, P]),
                                   chunk_rows[:, :].unsqueeze(2).broadcast_to([P, NQ, P]), ALU.mult
                                   ).then_inc(pair_v_ready, 1)
                pool.tensor_copy(vw, v_wins[:, bass.ds(3 * P * j, 3 * P)]).then_inc(pair_v_ready, 1)

            pool.wait_ge(v_ready, 1)
            pair_v(0)
            pool.wait_ge(v_ready, SWA_PAIRS)
            with pool.Fori(1, SWA_PAIRS) as j:
                pool.wait_ge(pv_done, 4 * j)
                pool.sem_inc(pair_begun, 1)
                pool.wait_ge(mpv_done, j)
                pool.sem_inc(pair_begun, 1)
                pair_v(j)

            def split_last(G):
                s = UNITS - 1
                pool.wait_ge(hi_ready, UNITS * G + s + 1)
                pool.tensor_tensor(w_lo[:, s], raw[:, s], w_hi[:, s].bitcast(F32),
                                   ALU.subtract).then_inc(pool_split, 1)

            split_last(G_FFN0)
            h_sum(1)
            for c in range(NQ - 1):
                pool.memset(p_diff[:, DIFF_AT[c] + DIFF_N[c]:DIFF_AT[c] + DIFF_PAD[c]], 0.0).then_inc(pads_zeroed, 1)
            split_last(G_DIFF)
            h_sum(2)
            split_last(G_FFN1)
            h_sum(3)

            for i, (c0, c1) in enumerate(POOL_BLOCKS):
                pool.wait_ge(y_scaled, i + 1)
                pool.tensor_tensor(h[:, c0:c1, X], h[:, c0:c1, X], y[:, c0:c1, X],
                                   ALU.add).then_inc(h_pool_ready, c1 - c0)

        @block.tensor
        def _(pe):
            def last_unit(G, hi, lo, tok):
                n, s = tok.stop - tok.start, UNITS - 1
                pe.wait_ge(lo_ready, UNITS * G + s + 1)
                for m in range(GT):
                    acc, cols = ps[:, 2 + m, 0:n], slice(P * m, P * (m + 1))
                    for kk in range(UK):
                        c = UK * s + kk
                        pe.matmul(acc, w_hi[:, s, kk, cols], hi[:, c, tok], start=False, stop=False)
                        pe.matmul(acc, w_hi[:, s, kk, cols], lo[:, c, tok], start=False, stop=False)
                        last = pe.matmul(acc, w_lo[:, s, kk, cols], hi[:, c, tok], start=False, stop=(c == KC - 1))
                    last.then_inc(units_used if m == GT - 1 else tile_done, 1)

            def unit(u, slot, G, s, parity, hi, lo, tok, ready=None, ready_lo=None):
                n = tok.stop - tok.start
                if s == 0 and (not isinstance(G, int) or G > 1):
                    pe.wait_ge(drained, G - 1)
                pe.wait_ge(lo_ready, u + 1)
                for kk in range(UK):
                    c = UK * s + kk
                    if ready:
                        ready(c)
                    for m in range(GT):
                        acc, cols = ps[:, 2 * parity + m, 0:n], slice(P * m, P * (m + 1))
                        pe.matmul(acc, w_lo[:, slot, kk, cols], hi[:, c, tok], start=(c == 0), stop=False)
                        pe.matmul(acc, w_hi[:, slot, kk, cols], hi[:, c, tok], start=False, stop=False)
                    if ready_lo:
                        ready_lo(c)
                    for m in range(GT):
                        acc, cols = ps[:, 2 * parity + m, 0:n], slice(P * m, P * (m + 1))
                        last = pe.matmul(acc, w_hi[:, slot, kk, cols], lo[:, c, tok], start=False,
                                         stop=(c == KC - 1))
                last.then_inc(units_used, 1)

            def group(G, parity, hi, lo, tok, ready=None, at=None):
                for s in range(UNITS):
                    unit(UNITS * G + s, s, G, s, parity, hi, lo, tok, ready)
                    for work in (at or {}).get(s, ()):
                        work()

            def two_groups(G, order, hi, lo, tok, ready, at=None, ready_lo=None):
                for i, (g, s) in enumerate(order):
                    unit(UNITS * G + i, i % UNITS, G + g, s, g, hi, lo, tok, ready, ready_lo)
                    for work in (at or {}).get(i, ()):
                        work()

            def x_groups(G, B, tok, at={}, more=()):
                more, done = iter(more), iter(range(2 * KC))

                def ready(c):
                    x_turn([x for _, x in zip(range(1), more)])
                    if next(done) == PRE_STAT_AT:
                        pre_stat_sum(B, tok.stop - tok.start)
                    pe.wait_ge(x_hi_ready, KC * B + c + 1)

                two_groups(G, BY_CHUNK, x_hi, x_lo, tok, ready, at, lambda c: pe.wait_ge(x_ready, KC * B + c + 1))

            def pre_stat_sum(B, n=L):
                pe.wait_ge(pre_sum_ready, B + 1)
                pe.matmul(ps[:, STAT, 0:n], ones[:, :], pre_sum[:, L - n:L], start=True,
                          stop=True).then_inc(pre_stat, 1)

            def stay_warm():
                for _ in range(FILLERS):
                    pe.matmul(ps[:, AUX, 0:P], ones[:, :], ones[:, :], start=True, stop=True)

            def post_stat_sum(p, tok, ended):
                n = tok.stop - tok.start
                if not ended:
                    pe.wait_ge(y_sum_ready, (PANEL - 1) * (p + 1))
                for m in range(GT):
                    if ended:
                        pe.wait_ge(y_sq_ready, Y_STEPS * p + PANEL + m)
                    src = sq if ended else sq_sum
                    last = pe.matmul(ps[:, STAT, 0:n], ones[:, :], src[:, m, tok], start=(m == 0 and not ended),
                                     stop=(m == GT - 1 and ended))
                if ended:
                    last.then_inc(post_stat, 1)
                    stay_warm()

            pe.wait_ge(consts, 6)

            def x_turn(chunks):
                for c in chunks:
                    half, c_half = c // (KC // 2), c % (KC // 2)
                    if c % 4 == 0:
                        pe.wait_ge(rows_in[c // 4], 16 * (2 if c_half else 3))
                    if c >= 4:
                        pe.wait_ge(h_ready, c - 3)
                    b = 4 + c % 4
                    pe.transpose(ps[:, b, 0:META], meta_rows[half][:, P * c_half:P * (c_half + 1)],
                                 ident[0:META, 0:META])
                    for r in range(2):
                        last = pe.transpose(ps[:, b, META + P * r:META + P * (r + 1)],
                                            rows[:, r, P * c:P * (c + 1)], ident[:, :])
                    last.then_inc(turned, 1)

            def lambda_turn():
                pe.wait_ge(small_in, 16 * SMALL_LOADS)
                pe.wait_ge(h_ready, KC)
                pe.transpose(ps[:, ATT1, 0:6], lam_rows[:, :], ident[0:6, 0:6]).then_inc(cols_done, 1)

            def lambda_sums():
                pe.wait_ge(cols_ready, 3)
                pe.wait_ge(h_ready, KC)
                pe.matmul(ps[:, ATT0, 0:2], ones[:, :], lam_prod[:, :], start=True, stop=True).then_inc(cols_done, 1)

            x_turn(range(0, 2))
            pe.wait_ge(gains_in, 16 * GAIN_LOADS)
            pe.transpose(ps[:, 0, 0:P], gain_rows[:, :], ident[:, :]).then_inc(cols_done, 1)
            x_turn(range(2, X_AHEAD))

            def v_turn(j):
                pe.wait_ge(v_out_ready, j // 2 + 1)
                src = v_tiles(j)
                for w in range(3):
                    t0 = META + CHUNK * w
                    pe.transpose(ps[:, ATT0 + j, P * w:P * (w + 1)], src[:, t0:t0 + P], ident[:, :])
                last = pe.transpose(ps[:, ATT0 + j, 3 * P:4 * P], v_first[:, P * j:P * (j + 1)], ident[:, :])
                last.then_inc(v_turned, 1)

            def swa_scores(j, g):
                pe.wait_ge(q_ready, 2 * j + g + 1)
                n = 4 * j + 2 * g
                if not isinstance(n, int) or n > 0:
                    pe.wait_ge(o_ready, n)
                k0 = (2 * j + g) * L
                for t in range(2):
                    for c in range(NQ):
                        qc = q[:, P * (NQ * t + c):P * (NQ * t + c + 1)]
                        keys = [(0, SWA_N[c])] if c < 2 else [(0, META), (META + CHUNK * (c - 1), SWA_WIN)]
                        col = SWA_OFF[c]
                        for at, nk in keys:
                            last = pe.matmul(ps[:, ATT0 + t, col:col + nk], qc, k_all[:, bass.ds(k0 + at, nk)],
                                             start=True, stop=True)
                            col += nk
                    last.then_inc(s_done, 1)

            def meta_scores(j):
                for g in range(2):
                    last = pe.matmul(ps[:, STAT, META * g:META * (g + 1)], q_meta[:, :],
                                     k_all[:, bass.ds((2 * j + g) * L, META)], start=True, stop=True)
                last.then_inc(ms_done, 1)

            def swa_turn(n):
                for t in range(2):
                    pe.wait_ge(pn_ready, n + t + 1)
                    for c in range(NQ):
                        last = pe.transpose(ps[:, ATT0 + t, P * c:P * (c + 1)], p_win[:, t, c, META:], ident[:, :])
                    last.then_inc(pt_done, 1)
                for t in range(2):
                    last = pe.transpose(ps[:, AUX, P * t:P * (t + 1)], p_keys[:, t].rearrange("p c k -> p (c k)"),
                                        ident[:, :])
                last.then_inc(pk_done, 1)

            def swa_values(j, g):
                n = 4 * j + 2 * g
                pe.wait_ge(pair_v_ready, 2 * (j + 1))
                pe.wait_ge(pt_keys_ready, 2 * j + g + 1)
                for t in range(2):
                    pe.wait_ge(pt_win_ready, n + t + 1)
                    pe.sem_inc(begun, 1)
                    for c in range(NQ):
                        cols = slice(P * c, P * (c + 1))
                        o = ps[0:SWA_DH, ATT0 + t, cols]
                        dv = slice(SWA_DH * g, SWA_DH * (g + 1))
                        pe.matmul(o, vz[:, c, dv], pt_keys[:, t, :],
                                  start=True, stop=False)
                        win = slice(P * max(c - 1, 0) + SWA_DH * g, P * max(c - 1, 0) + SWA_DH * (g + 1))
                        last = pe.matmul(o, vw[:, win], pt_win[:, t, cols], start=False, stop=True)
                    last.then_inc(pv_done, 1)

            def meta_turn(j):
                pe.wait_ge(mpn_ready, j + 1)
                pe.transpose(ps[0:META, STAT, P:2 * P], p_meta[:, :], ident[:, :]).then_inc(mpt_done, 1)

            def meta_values(j):
                pe.wait_ge(mpt_ready, j + 1)
                pe.sem_inc(begun, 1)
                for g in range(2):
                    last = pe.matmul(ps[0:SWA_DH, STAT, 2 * P + CHUNK * g:2 * P + CHUNK * (g + 1)],
                                     vz[:, 0, SWA_DH * g:SWA_DH * (g + 1)],
                                     pt_mq[:, CHUNK * g:CHUNK * (g + 1)], start=True, stop=True)
                last.then_inc(mpv_done, 1)

            def first(j):
                return {0: [lambda: swa_scores(j, 0)], 2: [lambda: swa_turn(4 * j)],
                        3: [lambda: swa_values(j, 0)]}

            def second(j):
                return {0: [lambda: swa_scores(j, 1), lambda: meta_scores(j)],
                        2: [lambda: swa_turn(4 * j + 2), lambda: meta_turn(j)],
                        3: [lambda: swa_values(j, 1), lambda: meta_values(j)]}

            x_groups(G_SWA, 0, A, {7: [lambda_turn]}, range(X_AHEAD, KC))
            group(G_SWA + 2, 0, x_hi, x_lo, A, at={3: [lambda_sums]})
            group(G_SWA + 3, 1, x_hi, x_lo, A, at={1: [lambda: pe.wait_ge(lam_ready, 1), lambda: v_turn(0)],
                                                   2: [lambda: v_turn(1)]})
            group(G_SWA_Q, 0, x_hi, x_lo, A, at={1: [lambda: v_turn(2)], 2: [lambda: v_turn(3)]})
            pe.wait_ge(v_ready, SWA_PAIRS)
            pe.wait_ge(k_both, 2)
            group(G_SWA_Q + 1, 1, x_hi, x_lo, A, at=first(0))
            with pe.Fori(1, SWA_PAIRS) as j:
                group(G_SWA_Q + 2 * j, 0, x_hi, x_lo, A, at=second(j - 1))
                group(G_SWA_Q + 2 * j + 1, 1, x_hi, x_lo, A, at=first(j))

            def panel(G, hi, lo, tok, ready=None, order=None, at=None, started=False):
                if order:
                    two_groups(G, order, hi, lo, tok, ready, at)
                elif not started:
                    group(G, 0, hi, lo, tok, ready)
                    group(G + 1, 1, hi, lo, tok)
                with pe.Fori(1, PANEL // 2 - 1) as i:
                    group(G + 2 * i, 0, hi, lo, tok)
                    group(G + 2 * i + 1, 1, hi, lo, tok)
                group(G + PANEL - 2, 0, hi, lo, tok)

            def mlp(G, layer, tok, B, p):
                n = tok.stop - tok.start

                def z_chunk(b):
                    z0 = PANEL * (BLOCKS * layer + b)
                    return lambda c: pe.wait_ge(z_ready, z0 + c // GT + 1) if c % GT == 0 else None

                def blocks(b, started=False):
                    G1 = G + 2 * PANEL * b
                    panel(G1, x_hi, x_lo, tok, started=started)
                    group(G1 + PANEL - 1, 1, x_hi, x_lo, tok)
                    panel(G1 + PANEL, z_hi, z_lo, tok, z_chunk(b))

                x_groups(G, B, tok)
                blocks(0, started=True)
                group(G + 2 * PANEL - 1, 1, z_hi, z_lo, tok)
                with pe.Fori(1, BLOCKS - 1) as b:
                    blocks(b)
                    group(G + 2 * PANEL * b + 2 * PANEL - 1, 1, z_hi, z_lo, tok)
                blocks(BLOCKS - 1)
                last_group(G + 2 * PANEL * BLOCKS - 1, tok, p)

            def last_group(G, tok, p):
                for s in range(UNITS - 1):
                    unit(UNITS * G + s, s, G, s, 1, z_hi, z_lo, tok)
                post_stat_sum(p, tok, False)
                last_unit(G, z_hi, z_lo, tok)
                post_stat_sum(p, tok, True)

            def z_parts(c):
                pe.wait_ge(o_ready, c + 1)
                pe.wait_ge(mo_ready, c // 4 + 1)

            at = second(SWA_PAIRS - 1)
            panel(G_WOUT0, z_hi, z_lo, A, z_parts, LATE_LAST, at)
            last_group(G_WOUT0 + PANEL - 1, A, 0)
            mlp(G_FFN0, 0, A, 1, 1)

            def dv_turn(hd):
                pe.wait_ge(dvt_ready, hd + 1)
                for f in range(2):
                    cols = slice(P * f, P * (f + 1))
                    pe.transpose(ps[0:META, ATT1, cols], vt[:, f, 2 * P:L], ident[:, :])
                    for r in range(2):
                        last = pe.transpose(ps[:, AUX, GW * r + P * f:GW * r + P * (f + 1)],
                                            vt[:, f, P * r:P * (r + 1)], ident[:, :])
                last.then_inc(dv_turned, 1)

            def diff_scores(hd):
                pe.wait_ge(dq_ready, hd + 1)
                for m in range(2):
                    half = slice(CHUNK * m, CHUNK * (m + 1))
                    for c in range(NQ):
                        last = pe.matmul(ps[half, DIFF_BANK[c], DIFF_OFF[c]:DIFF_OFF[c] + DIFF_N[c]],
                                         dq[:, m, CHUNK * c:CHUNK * (c + 1)],
                                         k[:, m, 0:DIFF_N[c]], start=True, stop=True)
                last.then_inc(ds_done, 1)

            def diff_turn(hd):
                pe.wait_ge(coef_ready, hd + 1)
                for c in range(NQ):
                    cols = slice(CHUNK * c, CHUNK * (c + 1))
                    at = DIFF_AT[c]
                    pe.matmul(ps[:, ATT1, cols], p_diff[:, at:at + P], coef[:, c, :], start=True, stop=True)
                    if c:
                        pe.matmul(ps[:, ATT0, cols], p_diff[:, at + P:at + 2 * P], coef[:, c, :],
                                  start=True, stop=True)
                pe.matmul(ps[0:META, ATT0, SEQ:SEQ + CHUNK], p_diff[:, at + 2 * P:at + L], coef[:, c, :],
                          start=True, stop=True).then_inc(dt_done, 1)

            def diff_values(hd):
                pe.wait_ge(dt_win_ready, hd + 1)
                pe.wait_ge(dt_end_ready, hd + 1)
                pe.wait_ge(dv_ready, hd + 1)
                for f in range(2):
                    cols, o = slice(P * f, P * (f + 1)), SEQ * f
                    pe.matmul(ps[:, STAT, o:o + SEQ], v[:, 0, cols], pt_win[:, 0, 0:SEQ], start=True, stop=False)
                    pe.matmul(ps[:, STAT, o + CHUNK:o + SEQ], v[:, 1, cols], pt_win[:, 1, CHUNK:SEQ],
                              start=False, stop=False)
                    last = pe.matmul(ps[:, STAT, o + SEQ - CHUNK:o + SEQ], v_end[:, cols], pt_end[:, :],
                                     start=False, stop=True)
                last.then_inc(dpv_done, 1)

            def diff_stat(hd):
                pe.wait_ge(o_sq_ready, hd + 1)
                for f in range(2):
                    last = pe.matmul(ps[:, ATT0, 0:SEQ], ones[:, :], o_sq[:, f, :], start=(f == 0), stop=(f == 1))
                last.then_inc(o_stat, 1)

            pe.wait_ge(pads_zeroed, 3)
            x_groups(G_DIFF, 2, A)

            def first(hd):
                return {0: [lambda: diff_scores(hd)], 2: [lambda: diff_turn(hd)], 3: [lambda: diff_values(hd)]}

            def second(hd):
                return {0: [lambda: diff_stat(hd)]}

            def head(hd, o, at=None):
                G = G_DIFF + 2 + 3 * hd
                group(G, o, x_hi, x_lo, X, at=at)
                group(G + 1, 1 - o, x_hi, x_lo, A, at=first(hd))
                group(G + 2, o, x_hi, x_lo, A, at={**second(hd), 1: [lambda: dv_turn(hd + 1)]})

            head(0, 0, {0: [lambda: dv_turn(0)]})
            with pe.Fori(0, (DIFF_HEADS - 2) // 2) as i:
                head(2 * i + 1, 1)
                head(2 * i + 2, 0)
            hd = DIFF_HEADS - 1
            group(G_DIFF + 2 + 3 * hd, 1, x_hi, x_lo, X)

            def diff_z(c):
                pe.wait_ge(do_ready, c // 2 + 1)

            at = {**first(hd), UNITS: second(hd)[0]}
            panel(G_WOUT1, z_hi, z_lo, X, diff_z, LATE_LAST, at)
            last_group(G_WOUT1 + PANEL - 1, X, 2)
            mlp(G_FFN1, 1, X, 3, 3)

            for n in range(8):
                c4, r = n // 2, n % 2
                by_pool = sum(c1 - c0 for c0, c1 in POOL_BLOCKS if c1 <= 4 * (c4 + 1))
                pe.wait_ge(h_ready, KC * 4 + 4 * (c4 + 1) - by_pool)
                if by_pool:
                    pe.wait_ge(h_pool_ready, by_pool)
                if n >= 4:
                    pe.wait_ge(out_ready, n - 3)
                for i in range(4):
                    last = pe.transpose(ps[:, n % 4, P * i:P * (i + 1)],
                                        h[:, 4 * c4 + i, META + P * r:META + P * (r + 1)], ident[:, :])
                last.then_inc(out_turned, 1)

        @block.scalar
        def _(act):
            own = Tally(act, sca)

            def split_hi(G, s):
                act.wait_ge(landed[s], 16 * (G + 1))
                if not isinstance(G, int) or G > 0:
                    act.wait_ge(units_used, UNITS * (G - 1) + s + 1)
                act.activation(w_hi[:, s], raw[:, s], ACT.Copy).then_inc(hi_ready, 1)

            def slot(G, at=None, following=UNITS):
                for s in range(UNITS):
                    if s < following:
                        split_hi(G + 1, s)
                    for work in (at or {}).get(s, ()):
                        work()

            def two_slots(G, at):
                slot(G, at)
                slot(G + 1, {i - UNITS: work for i, work in at.items()})

            def x_split(B, c, gain):
                act.wait_ge(h_ready, KC * B + c + 1)
                act.activation(x_hi[:, c, :], h[:, c, :], ACT.Copy,
                               scale=gains[:, gain + c:gain + c + 1]).then_inc(x_hi_ready, 1)

            def operand(B, G, gain):
                for c in range(KC):
                    x_split(B, c, gain)
                    units = [u for u in (SPLITS if B else FIRST_SPLITS).get(c, ()) if not B or u >= UNITS]
                    if c < KC - 1:
                        for u in units:
                            split_hi(G + u // UNITS, u % UNITS)
                    if c % 2:
                        h_square(c - 1, c + 1)
                    if c == KC - 1:
                        for u in units:
                            split_hi(G + u // UNITS, u % UNITS)

            def use_table(func):
                act.activation(table[:, 0:1], table[:, 1:2], func)

            def h_square(c0, c1):
                act.activation(y[:, c0:c1, :], h[:, c0:c1, :], ACT.Square).then_inc(h_sq_ready, c1 - c0)

            def pre_root(B, n=L):
                act.wait_ge(pre_stat, B + 1)
                act.activation(std[:, L - n:L], ps[:, STAT, 0:n], ACT.Sqrt, bias=eps_norm,
                               scale=1.0 / D).then_inc(pre_std, 1)

            eps_norm = eps[:, 0:1]
            eps_ln = eps[:, 1:2]

            for i, name in enumerate(("mix_pre_g", "mix_post_g", "ffn_pre_g", "ffn_post_g")):
                act.dma_start(gain_rows[2 * KC * i:2 * KC * (i + 1), :],
                              a[name].rearrange("l (c p) -> (l c) p", p=P)).then_inc(gains_in, 16)
            act.wait_ge(eps_ready, 3)
            use_table(ACT.Sqrt)
            act.wait_ge(cols_ready, 1)
            operand(0, G_SWA, column(MIX_PRE, 0, 0))
            def swa_exp(n):
                for t in range(2):
                    act.wait_ge(neg_ready, n + t + 1)
                    for c in range(NQ):
                        act.activation(p_win[:, t, c, 0:SWA_N[c]],
                                       ps[:, ATT0 + t, SWA_OFF[c]:SWA_OFF[c] + SWA_N[c]], ACT.Exp,
                                       bias=neg[:, t, c:c + 1], scale=SWA_DH ** -0.5,
                                       accum_out=total[:, t, c:c + 1])
                    act.activation(e_sink[:, t, :], neg[:, t, :], ACT.Exp,
                                   bias=sink_at(n, t)).then_inc(p_ready, 1)

            def sink_at(n, t):
                return sink[:, bass.ds(n + t, 1)]

            def meta_exp(j):
                act.wait_ge(mneg_ready, j + 1)
                for g in range(2):
                    half = slice(CHUNK * g, CHUNK * (g + 1))
                    act.activation(p_meta[half, :], ps[half, STAT, META * g:META * (g + 1)], ACT.Exp,
                                   bias=mq[half, 2:3], scale=SWA_DH ** -0.5, accum_out=mq[half, 3:4])
                act.activation(mq[:, 4:5], mq[:, 2:3], ACT.Exp,
                               bias=sink_meta[:, bass.ds(j, 1)]).then_inc(mp_ready, 1)

            def swa_pt_keys(i):
                act.wait_ge(pk_done, i + 1)
                act.activation(pt_keys[:, :, :], ps[:, AUX, 0:2 * P].rearrange("p (t r) -> p t r", t=2),
                               ACT.Copy).then_inc(pt_keys_ready, 1)

            def swa_o_hi(n):
                for t in range(2):
                    act.wait_ge(pv_done, n + t + 1)
                    for e in range(2):
                        last = act.activation(swa_z(z_hi, e, bass.ds(n + t, 1)), swa_o(t, e), ACT.Copy)
                    last.then_inc(o_hi_ready, 1)

            def meta_o_hi(j):
                act.wait_ge(mpv_done, j + 1)
                for e in range(2):
                    last = act.activation(meta_z(z_hi, e, bass.ds(4 * j, 4)), meta_o(e), ACT.Copy)
                last.then_inc(mo_hi_ready, 1)

            def first(j):
                n = 4 * j
                return {0: [lambda: swa_exp(n)], 2: [lambda: swa_pt_keys(2 * j)], 3: [lambda: swa_o_hi(n)]}

            def second(j):
                n = 4 * j + 2
                return {0: [lambda: swa_exp(n), lambda: meta_exp(j)], 2: [lambda: swa_pt_keys(2 * j + 1)],
                        3: [lambda: swa_o_hi(n), lambda: meta_o_hi(j)]}

            slot(G_SWA + 1, {0: [lambda: pre_root(0), lambda: use_table(ACT.Exp)]})
            def k_copy(i):
                act.wait_ge(k_ready, i + 1)
                for g in range(2):
                    last = act.activation(k_of(i, g, 1 - g), k_of(i, g, g), ACT.Copy)
                last.then_inc(k_both, 1)

            slot(G_SWA + 2, {1: [lambda: k_copy(0)], 2: [lambda: k_copy(1)]})
            act.wait_ge(cols_done, 3)
            act.activation(lam_exp[:, :], ps[:, ATT0, 0:2], ACT.Exp).then_inc(lam_ready, 1)
            slot(G_SWA + 3)
            slot(G_SWA_Q)
            act.wait_ge(sinks_ready, 1)
            slot(G_SWA_Q + 1, first(0))
            with act.Fori(1, SWA_PAIRS) as j:
                slot(G_SWA_Q + 2 * j, second(j - 1))
                slot(G_SWA_Q + 2 * j + 1, first(j))

            def y_square(p, i, gain):
                act.wait_ge(y_ready, Y_STEPS * p + i + 1)
                act.activation(sq[:, :, :], y[:, bass.ds(GT * i, GT), :], ACT.Square).then_inc(y_sq_ready, 1)
                act.wait_ge(y_sq_ready, Y_STEPS * p + i + 1)
                for m in range(GT):
                    y_gain(bass.ds(GT * i + m, 1), bass.ds(gain + GT * i + m, 1))

            def y_gain(chunk, at):
                act.activation(y[:, chunk, :], y[:, chunk, :], ACT.Copy, scale=gains[:, at]).then_inc(y_gained, 1)

            def final_panel(G, p, gain, following=UNITS - 1, at=None):
                if at is not None:
                    two_slots(G, {**at, FIRST_DONE + 1: [lambda: y_square(p, 0, gain)]})
                    y_square(p, 1, gain)
                with act.Fori(2 if at is not None else 0, PANEL - 1) as i:
                    slot(G + i)
                    y_square(p, i, gain)
                slot(G + PANEL - 1, following=following)
                use_table(ACT.Sqrt)
                for m in range(GT):
                    act.wait_ge(y_ready, Y_STEPS * p + PANEL + m)
                    act.activation(sq[:, m, :], y[:, KC - GT + m, :], ACT.Square).then_inc(y_sq_ready, 1)
                act.wait_ge(y_sq_ready, Y_STEPS * (p + 1))
                for m in range(GT):
                    c = KC - GT + m
                    y_gain(slice(c, c + 1), slice(gain + c, gain + c + 1))

            def post_root(p, tok):
                act.wait_ge(post_stat, p + 1)
                n = tok.stop - tok.start
                act.activation(std[:, tok], ps[:, STAT, 0:n], ACT.Sqrt, bias=eps_norm,
                               scale=1.0 / D).then_inc(post_std, 1)

            def mlp(G, layer, p, B, n, gain, following=UNITS - 1):
                def hidden(b, i):
                    act.wait_ge(relu_ready, PANEL * (BLOCKS * layer + b) + i + 1)
                    own.mark(act.activation(sq[:, :, :], relu[:, :, :], ACT.Square))
                    own.wait()
                    act.activation(z_hi[:, bass.ds(GT * i, GT), :], sq[:, :, :], ACT.Copy).then_inc(z_hi_ready, 1)

                def up(b, i0=0):
                    G1 = G + 2 * PANEL * b
                    with act.Fori(i0, PANEL) as i, own.turns(i - i0, PANEL - i0, 1):
                        slot(G1 + i)
                        hidden(b, i)

                slot(G + 1, {0: [lambda: pre_root(B, n)], 1: [lambda: hidden(0, 0)]})
                hidden(0, 1)
                up(0, 2)
                with act.Fori(0, PANEL) as i:
                    slot(G + PANEL + i)
                with act.Fori(1, BLOCKS - 1) as b, own.turns(b - 1, BLOCKS - 2, PANEL):
                    up(b)
                    with act.Fori(0, PANEL) as i:
                        slot(G + 2 * PANEL * b + PANEL + i)
                up(BLOCKS - 1)
                final_panel(G + (2 * BLOCKS - 1) * PANEL, p, gain, following)

            def boundary(B, G, p, gain):
                post_root(p, A if p < 2 else X)
                split_hi(G, UNITS - 1)
                operand(B, G, gain)

            final_panel(G_WOUT0, 0, column(MIX_POST, 0, 0), at=second(SWA_PAIRS - 1))
            boundary(1, G_FFN0, 0, column(FFN_PRE, 0, 0))
            mlp(G_FFN0, 0, 1, 1, L, column(FFN_POST, 0, 0))
            boundary(2, G_DIFF, 1, column(MIX_PRE, 1, 0))

            def diff_exp(hd):
                act.wait_ge(dneg_ready, hd + 1)
                for c in range(NQ):
                    last = act.activation(p_diff[:, DIFF_AT[c]:DIFF_AT[c] + DIFF_N[c]],
                                          ps[:, DIFF_BANK[c], DIFF_OFF[c]:DIFF_OFF[c] + DIFF_N[c]], ACT.Exp,
                                          bias=neg[:, 0, c:c + 1], scale=P ** -0.5,
                                          accum_out=total[:, 0, c:c + 1])
                last.then_inc(dp_ready, 1)

            def diff_pt_end(hd):
                act.wait_ge(dt_done, hd + 1)
                act.activation(pt_end[:, :], ps[0:META, ATT0, SEQ:SEQ + CHUNK], ACT.Copy)
                act.activation(pt_win[:, 1, CHUNK:SEQ], ps[:, ATT0, CHUNK:SEQ], ACT.Copy).then_inc(dt_end_ready, 1)

            def diff_square(hd):
                act.wait_ge(dpv_done, hd + 1)
                act.activation(o_sq, ps[:, STAT, :].rearrange("p (f t) -> p f t", f=2),
                               ACT.Square).then_inc(o_sq_ready, 1)

            def diff_root(hd):
                act.wait_ge(o_stat, hd + 1)
                act.activation(std[:, 0:SEQ], ps[:, ATT0, 0:SEQ], ACT.Sqrt, bias=eps_ln,
                               scale=1.0 / GW).then_inc(o_std, 1)

            def diff_o_hi(hd):
                act.wait_ge(on_ready, hd + 1)
                act.activation(z_hi[:, bass.ds(2 * hd, 2), X], o_norm, ACT.Copy).then_inc(do_hi_ready, 1)

            slot(G_DIFF + 1, {0: [lambda: pre_root(2), lambda: use_table(ACT.Exp)]})
            def first(hd):
                return {0: [lambda: diff_exp(hd), lambda: use_table(ACT.Sqrt)], 2: [lambda: diff_pt_end(hd)],
                        3: [lambda: diff_square(hd)]}

            def second(hd):
                return {0: [lambda: diff_root(hd), lambda: use_table(ACT.Exp), lambda: diff_o_hi(hd)]}

            def head(hd):
                slot(G_DIFF + 2 + 3 * hd)
                slot(G_DIFF + 3 + 3 * hd, first(hd))
                slot(G_DIFF + 4 + 3 * hd, second(hd))

            with act.Fori(0, DIFF_HEADS - 1) as hd:
                head(hd)
            hd = DIFF_HEADS - 1
            slot(G_DIFF + 2 + 3 * hd)
            final_panel(G_WOUT1, 2, column(MIX_POST, 1, 0), at={**first(hd), UNITS: second(hd)[0]})
            boundary(3, G_FFN1, 2, column(FFN_PRE, 1, 0))
            mlp(G_FFN1, 1, 3, 3, SEQ, column(FFN_POST, 1, 0), 0)
            post_root(3, X)
            for n in range(8):
                c4, r = n // 2, n % 2
                act.wait_ge(out_turned, n + 1)
                act.activation(rows[:, r, 512 * c4:512 * (c4 + 1)], ps[:, n % 4, :], ACT.Copy).then_inc(out_ready, 1)

        @block.vector
        def _(dve):
            own = Tally(dve, vec)

            def split_lo(G, s):
                dve.wait_ge(hi_ready, UNITS * G + s + 1)
                dve.tensor_tensor(w_lo[:, s], raw[:, s], w_hi[:, s].bitcast(F32), ALU.subtract).then_inc(lo_ready, 1)

            def slot(G, ended=None, at=None, following=UNITS):
                for s in range(UNITS):
                    if s == UNITS - 1 and ended:
                        group_done(G)
                        ended()
                    if s < following:
                        split_lo(G + 1, s)
                    for work in (at or {}).get(s, ()):
                        work()

            def two_slots(G, first_ended, second_ended, at):
                slot(G, at=at)
                late = {i - UNITS: list(work) for i, work in at.items()}
                late.setdefault(FIRST_DONE - UNITS, []).extend([lambda: first_done(G), first_ended])
                slot(G + 1, second_ended, late)

            def first_done(G):
                dve.wait_ge(units_used, UNITS * G + FIRST_DONE + 1)

            def group_done(G):
                dve.wait_ge(units_used, UNITS * (G + 1))

            def scaled(out_, pair, tok):
                n = tok.stop - tok.start
                return dve.tensor_tensor(out_, ps[:, 2 * pair:2 * pair + 2, 0:n],
                                         rstd[:, tok].unsqueeze(1).broadcast_to([P, 2, n]), ALU.mult)

            def x_lo_split(B, c, gain):
                dve.wait_ge(x_hi_ready, KC * B + c + 1)
                dve.scalar_tensor_tensor(x_lo[:, c, :], h[:, c, :], gains[:, gain + c:gain + c + 1],
                                         x_hi[:, c, :].bitcast(F32), ALU.mult, ALU.subtract).then_inc(x_ready, 1)

            def pre_inverse(B):
                dve.wait_ge(pre_std, B + 1)
                own.mark(dve.reciprocal(rstd[:, :], std[:, :]))
                own.wait()

            dve.memset(eps[:, 0:1], NORM_EPS).then_inc(eps_ready, 1)
            dve.memset(eps[:, 1:2], LN_EPS).then_inc(eps_ready, 1)
            dve.memset(table[:, :], 1.0).then_inc(eps_ready, 1)
            own.mark(dve.memset(map_sign[:, :], 1.0))
            for c in range(KC + 1):
                if c < KC:
                    dve.wait_ge(turned, c + 1)
                    dve.tensor_copy(h[:, c, :], ps[:, 4 + c % 4, 0:L]).then_inc(h_ready, 1)
                if c == 1:
                    dve.wait_ge(cols_done, 1)
                    dve.tensor_copy(gains[:, :], ps[:, 0, 0:P]).then_inc(cols_ready, 1)
                if c:
                    x_lo_split(0, c - 1, column(MIX_PRE, 0, 0))
                    for u in FIRST_SPLITS.get(c - 1, ()):
                        split_lo(u // UNITS, u % UNITS)

            def sinks():
                dve.wait_ge(cols_done, 2)
                dve.tensor_copy(lam_cols[:, :], ps[:, ATT1, 0:6]).then_inc(cols_ready, 1)
                dve.wait_ge(cols_ready, 2)
                own.mark(dve.tensor_scalar(sub_gain[:, :], lam_cols[:, 4:6], 1.0 - LAMBDA_INIT, None, ALU.mult))
                dve.tensor_tensor(lam_prod[:, :], lam_cols[:, 0:4:2], lam_cols[:, 1:4:2],
                                  ALU.mult).then_inc(cols_ready, 1)
                dve.wait_ge(small_in, 16 * SMALL_LOADS)
                for e in range(2):
                    half = slice(CHUNK * e, CHUNK * (e + 1))
                    own.mark(dve.tensor_copy(sink[half, :], sink_rows[half, e:2 * KC:2]))
                dve.wait_ge(consts, 6)
                meta_of = ident[:, :].rearrange("p (c k) -> p c k", c=NQ)[:, :, 0:META]
                own.mark(dve.tensor_reduce(chunk_rows[:, :], meta_of, AX.X, ALU.add))
                own.mark(dve.tensor_reduce(row_tile[:, :], ident[:, :].rearrange("p (a t b) -> p t a b", a=4, t=2),
                                           AX.XY, ALU.add))
                own.wait()
                for g in range(2):
                    for e in range(2):
                        r = slice(32 * (2 * g + e), 32 * (2 * g + e) + 32)
                        of_tile = [sink_rows[r, 4 * g + 2 * t + e:2 * KC:8] for t in range(2)]
                        own.mark(dve.tensor_scalar(sink_part[r, :], of_tile[0], row_tile[r, 0:1], None, ALU.mult))
                        own.wait()
                        own.mark(dve.scalar_tensor_tensor(sink_meta[r, :], of_tile[1], row_tile[r, 1:2],
                                                          sink_part[r, :], ALU.mult, ALU.add))
                own.wait()
                dve.sem_inc(sinks_ready, 1)

            def k_out(i):
                for g in range(2):
                    half = slice(CHUNK * g, CHUNK * (g + 1))
                    last = dve.tensor_tensor(k_of(i, g, g), ps[half, 2 * i:2 * i + 2, 0:L],
                                             rstd[half, :].unsqueeze(1).broadcast_to([CHUNK, 2, L]), ALU.mult)
                last.then_inc(k_ready, 1)
                free(k_ready, i + 1)

            def v_out(i):
                first_v = v_first.rearrange("p (j c k) -> p j c k", j=SWA_PAIRS, c=NQ)[:, 2 * i:2 * i + 2]
                wide = [P, 2, NQ, META_PAD]
                dve.tensor_tensor(first_v, ps[:, 2 * i:2 * i + 2, 0:META_PAD].unsqueeze(2).broadcast_to(wide),
                                  rstd[:, 0:META_PAD].unsqueeze(1).unsqueeze(1).broadcast_to(wide), ALU.mult)
                scaled((relu, sq)[i][:, :, :], i, A).then_inc(v_out_ready, 1)
                free(v_out_ready, i + 1)

            def free(made, value):
                dve.wait_ge(made, value)
                dve.sem_inc(drained, 1)

            def q_out(i, parity):
                for e in range(2):
                    half = slice(CHUNK * e, CHUNK * (e + 1))
                    src = ps[half, 2 * parity:2 * parity + 2, :]
                    qm = q_meta[half, CHUNK * parity:CHUNK * (parity + 1)].rearrange("p (e t r) -> p t e r", e=2, t=2)
                    dve.tensor_tensor(qm[:, :, e, :], src[:, :, 0:META],
                                      rstd[half, 0:META].unsqueeze(1).broadcast_to([CHUNK, 2, META]), ALU.mult)
                    for t in range(2):
                        last = dve.tensor_tensor(qz[half, t, :, e, :],
                                                 src[:, t, META:L].rearrange("p (c r) -> p c r", c=NQ),
                                                 rstd[half, META:L].rearrange("p (c r) -> p c r", c=NQ), ALU.mult)
                last.then_inc(q_ready, 1)
                free(q_ready, i + 1)

            def v_turn_out(j):
                dve.wait_ge(v_turned, j + 1)
                dve.tensor_copy(v_wins[:, 3 * P * j:3 * P * (j + 1)], ps[:, ATT0 + j, 0:3 * P])
                dve.tensor_copy(v_meta[:, P * j:P * (j + 1)], ps[:, ATT0 + j, 3 * P:4 * P]).then_inc(v_ready, 1)

            def swa_max(n):
                for t in range(2):
                    dve.wait_ge(s_done, n + t + 1)
                    b = ATT0 + t
                    dve.tensor_reduce(mx[:, t, 0:1], ps[:, b, 0:SWA_N[0]], AX.X, ALU.max)
                    own.mark(dve.tensor_reduce(mx[:, t, 1:NQ],
                                               ps[:, b, SWA_N[0]:].rearrange("p (c k) -> p c k", k=SWA_KEYS),
                                               AX.X, ALU.max))
                    own.wait()
                    own.mark(dve.tensor_scalar(top[:, t, :], mx[:, t, :], SWA_DH ** -0.5,
                                               sink[:, bass.ds(n + t, 1)], ALU.mult, ALU.max))
                    own.wait()
                    dve.tensor_scalar(neg[:, t, :], top[:, t, :], -1.0, None, ALU.mult).then_inc(neg_ready, 1)

            def meta_max(j):
                dve.wait_ge(ms_done, j + 1)
                for g in range(2):
                    half = slice(CHUNK * g, CHUNK * (g + 1))
                    own.mark(dve.tensor_reduce(mq[half, 0:1], ps[half, STAT, META * g:META * (g + 1)], AX.X, ALU.max))
                own.wait()
                own.mark(dve.tensor_scalar(mq[:, 1:2], mq[:, 0:1], SWA_DH ** -0.5,
                                           sink_meta[:, bass.ds(j, 1)], ALU.mult, ALU.max))
                own.wait()
                dve.tensor_scalar(mq[:, 2:3], mq[:, 1:2], -1.0, None, ALU.mult).then_inc(mneg_ready, 1)

            def swa_norm(n):
                for t in range(2):
                    dve.wait_ge(p_ready, n + t + 1)
                    own.mark(dve.tensor_tensor(denom[:, t, :], total[:, t, :], e_sink[:, t, :], ALU.add))
                    own.wait()
                    own.mark(dve.reciprocal(inv[:, t, :], denom[:, t, :]))
                    own.wait()
                    win = p_win[:, t, :, META:]
                    dve.tensor_tensor(win, win, inv[:, t, :].unsqueeze(2).broadcast_to([P, NQ, SWA_WIN]), ALU.mult)
                    dve.tensor_tensor(p_keys[:, t, :, 0:META], p_win[:, t, :, 0:META],
                                      inv[:, t, :].unsqueeze(2).broadcast_to([P, NQ, META]),
                                      ALU.mult).then_inc(pn_ready, 1)

            def meta_norm(j):
                dve.wait_ge(mp_ready, j + 1)
                own.mark(dve.tensor_tensor(mq[:, 5:6], mq[:, 3:4], mq[:, 4:5], ALU.add))
                own.wait()
                own.mark(dve.reciprocal(mq[:, 6:7], mq[:, 5:6]))
                own.wait()
                dve.tensor_scalar(p_meta[:, :], p_meta[:, :], mq[:, 6:7], None, ALU.mult).then_inc(mpn_ready, 1)

            def swa_pt_win(n):
                for t in range(2):
                    dve.wait_ge(pt_done, n + t + 1)
                    dve.tensor_copy(pt_win[:, t, :], ps[:, ATT0 + t, :]).then_inc(pt_win_ready, 1)

            def meta_pt(j):
                dve.wait_ge(mpt_done, j + 1)
                dve.tensor_copy(pt_mq[0:META, :], ps[0:META, STAT, P:2 * P]).then_inc(mpt_ready, 1)

            def swa_o_lo(n):
                for t in range(2):
                    dve.wait_ge(o_hi_ready, n + t + 1)
                    for e in range(2):
                        tile = bass.ds(n + t, 1)
                        last = dve.tensor_tensor(swa_z(z_lo, e, tile), swa_o(t, e), swa_z(z_hi, e, tile).bitcast(F32),
                                                 ALU.subtract)
                    last.then_inc(o_ready, 1)

            def meta_o_lo(j):
                dve.wait_ge(mo_hi_ready, j + 1)
                for e in range(2):
                    tiles = bass.ds(4 * j, 4)
                    last = dve.tensor_tensor(meta_z(z_lo, e, tiles), meta_o(e), meta_z(z_hi, e, tiles).bitcast(F32),
                                             ALU.subtract)
                last.then_inc(mo_ready, 1)

            def first(j):
                n = 4 * j
                return {0: [lambda: swa_max(n), lambda: swa_norm(n)], 2: [lambda: swa_pt_win(n)],
                        3: [lambda: swa_o_lo(n)]}

            def second(j):
                n = 4 * j + 2
                return {0: [lambda: swa_max(n), lambda: meta_max(j), lambda: swa_norm(n), lambda: meta_norm(j)],
                        2: [lambda: swa_pt_win(n), lambda: meta_pt(j)], 3: [lambda: swa_o_lo(n), lambda: meta_o_lo(j)]}

            dve.wait_ge(zeroed, 5)
            slot(G_SWA + 1, lambda: k_out(1),
                 {0: [lambda: pre_inverse(0), lambda: first_done(G_SWA), lambda: k_out(0)]})
            sinks()
            slot(G_SWA + 2, lambda: v_out(0))
            slot(G_SWA + 3, lambda: v_out(1), {1: [lambda: v_turn_out(0)], 2: [lambda: v_turn_out(1)]})
            dve.wait_ge(lam_ready, 1)
            own.wait()
            own.mark(dve.scalar_tensor_tensor(map_sign[CHUNK:P, :], lam_exp[CHUNK:P, 1:2], -LAMBDA_INIT,
                                              lam_exp[CHUNK:P, 0:1], ALU.add, ALU.subtract))
            slot(G_SWA_Q, lambda: q_out(0, 0), {1: [lambda: v_turn_out(2)], 2: [lambda: v_turn_out(3)]})
            slot(G_SWA_Q + 1, lambda: q_out(1, 1), first(0))
            SWA_STEPS = 21
            with dve.Fori(1, SWA_PAIRS) as j, own.turns(j - 1, SWA_PAIRS - 1, SWA_STEPS):
                slot(G_SWA_Q + 2 * j, lambda: q_out(2 * j, 0), second(j - 1))
                slot(G_SWA_Q + 2 * j + 1, lambda: q_out(2 * j + 1, 1), first(j))

            def y_sum(p, i):
                dve.wait_ge(y_sq_ready, Y_STEPS * p + i + 1)
                own.wait()
                own.mark(dve.tensor_tensor(sq_sum[:, :, :], sq_sum[:, :, :], sq[:, :, :], ALU.add))
                own.wait()
                dve.sem_inc(y_sum_ready, 1)

            def tiles_of(i):
                return bass.ds(GT * i, GT)

            def columns(tok):
                return tok.stop - tok.start

            def final_panel(G, p, tok, add, following=UNITS - 1, at=None):
                def y_out(i, parity):
                    dst, src = y[:, tiles_of(i), tok], ps[:, 2 * parity:2 * parity + 2, 0:columns(tok)]
                    if add:
                        dve.tensor_tensor(dst, dst, src, ALU.add).then_inc(y_ready, 1)
                    else:
                        dve.tensor_copy(dst, src).then_inc(y_ready, 1)
                    free(y_ready, Y_STEPS * p + i + 1)

                own.mark(dve.memset(sq_sum[:, :, :], 0.0))
                if at is not None:
                    two_slots(G, lambda: (y_out(0, 0), y_sum(p, 0)), lambda: y_out(1, 1), at)
                    y_sum(p, 1)
                start = 1 if at is not None else 0
                with dve.Fori(start, PANEL // 2 - 1) as i, own.turns(i - start, PANEL // 2 - 1 - start, 2):
                    for o in range(2):
                        slot(G + 2 * i + o, lambda: y_out(2 * i + o, o))
                        y_sum(p, 2 * i + o)
                slot(G + PANEL - 2, lambda: y_out(PANEL - 2, 0))
                y_sum(p, PANEL - 2)

                def last_tiles():
                    dve.wait_ge(tile_done, p + 1)
                    for m in range(GT):
                        if m == GT - 1:
                            group_done(G + PANEL - 1)
                        dst, src = y[:, KC - GT + m, tok], ps[:, 2 + m, 0:columns(tok)]
                        if add:
                            dve.tensor_tensor(dst, dst, src, ALU.add).then_inc(y_ready, 1)
                        else:
                            dve.tensor_copy(dst, src).then_inc(y_ready, 1)
                    free(y_ready, Y_STEPS * (p + 1))

                slot(G + PANEL - 1, following=following)
                last_tiles()

            def boundary(B, G, p, pre, tok):
                def operand(c0, c1):
                    for c in range(c0, c1):
                        x_lo_split(B, c, pre)
                        for u in SPLITS.get(c, ()):
                            if u < UNITS:
                                dve.wait_ge(pool_split, B)
                                dve.sem_inc(lo_ready, 1)
                            else:
                                split_lo(G + u // UNITS, u % UNITS)

                dve.wait_ge(post_std, p + 1)
                own.mark(dve.reciprocal(rpost[:, tok], std[:, tok]))
                own.wait()
                n = columns(tok)
                for b, (c0, c1) in enumerate(H_BLOCKS):
                    some = slice(c0, c1)
                    dve.wait_ge(y_gained, KC * p + c1)
                    own.mark(dve.tensor_tensor(y[:, some, tok], y[:, some, tok],
                                               rpost[:, tok].unsqueeze(1).broadcast_to([P, c1 - c0, n]), ALU.mult))
                    if pre is not None and b:
                        operand(*H_BLOCKS[b - 1])
                    own.wait()
                    if pre is None and (c0, c1) in POOL_BLOCKS:
                        dve.sem_inc(y_scaled, 1)
                    else:
                        dve.tensor_tensor(h[:, some, tok], h[:, some, tok], y[:, some, tok],
                                          ALU.add).then_inc(h_ready, c1 - c0)
                if pre is not None:
                    operand(*H_BLOCKS[-1])

            def mlp(G, layer, p, B, tok, following):
                n = columns(tok)

                def up_out(i, parity):
                    dve.scalar_tensor_tensor(relu[:, :, tok], ps[:, 2 * parity:2 * parity + 2, 0:n], 0.0,
                                             rstd[:, tok].unsqueeze(1).broadcast_to([P, 2, n]), ALU.max,
                                             ALU.mult).then_inc(relu_ready, 1)
                    free(relu_ready, i)

                def z_split(b, i):
                    dve.wait_ge(z_hi_ready, number(b, i))
                    dve.tensor_tensor(z_lo[:, tiles_of(i), :], sq[:, :, :], z_hi[:, tiles_of(i), :].bitcast(F32),
                                      ALU.subtract).then_inc(z_ready, 1)

                def number(b, i):
                    return PANEL * (BLOCKS * layer + b) + i + 1

                def up(b, start=0):
                    with dve.Fori(start, PANEL // 2) as i:
                        for o in range(2):
                            slot(G + 2 * PANEL * b + 2 * i + o, lambda: up_out(number(b, 2 * i + o), o))
                            z_split(b, 2 * i + o)

                def down(b):
                    G2 = G + 2 * PANEL * b + PANEL
                    def y_add(i, parity):
                        dst, src = y[:, tiles_of(i), tok], ps[:, 2 * parity:2 * parity + 2, 0:n]
                        if isinstance(b, int) and b == 0:
                            own.mark(dve.tensor_copy(dst, src))
                        else:
                            own.mark(dve.tensor_tensor(dst, dst, src, ALU.add))
                        own.wait()
                        dve.sem_inc(drained, 1)

                    with dve.Fori(0, PANEL // 2) as i, own.turns(i, PANEL // 2, 2):
                        for o in range(2):
                            slot(G2 + 2 * i + o, lambda: y_add(2 * i + o, o))

                slot(G + 1, lambda: up_out(number(0, 1), 1),
                     {0: [lambda: pre_inverse(B), lambda: first_done(G), lambda: up_out(number(0, 0), 0)],
                      1: [lambda: z_split(0, 0)]})
                z_split(0, 1)
                up(0, 1)
                down(0)
                with dve.Fori(1, BLOCKS - 1) as b, own.turns(b - 1, BLOCKS - 2, PANEL):
                    up(b)
                    down(b)
                up(BLOCKS - 1)
                final_panel(G + (2 * BLOCKS - 1) * PANEL, p, tok, True, following)

            final_panel(G_WOUT0, 0, A, False, at=second(SWA_PAIRS - 1))
            boundary(1, G_FFN0, 0, column(FFN_PRE, 0, 0), A)
            mlp(G_FFN0, 0, 1, 1, A, UNITS - 1)
            boundary(2, G_DIFF, 1, column(MIX_PRE, 1, 0), A)

            def tiles_out(dst, pair, tok, made, value):
                scaled(dst, pair, tok).then_inc(made, 1)
                free(made, value)

            def dv_out(hd):
                dve.wait_ge(dv_turned, hd + 1)
                dve.tensor_copy(v[:, :, :], ps[:, AUX, :].rearrange("p (r f) -> p r f", r=2))
                dve.tensor_copy(v_end[:, :], ps[0:META, ATT1, 0:GW]).then_inc(dv_ready, 1)

            def diff_max(hd):
                dve.wait_ge(ds_done, hd + 1)
                for c in range(NQ):
                    last = dve.tensor_reduce(mx[:, 0, c:c + 1],
                                             ps[:, DIFF_BANK[c], DIFF_OFF[c]:DIFF_OFF[c] + DIFF_N[c]], AX.X, ALU.max)
                own.mark(last)
                own.wait()
                dve.tensor_scalar(neg[:, 0, :], mx[:, 0, :], -(P ** -0.5), None, ALU.mult).then_inc(dneg_ready, 1)

            def diff_coef(hd):
                dve.wait_ge(dp_ready, hd + 1)
                own.mark(dve.reciprocal(inv[:, 0, :], total[:, 0, :]))
                own.wait()
                for c in range(NQ):
                    last = dve.tensor_scalar(coef[:, c, :], fold[:, :], inv[:, 0, c:c + 1], map_sign[:, 0:1],
                                             ALU.mult, ALU.mult)
                last.then_inc(coef_ready, 1)

            def diff_pt_win(hd):
                dve.wait_ge(dt_done, hd + 1)
                dve.tensor_copy(pt_win[:, 0, 0:SEQ], ps[:, ATT1, 0:SEQ]).then_inc(dt_win_ready, 1)

            def diff_norm(hd):
                dve.wait_ge(o_std, hd + 1)
                own.mark(dve.reciprocal(o_inv, std[:, 0:SEQ]))
                own.wait()
                for f in range(2):
                    last = dve.scalar_tensor_tensor(o_norm[:, f, :], ps[:, STAT, SEQ * f:SEQ * (f + 1)],
                                                    sub_gain[:, f:f + 1], o_inv, ALU.mult, ALU.mult)
                last.then_inc(on_ready, 1)

            def diff_o_lo(hd):
                dve.wait_ge(do_hi_ready, hd + 1)
                dve.tensor_tensor(z_lo[:, bass.ds(2 * hd, 2), X], o_norm, z_hi[:, bass.ds(2 * hd, 2), X].bitcast(F32),
                                  ALU.subtract).then_inc(do_ready, 1)

            slot(G_DIFF + 1, lambda: tiles_out(k, 1, A, dk_ready, 1),
                 {0: [lambda: pre_inverse(2), lambda: first_done(G_DIFF), lambda: tiles_out(vt, 0, A, dvt_ready, 1)]})
            def first(hd):
                return {0: [lambda: diff_max(hd), lambda: diff_coef(hd)], 2: [lambda: diff_pt_win(hd)]}

            def second(hd):
                return {0: [lambda: diff_norm(hd), lambda: diff_o_lo(hd)]}

            def head(hd, o, at=None):
                G = G_DIFF + 2 + 3 * hd
                slot(G, lambda: tiles_out(dq, o, X, dq_ready, hd + 1), at)
                slot(G + 1, lambda: tiles_out(vt, 1 - o, A, dvt_ready, hd + 2), first(hd))
                slot(G + 2, lambda: tiles_out(k, o, A, dk_ready, hd + 2), {**second(hd), 1: [lambda: dv_out(hd + 1)]})

            DIFF_STEPS = 3
            head(0, 0, {0: [lambda: dv_out(0)]})
            with dve.Fori(0, (DIFF_HEADS - 2) // 2) as i, own.turns(i, (DIFF_HEADS - 2) // 2, 2 * DIFF_STEPS):
                head(2 * i + 1, 1)
                head(2 * i + 2, 0)
            hd = DIFF_HEADS - 1
            slot(G_DIFF + 2 + 3 * hd, lambda: tiles_out(dq, 1, X, dq_ready, hd + 1))

            final_panel(G_WOUT1, 2, X, False, at={**first(hd), UNITS: second(hd)[0]})
            boundary(3, G_FFN1, 2, column(FFN_PRE, 1, 0), X)
            mlp(G_FFN1, 1, 3, 3, X, 0)
            boundary(4, None, 3, None, X)


INPUTS = ["x", "meta_tokens", "mix_pre_g", "mix_post_g", "ffn_pre_g", "ffn_post_g", "swa_w_in", "swa_sinks",
          "swa_w_out", "diff_w_in", "diff_lam_q1", "diff_lam_k1", "diff_lam_q2", "diff_lam_k2", "diff_subln_g",
          "diff_w_out", "ffn_w1", "ffn_w2"]


def kernel(**inputs):
    import concourse.bacc as bacc
    from concourse.bass_utils import run_bass_kernel_spmd

    nc = bacc.Bacc("TRN2", target_bir_lowering=False, num_devices=1)
    arrays, args = {}, {}
    for name in INPUTS:
        value = np.ascontiguousarray(inputs[name])
        arrays[name] = value
        args[name] = nc.dram_tensor(name, value.shape, mybir.dt.from_np(value.dtype), kind="ExternalInput").ap()
    out = nc.dram_tensor("out", (1, SEQ, D), F32, kind="ExternalOutput").ap()
    trunk(nc, args, out)
    result = run_bass_kernel_spmd(nc, [arrays], core_ids=[0])
    return result.results[0]["out"]
```
